# Optimizing a Trainium2 kernel written in Bass

```python
import jax, jax.numpy as jnp
from jax import lax
import numpy as np

D_MODEL = 1024
BATCH = 1
SEQ = 1024
DEPTH = 1
DEC_BATCH = 8
DEC_SEQ = 8
PAST_LEN = 512
PAGE_SIZE = 128

HEAD_DIM = 64
N_MIXERS = 4
GROUP_W = D_MODEL // N_MIXERS
GROUP_HEADS = GROUP_W // HEAD_DIM
CHUNK = 128
Q_BLOCK = 128
CMP_LEN = 32
CMP_STRIDE = 16
CMP_HID = 128
SEL_LEN = 64
SEL_TOPK = 16
WINDOW = 512
CONV_W = 3
N_EXPERTS = 16
N_GROUPS = 4
EXP_PER_GROUP = N_EXPERTS // N_GROUPS
TOP_K = 2
D_EXPERT = D_MODEL // 4
FORGET_BIAS_INIT = 2.0
LN_EPS = 1e-5
SCALE = HEAD_DIM ** -0.5
NEG = -1e30
BIG = 1e30
DEEPNORM_ALPHA = (2 * DEPTH) ** 0.25
DEEPNORM_BETA = (8 * DEPTH) ** -0.25
SPLIT_SIZES = (GROUP_W, GROUP_W, GROUP_W, GROUP_W, GROUP_W, GROUP_HEADS, GROUP_W, 6 * HEAD_DIM, 3 * GROUP_HEADS, GROUP_W, GROUP_W, GROUP_W)
P_IN = sum(SPLIT_SIZES)

kernel_name = 'hybrid_gmlp_fox_nsa_conv_moe_step'

f32 = jnp.float32

def layer_norm(x, g, b):
    xf = x.astype(f32)
    mu = xf.mean(-1, keepdims=True)
    var = jnp.square(xf - mu).mean(-1, keepdims=True)
    return ((xf - mu) * lax.rsqrt(var + LN_EPS) * g.astype(f32) + b.astype(f32)).astype(x.dtype)

def in_proj(x, w):
    h = x @ w
    return jnp.split(h, [int(i) for i in np.cumsum(SPLIT_SIZES)[:-1]], axis=-1)

def heads(a):
    return a.reshape(*a.shape[:-1], GROUP_HEADS, HEAD_DIM)

def to_blocks(a, n):
    return a.reshape(a.shape[0], n, Q_BLOCK, *a.shape[2:]).swapaxes(0, 1)

def from_blocks(a):
    return a.swapaxes(0, 1).reshape(a.shape[1], -1, *a.shape[3:])

def gmlp_uv(a_u, a_v):
    u = heads(jax.nn.gelu(a_u))
    v = heads(jax.nn.gelu(a_v)).astype(f32)
    mu = v.mean(-1, keepdims=True)
    var = jnp.square(v - mu).mean(-1, keepdims=True)
    return u, ((v - mu) * lax.rsqrt(var + LN_EPS)).astype(a_v.dtype)

def gmlp_gate(u, v, w_s, b_s):
    n = v.shape[2]
    w = w_s[:, :n, :n] * jnp.tril(jnp.ones((n, n), w_s.dtype))
    z = jnp.einsum('hts,bcshd->bcthd', w, v) + b_s[:, :n].T[None, None, :, :, None]
    return u * z

def fox_attend(q, cq, qpos, k, v, ck, kpos):
    s = jnp.einsum('bqhd,bkhd->bhqk', q, k, preferred_element_type=f32) * SCALE
    s = s + jnp.swapaxes(cq, 1, 2)[..., :, None] - jnp.swapaxes(ck, 1, 2)[..., None, :]
    s = jnp.where((kpos[None, :] <= qpos[:, None])[None, None], s, NEG)
    p = jax.nn.softmax(s, axis=-1)
    return jnp.einsum('bhqk,bkhd->bqhd', p.astype(v.dtype), v)

def nsa_compress(rows, pe, w1, w2):
    bsz, t, d = rows.shape
    n_cmp = (t - CMP_LEN) // CMP_STRIDE + 1
    idx = np.arange(n_cmp)[:, None] * CMP_STRIDE + np.arange(CMP_LEN)[None, :]
    blocks = (rows[:, idx] + pe).reshape(bsz, n_cmp, CMP_LEN * d)
    return jax.nn.gelu(blocks @ w1) @ w2

def nsa_static(t, n_sel):
    n_cmp = (t - CMP_LEN) // CMP_STRIDE + 1
    start = np.arange(n_cmp) * CMP_STRIDE
    sstart = np.arange(n_sel) * SEL_LEN
    ov = np.minimum(start[:, None] + CMP_LEN, sstart[None, :] + SEL_LEN) - np.maximum(start[:, None], sstart[None, :])
    ov = np.clip(ov, 0, None) / CMP_STRIDE
    return jnp.asarray(start + CMP_LEN - 1, jnp.int32), jnp.asarray(ov, f32)

def nsa_attend(q, qpos, gates, kc, vc, cmp_end, sel_w, ks_blk, vs_blk, kw, vw, wpos):
    bsz, tq = q.shape[0], q.shape[1]
    vis_c = cmp_end[None, :] <= qpos[:, None]
    s_c = jnp.einsum('bqhd,bnd->bqhn', q, kc, preferred_element_type=f32) * SCALE
    p_c = jax.nn.softmax(jnp.where(vis_c[None, :, None, :], s_c, NEG), axis=-1)
    p_c = p_c * jnp.any(vis_c, axis=-1)[None, :, None, None].astype(f32)
    o_c = jnp.einsum('bqhn,bnd->bqhd', p_c.astype(vc.dtype), vc)
    n_sel = ks_blk.shape[1]
    imp = jnp.einsum('bqhn,nm->bqm', p_c, sel_w)
    blk = jnp.arange(n_sel)
    cur = qpos // SEL_LEN
    valid = blk[None, :] * SEL_LEN <= qpos[:, None]
    forced = (blk[None, :] == 0) | (blk[None, :] == cur[:, None]) | (blk[None, :] == cur[:, None] - 1)
    imp = jnp.where(valid[None], jnp.where(forced[None], BIG, imp), -BIG)
    _, top_i = lax.top_k(imp, min(SEL_TOPK, n_sel))
    ok = valid[jnp.arange(tq)[None, :, None], top_i]
    bidx = jnp.arange(bsz)[:, None, None]
    kg = ks_blk[bidx, top_i]
    vg = vs_blk[bidx, top_i]
    pos_g = top_i[..., None] * SEL_LEN + jnp.arange(SEL_LEN)
    m_g = ok[..., None] & (pos_g <= qpos[None, :, None, None])
    s_s = jnp.einsum('bqhd,bqkld->bqhkl', q, kg, preferred_element_type=f32) * SCALE
    p_s = jax.nn.softmax(jnp.where(m_g[:, :, None], s_s, NEG), axis=(-2, -1))
    o_s = jnp.einsum('bqhkl,bqkld->bqhd', p_s.astype(vg.dtype), vg)
    m_w = (wpos[None, :] <= qpos[:, None]) & (wpos[None, :] > qpos[:, None] - WINDOW) & (wpos[None, :] >= 0)
    s_w = jnp.einsum('bqhd,bkd->bqhk', q, kw, preferred_element_type=f32) * SCALE
    p_w = jax.nn.softmax(jnp.where(m_w[None, :, None, :], s_w, NEG), axis=-1)
    o_w = jnp.einsum('bqhk,bkd->bqhd', p_w.astype(vw.dtype), vw)
    g = gates.astype(o_c.dtype)
    o = g[:, :, 0, :, None] * o_c + g[:, :, 1, :, None] * o_s + g[:, :, 2, :, None] * o_w
    return o.reshape(bsz, tq, GROUP_W)

def short_conv(z, past, w):
    zp = jnp.concatenate([past.astype(z.dtype), z], axis=1)
    t = z.shape[1]
    y = sum(w[j] * zp[:, j:j + t] for j in range(CONV_W))
    return y, zp[:, -(CONV_W - 1):]

def moe(x, w_router, w_gate, w_up, w_down):
    shp = x.shape
    xt = x.reshape(-1, shp[-1])
    probs = jax.nn.softmax(jnp.matmul(xt, w_router, preferred_element_type=f32), axis=-1)
    grp_top, _ = lax.top_k(probs.reshape(-1, N_GROUPS, EXP_PER_GROUP), TOP_K)
    g_sel = jnp.argmax(grp_top.sum(-1), axis=-1)
    in_grp = (jnp.arange(N_EXPERTS) // EXP_PER_GROUP)[None, :] == g_sel[:, None]
    top_w, top_i = lax.top_k(jnp.where(in_grp, probs, -1.0), TOP_K)
    top_w = top_w / top_w.sum(-1, keepdims=True)
    gate = jnp.einsum('nk,nke->ne', top_w, jax.nn.one_hot(top_i, N_EXPERTS, dtype=f32))
    h = jax.nn.silu(jnp.einsum('nd,edf->nef', xt, w_gate)) * jnp.einsum('nd,edf->nef', xt, w_up)
    y = jnp.einsum('nef,efd->nd', h * gate.astype(h.dtype)[..., None], w_down)
    return y.reshape(shp)

def post_block(x, mixed, w_out, ln_g, ln_b, w_router, w_gate, w_up, w_down):
    x = layer_norm(DEEPNORM_ALPHA * x + mixed @ w_out, ln_g[0], ln_b[0])
    return layer_norm(DEEPNORM_ALPHA * x + moe(x, w_router, w_gate, w_up, w_down), ln_g[1], ln_b[1])

def prompt_mixers(x, w_in, fox_bias, w_s, b_s, cmp_pe, cmp_w1, cmp_w2, conv_w):
    bsz, seq, _ = x.shape
    n_chunk = seq // CHUNK
    n_blk = seq // Q_BLOCK
    a_u, a_v, b_q, b_k, b_v, b_f, c_q, c_kv, c_g, d_h, d_b, d_c = in_proj(x, w_in)
    u, v = gmlp_uv(a_u, a_v)
    cshape = (bsz, n_chunk, CHUNK, GROUP_HEADS, HEAD_DIM)
    y_a = gmlp_gate(u.reshape(cshape), v.reshape(cshape), w_s, b_s).reshape(bsz, seq, GROUP_W)
    q, k, vv = heads(b_q), heads(b_k), heads(b_v)
    logf = jax.nn.log_sigmoid(b_f.astype(f32) + fox_bias.astype(f32))
    c = jnp.cumsum(logf, axis=1)
    kpos = jnp.arange(seq)
    starts = jnp.arange(n_blk) * Q_BLOCK

    def fox_block(args):
        qi, ci, s0 = args
        return fox_attend(qi, ci, s0 + jnp.arange(Q_BLOCK), k, vv, c, kpos)

    y_b = from_blocks(lax.map(fox_block, (to_blocks(q, n_blk), to_blocks(c, n_blk), starts))).reshape(bsz, seq, GROUP_W)
    qc = heads(c_q)
    gates = jax.nn.sigmoid(c_g.astype(f32)).reshape(bsz, seq, 3, GROUP_HEADS)
    kc, vc, ks, vs, kw, vw = jnp.split(c_kv, 6, axis=-1)
    k_cmp = nsa_compress(kc, cmp_pe[0], cmp_w1[0], cmp_w2[0])
    v_cmp = nsa_compress(vc, cmp_pe[1], cmp_w1[1], cmp_w2[1])
    n_sel = seq // SEL_LEN
    cmp_end, sel_w = nsa_static(seq, n_sel)
    ks_blk = ks.reshape(bsz, n_sel, SEL_LEN, HEAD_DIM)
    vs_blk = vs.reshape(bsz, n_sel, SEL_LEN, HEAD_DIM)
    pad = ((0, 0), (WINDOW, 0), (0, 0))
    kw_pad = jnp.pad(kw, pad)
    vw_pad = jnp.pad(vw, pad)

    def nsa_block(args):
        qi, gi, s0 = args
        kwi = lax.dynamic_slice_in_dim(kw_pad, s0, WINDOW + Q_BLOCK, axis=1)
        vwi = lax.dynamic_slice_in_dim(vw_pad, s0, WINDOW + Q_BLOCK, axis=1)
        wpos = s0 - WINDOW + jnp.arange(WINDOW + Q_BLOCK)
        return nsa_attend(qi, s0 + jnp.arange(Q_BLOCK), gi, k_cmp, v_cmp, cmp_end, sel_w, ks_blk, vs_blk, kwi, vwi, wpos)

    y_c = from_blocks(lax.map(nsa_block, (to_blocks(qc, n_blk), to_blocks(gates, n_blk), starts)))
    y_conv, conv_state = short_conv(d_c * d_h, jnp.zeros((bsz, CONV_W - 1, GROUP_W), x.dtype), conv_w)
    y_d = d_b * y_conv
    mixed = jnp.concatenate([y_a, y_b, y_c, y_d], axis=-1)
    win_keep = min(WINDOW, seq)
    return mixed, (jnp.stack([k, vv], axis=2), logf, jnp.stack([kc, vc, ks, vs], axis=2),
                   jnp.stack([kw, vw], axis=2)[:, seq - win_keep:], conv_state)

def sample_mixers(x, fox_kv_c, fox_lf_c, nsa_kv_c, win_c, conv_c, page_table,
                  w_in, fox_bias, w_s, b_s, cmp_pe, cmp_w1, cmp_w2, conv_w):
    bsz, tn, _ = x.shape
    a_u, a_v, b_q, b_k, b_v, b_f, c_q, c_kv, c_g, d_h, d_b, d_c = in_proj(x, w_in)
    u, v = gmlp_uv(a_u, a_v)
    y_a = gmlp_gate(u[:, None], v[:, None], w_s, b_s).reshape(bsz, tn, GROUP_W)
    q, k, vv = heads(b_q), heads(b_k), heads(b_v)
    logf = jax.nn.log_sigmoid(b_f.astype(f32) + fox_bias.astype(f32))
    kv_past = fox_kv_c[page_table].reshape(bsz, -1, 2, GROUP_HEADS, HEAD_DIM).astype(k.dtype)
    lf_past = fox_lf_c[page_table].reshape(bsz, -1, GROUP_HEADS).astype(f32)
    past = kv_past.shape[1]
    kv_new = jnp.stack([k, vv], axis=2)
    kv_all = jnp.concatenate([kv_past, kv_new], axis=1)
    c_all = jnp.cumsum(jnp.concatenate([lf_past, logf], axis=1), axis=1)
    qpos = past + jnp.arange(tn)
    y_b = fox_attend(q, c_all[:, past:], qpos, kv_all[:, :, 0], kv_all[:, :, 1], c_all,
                     jnp.arange(past + tn)).reshape(bsz, tn, GROUP_W)
    qc = heads(c_q)
    gates = jax.nn.sigmoid(c_g.astype(f32)).reshape(bsz, tn, 3, GROUP_HEADS)
    kc, vc, ks, vs, kw, vw = jnp.split(c_kv, 6, axis=-1)
    rows_new = jnp.stack([kc, vc, ks, vs], axis=2)
    rows_past = nsa_kv_c[page_table].reshape(bsz, -1, 4, HEAD_DIM).astype(rows_new.dtype)
    rows = jnp.concatenate([rows_past, rows_new], axis=1)
    t_all = rows.shape[1]
    k_cmp = nsa_compress(rows[:, :, 0], cmp_pe[0], cmp_w1[0], cmp_w2[0])
    v_cmp = nsa_compress(rows[:, :, 1], cmp_pe[1], cmp_w1[1], cmp_w2[1])
    n_sel = -(-t_all // SEL_LEN)
    sel = jnp.pad(rows[:, :, 2:4], ((0, 0), (0, n_sel * SEL_LEN - t_all), (0, 0), (0, 0)))
    sel = sel.reshape(bsz, n_sel, SEL_LEN, 2, HEAD_DIM)
    cmp_end, sel_w = nsa_static(t_all, n_sel)
    win_keep = win_c.shape[1]
    win = jnp.concatenate([win_c.astype(kw.dtype), jnp.stack([kw, vw], axis=2)], axis=1)
    wpos = past - win_keep + jnp.arange(win_keep + tn)
    y_c = nsa_attend(qc, qpos, gates, k_cmp, v_cmp, cmp_end, sel_w, sel[:, :, :, 0], sel[:, :, :, 1],
                     win[:, :, 0], win[:, :, 1], wpos)
    y_conv, conv_state = short_conv(d_c * d_h, conv_c, conv_w)
    y_d = d_b * y_conv
    mixed = jnp.concatenate([y_a, y_b, y_c, y_d], axis=-1)
    return mixed, (kv_new, logf, rows_new, win[:, -win_keep:], conv_state, v)

def setup_inputs(seed: int = 0) -> dict:
    key = jax.random.key(seed)
    ks = jax.random.split(key, 24)
    n_pages = PAST_LEN // PAGE_SIZE
    n_pool = (DEC_BATCH * n_pages * 5) // 4
    win_cache = min(WINDOW, PAST_LEN)

    def nrm(k, shape, s):
        return jax.random.normal(k, shape, f32) * s

    offs = np.cumsum((0,) + SPLIT_SIZES)
    col = np.ones(P_IN, np.float32)
    col[offs[4]:offs[4] + GROUP_W] = DEEPNORM_BETA
    for j in (1, 3, 5):
        o = offs[7] + j * HEAD_DIM
        col[o:o + HEAD_DIM] = DEEPNORM_BETA
    page_table = jax.random.permutation(ks[7], n_pool)[:DEC_BATCH * n_pages]
    return {
        'x_prompt': nrm(ks[0], (BATCH, SEQ, D_MODEL), 1.0),
        'x_sample': nrm(ks[1], (DEC_BATCH, DEC_SEQ, D_MODEL), 1.0),
        'cache_fox_kv': nrm(ks[2], (DEPTH, n_pool, PAGE_SIZE, 2, GROUP_HEADS, HEAD_DIM), 1.0),
        'cache_fox_logf': jax.nn.log_sigmoid(nrm(ks[3], (DEPTH, n_pool, PAGE_SIZE, GROUP_HEADS), 1.0) + FORGET_BIAS_INIT),
        'cache_nsa_kv': nrm(ks[4], (DEPTH, n_pool, PAGE_SIZE, 4, HEAD_DIM), 1.0),
        'state_nsa_win': nrm(ks[5], (DEPTH, DEC_BATCH, win_cache, 2, HEAD_DIM), 1.0),
        'state_conv': nrm(ks[6], (DEPTH, DEC_BATCH, CONV_W - 1, GROUP_W), 1.0),
        'page_table': page_table.reshape(DEC_BATCH, n_pages).astype(jnp.int32),
        'w_in': nrm(ks[8], (DEPTH, D_MODEL, P_IN), D_MODEL ** -0.5) * jnp.asarray(col),
        'fox_b_f': FORGET_BIAS_INIT + nrm(ks[9], (DEPTH, GROUP_HEADS), 0.1),
        'gmlp_w_s': nrm(ks[10], (DEPTH, GROUP_HEADS, CHUNK, CHUNK), CHUNK ** -0.5),
        'gmlp_b_s': 1.0 + nrm(ks[11], (DEPTH, GROUP_HEADS, CHUNK), 0.1),
        'nsa_cmp_pe': nrm(ks[12], (DEPTH, 2, CMP_LEN, HEAD_DIM), 0.1),
        'nsa_cmp_w1': nrm(ks[13], (DEPTH, 2, CMP_LEN * HEAD_DIM, CMP_HID), (CMP_LEN * HEAD_DIM) ** -0.5),
        'nsa_cmp_w2': nrm(ks[14], (DEPTH, 2, CMP_HID, HEAD_DIM), CMP_HID ** -0.5),
        'conv_w': nrm(ks[15], (DEPTH, CONV_W, GROUP_W), CONV_W ** -0.5),
        'w_out': nrm(ks[16], (DEPTH, D_MODEL, D_MODEL), D_MODEL ** -0.5 * DEEPNORM_BETA),
        'ln_g': 1.0 + nrm(ks[17], (DEPTH, 2, D_MODEL), 0.05),
        'ln_b': nrm(ks[18], (DEPTH, 2, D_MODEL), 0.02),
        'w_router': nrm(ks[19], (D_MODEL, N_EXPERTS), D_MODEL ** -0.5),
        'w_exp_gate': nrm(ks[20], (DEPTH, N_EXPERTS, D_MODEL, D_EXPERT), D_MODEL ** -0.5),
        'w_exp_up': nrm(ks[21], (DEPTH, N_EXPERTS, D_MODEL, D_EXPERT), D_MODEL ** -0.5 * DEEPNORM_BETA),
        'w_exp_down': nrm(ks[22], (DEPTH, N_EXPERTS, D_EXPERT, D_MODEL), D_EXPERT ** -0.5 * DEEPNORM_BETA),
    }

def reference(x_prompt, x_sample, cache_fox_kv, cache_fox_logf, cache_nsa_kv, state_nsa_win, state_conv, page_table,
              w_in, fox_b_f, gmlp_w_s, gmlp_b_s, nsa_cmp_pe, nsa_cmp_w1, nsa_cmp_w2, conv_w, w_out, ln_g, ln_b,
              w_router, w_exp_gate, w_exp_up, w_exp_down):
    xp, xs = x_prompt, x_sample
    st_p = [[] for _ in range(5)]
    st_s = [[] for _ in range(6)]
    for l in range(DEPTH):
        mp, sp = prompt_mixers(xp, w_in[l], fox_b_f[l], gmlp_w_s[l], gmlp_b_s[l], nsa_cmp_pe[l], nsa_cmp_w1[l],
                               nsa_cmp_w2[l], conv_w[l])
        ms, ss = sample_mixers(xs, cache_fox_kv[l], cache_fox_logf[l], cache_nsa_kv[l], state_nsa_win[l], state_conv[l],
                               page_table, w_in[l], fox_b_f[l], gmlp_w_s[l], gmlp_b_s[l], nsa_cmp_pe[l], nsa_cmp_w1[l],
                               nsa_cmp_w2[l], conv_w[l])
        xp = post_block(xp, mp, w_out[l], ln_g[l], ln_b[l], w_router, w_exp_gate[l], w_exp_up[l], w_exp_down[l])
        xs = post_block(xs, ms, w_out[l], ln_g[l], ln_b[l], w_router, w_exp_gate[l], w_exp_up[l], w_exp_down[l])
        for lst, a in zip(st_p, sp):
            lst.append(a)
        for lst, a in zip(st_s, ss):
            lst.append(a)
    fox_kv_p, fox_lf_p, nsa_kv_p, nsa_win_p, conv_p = [jnp.stack(a, axis=0) for a in st_p]
    fox_kv_s, fox_lf_s, nsa_kv_s, nsa_win_s, conv_s, gmlp_v_s = [jnp.stack(a, axis=0) for a in st_s]
    return (xp, xs, fox_kv_p, fox_kv_s, fox_lf_p, fox_lf_s, nsa_kv_p, nsa_kv_s, nsa_win_p, nsa_win_s, conv_p, conv_s, gmlp_v_s)


_drawn_inputs = setup_inputs


def setup_inputs(seed=0):
    import zlib

    import numpy as np

    out = dict(_drawn_inputs(seed))
    spreads = {}
    factors = {}
    for name, (base, spread) in spreads.items():
        noise = np.random.default_rng([zlib.crc32(name.encode()), seed]).standard_normal(out[name].shape)
        drawn = base * np.exp(spread * noise) if base else spread * noise
        out[name] = __import__('jax').numpy.asarray(drawn.astype(out[name].dtype))
    for name, factor in factors.items():
        out[name] = (out[name] * factor).astype(out[name].dtype)
    return out
```

```python
from contextlib import ExitStack

import concourse.bass as bass
from concourse import mybir

ALU = mybir.AluOpType
ACT = mybir.ActivationFunctionType
F32 = mybir.dt.float32
BF16 = mybir.dt.bfloat16
I32 = mybir.dt.int32
AX = mybir.AxisListType

P = 128
NEG = -1e30
LN_EPS = 1e-5


def build(nc, x_prompt, x_sample, cache_fox_kv, cache_fox_logf, cache_nsa_kv, state_nsa_win, state_conv,
          page_table, w_in, fox_b_f, gmlp_w_s, gmlp_b_s, nsa_cmp_pe, nsa_cmp_w1, nsa_cmp_w2, conv_w, w_out,
          ln_g, ln_b, w_router, w_exp_gate, w_exp_up, w_exp_down, *outs):
    (y_prompt, y_sample, fox_kv_p, fox_kv_s, fox_lf_p, fox_lf_s, nsa_kv_p, nsa_kv_s, nsa_win_p, nsa_win_s,
     conv_p, conv_s, gmlp_v_s) = outs

    SEQ, D = x_prompt.shape[1], x_prompt.shape[2]
    NB, TN = x_sample.shape[0], x_sample.shape[1]
    H, DH = 4, 64
    GW = H * DH
    KD = D // P
    NT = SEQ // P
    TILES = NT + 1
    NS = NB * TN
    TOK = SEQ + NS
    PAST = state_nsa_win.shape[2]
    PAGE = cache_nsa_kv.shape[2]
    NPG = PAST // PAGE
    NPOOL = cache_nsa_kv.shape[1]
    WINDOW = 512
    assert PAGE == P and NS == 64 and PAST == WINDOW
    SCALE = DH ** -0.5
    rows_of = [P] * NT + [NS]

    A_U, A_V, B_Q, B_K, B_V, B_F = 0, GW, 2 * GW, 3 * GW, 4 * GW, 5 * GW
    C_Q = B_F + H
    C_KV = C_Q + GW
    C_G = C_KV + 6 * DH
    D_H = C_G + 3 * H
    D_B, D_C = D_H + GW, D_H + 2 * GW

    ctx = ExitStack()
    with ctx:
        def sb(name, shape, dt=F32):
            return ctx.enter_context(nc.sbuf_tensor(name, shape, dt))

        def sem(name):
            return ctx.enter_context(nc.semaphore(name))

        psum_all = ctx.enter_context(nc.psum_tensor("psum_all", [P, 8, 512], F32))
        psum = [psum_all[:, i, :] for i in range(8)]

        def banks(i, n):
            return psum_all[:, i:i + n, :].rearrange("p i n -> p (i n)")

        arena = sb("arena", [P, 47084])

        def at(off, *dims, part=P):
            n = 1
            for d in dims:
                n *= d
            v = arena[0:part, off:off + n]
            names = " ".join(f"d{i}" for i in range(len(dims)))
            return v.rearrange(f"p ({names}) -> p {names}", **{f"d{i}": d for i, d in enumerate(dims)}) if len(dims) > 1 else v

        R_X = 0
        R_W = R_X + KD * TOK
        R_FOX = R_W + 2 * KD * 512
        R_NQ = R_FOX + 2 * H * SEQ
        R_XR = R_NQ + H * SEQ
        R_UV = R_XR + 2 * D + 2 * 512
        R_FV = R_UV + TILES * 2 * GW
        R_NR = R_FV + TILES * GW
        R_SK = R_NR + TILES * (6 * DH + 12)
        R_YD = R_SK + 2 * TOK

        ident = sb("ident", [P, P])
        ident_bf = sb("ident_bf", [P, P], BF16)
        ones = sb("ones", [P, P])
        tri_u = sb("tri_u", [P, P])

        causal_m = sb("causal_m", [P, P], BF16)
        far_m = sb("far_m", [P, P], BF16)
        zeros_bf = sb("zeros_bf", [P, P], BF16)

        x_rows = at(R_XR, 2, D)
        xT = at(R_X, KD, TOK)
        w_buf = at(R_W, 2, KD * 512)
        uv = at(R_UV, TILES, 2 * GW)
        qk_rows = at(R_XR + 2 * D, 2, 2 * GW)
        foxT_q = at(R_FOX, H, SEQ, part=DH + 2)
        foxT_k = at(R_FOX + H * SEQ, H, SEQ, part=DH + 2)
        nsaT_q = at(R_NQ, H, SEQ, part=DH)
        fox_v = at(R_FV, TILES, GW)
        nsa_rows = at(R_NR, TILES, 6 * DH + 12)
        b_f = sb("b_f", [P, H, TILES])
        selT_k = at(R_SK, TOK, part=DH)
        winT_k = at(R_SK + TOK, TOK, part=DH)
        yd_T = at(R_YD, 2, TOK)

        ws_T = sb("ws_T", [P, H, P])
        ws_rows = qk_rows[:, 0, :].rearrange("p (h s) -> p h s", h=H)
        ws_s = sb("ws_s", [NS, H, NS])
        bs = sb("bs", [P, 2, H])
        ln_stat = sb("ln_stat", [P, TILES, H, 2])
        ln_sq = sb("ln_sq", [P, GW])
        lnc = sb("lnc", [P, 4])
        cw = sb("cw", [P, 2, 3])
        tail_w = R_W + KD * 512 + KD * 3 * P
        conv_y = at(tail_w, 512)
        dh_T = [at(tail_w + 512, 512), at(R_XR + 2 * (2 + SEQ), 512), at(R_XR + 2 * (2 + SEQ) + 512, NS)]
        z_p = at(R_XR, 2, 2 + SEQ)
        z_s = sb("z_s", [P, 2, NB, 2 + TN])

        foxS_q = sb("foxS_q", [P, 2, NB, H, TN])
        foxS_k = sb("foxS_k", [P, 2, NS])
        nsaS_q = sb("nsaS_q", [DH, NB, H, TN])

        bias_f = sb("bias_f", [P, H])
        lf_x = sb("lf_x", [P, H, TILES])
        lf_e = sb("lf_e", [P, H, TILES])
        lf = sb("lf", [P, H, TILES])
        lf_rows = sb("lf_rows", [P, TILES, H])
        carry = sb("carry", [P, H, NT])
        cum = sb("cum", [P, H, NT])
        cum_T = sb("cum_T", [H * NT, 2, P])

        P_buf = at(R_W, 2, SEQ)
        PT_buf = at(R_W + 2 * SEQ, 2, SEQ)
        gates = sb("gates", [P, TILES, 3, H])
        neg_max = sb("neg_max", [P, 4])
        row_sum = sb("row_sum", [P, 4])
        recip = sb("recip", [P, 4])
        coef = sb("coef", [P, 4])
        win_tiles = WINDOW // P
        jobs = [("fox", qt, h) for qt in range(NT) for h in range(H)]
        N_FOX = len(jobs)
        jobs += [(br, qt, h) for qt in range(NT) for h in range(H) for br in ("sel", "win")]
        J = len(jobs)

        def keys_of(i):
            br, qt, _ = jobs[i]
            k0 = max(0, qt - win_tiles) if br == "win" else 0
            return k0, qt + 1 - k0

        def wide_jobs(i):
            return sum(keys_of(n)[1] > 4 for n in range(i + 1))

        x_biased = sem("x_biased")
        lf_parts = sem("lf_parts")
        lf_ready = sem("lf_ready")
        cum_done = sem("cum_done")
        c_ready = sem("c_ready")
        cT_done = sem("cT_done")
        cT_copied = sem("cT_copied")
        c_rows = sem("c_rows")
        gate_x = sem("gate_x")
        gates_ready = sem("gates_ready")
        s_ready = sem("s_ready")
        max_ready = sem("max_ready")
        p_ready = sem("p_ready")
        p_turned = sem("p_turned")
        pt_dve = sem("pt_dve")
        pt_act = sem("pt_act")
        o_ready = sem("o_ready")
        y_done = sem("y_done")

        CMP_LEN, UNIT = nsa_cmp_pe.shape[2], 16
        HID = nsa_cmp_w1.shape[3]
        U_P, U_S = SEQ // UNIT, PAST // UNIT
        NU = U_P + NB * U_S
        NC_P, NC_S = U_P - 1, U_S - 1
        NCB = NU - 1
        kcvc_T = at(R_X, UNIT, NU + 2)
        cmp_w1 = at(R_W + 4 * SEQ, CMP_LEN, HID)
        cmp_w2 = sb("cmp_w2", [HID, 2, DH])
        pe_rows = sb("pe_rows", [CMP_LEN, 2 * DH])
        hid_bias = sb("hid_bias", [HID, 2])
        hid = at(R_XR, 2, NU)
        cmpT_k = at(R_XR + 2 * NU, NU, part=DH)
        cmp_v_p = at(R_XR + 3 * NU, DH)
        cmp_v_s = at(R_XR + 3 * NU + DH, NB, DH)
        lf_rep = at(R_XR + 3 * NU + DH + NB * DH, 2, NPG, P)
        nsa_cache = at(R_FOX, NB * NPG, 4 * DH)
        fox_cache = at(R_X, 4 * NPG, 2 * GW)
        win_cache = at(R_W + 4 * SEQ, NB, NPG, 2 * DH)
        lf_past = sb("lf_past", [P, NB * NPG, H])
        pages = sb("pages", [1, NB * NPG], I32)
        cmp_m = sb("cmp_m", [P, NT, NC_P], BF16)
        any_cmp = sb("any_cmp", [P, 1])
        head_v = sb("head_v", [P, 4, H])

        sjobs = [("fox", 0), ("sel", 0), ("sel", 1), ("win", 0), ("win", 1), ("cmp", 0), ("cmp", 1), ("fox", 1)]
        units = []
        for u, (br, g) in enumerate(sjobs):
            if br != "cmp":
                units += [(u, b, pr) for b in range(4) for pr in range(2 if br == "fox" else 1)]
        SW = PAST + NS
        Ps = at(R_W, 2, SW)
        PTs = at(R_W + 2 * SW, NPG + 1, P)
        KTs = at(R_W + 2 * SW + (NPG + 1) * P, 4, PAST)
        o_m = at(R_NQ + D, 4, GW)
        o_nsa = at(R_NQ + D + 4 * GW, 2, DH)
        o_coef = at(R_NQ + D + 4 * GW + 2 * DH, 2, H)
        later = sb("later", [P, PAST])
        same = sb("same", [NS, NS])
        new_m = sb("new_m", [NS, NS], BF16)
        left_m = sb("left_m", [NS, TN], BF16)
        left_f = sb("left_f", [NS, TN])
        spread = sb("spread", [NS, 2, P])
        spread_bf = sb("spread_bf", [NS, 2, P], BF16)
        gather = sb("gather", [P, 2, NS])
        lf_new = sb("lf_new", [NS, 2, P])
        head_m = sb("head_m", [P, H])
        gate_s = sb("gate_s", [P, 2, 3])
        gate_t = sb("gate_t", [P, 3, H])
        s_stat = sb("s_stat", [P, 2, 4])

        pages_loaded = sem("pages_loaded")
        nsa_cache_in = sem("nsa_cache_in")
        cmp_w_in = sem("cmp_w_in")
        fox_cache_in = sem("fox_cache_in")
        win_cache_in = sem("win_cache_in")
        masks_ready = sem("masks_ready")
        cc_turned = sem("cc_turned")
        cc_dve = sem("cc_dve")
        cc_act = sem("cc_act")
        pe_turned = sem("pe_turned")
        pe_copied = sem("pe_copied")
        comp_done = sem("comp_done")
        hid_ready = sem("hid_ready")
        cmp_proj = sem("cmp_proj")
        cmp_kv = sem("cmp_kv")
        c_scored = sem("c_scored")
        c_shifted = sem("c_shifted")
        c_exp = sem("c_exp")
        c_turned = sem("c_turned")
        c_pt = sem("c_pt")
        c_out = sem("c_out")
        c_added = sem("c_added")
        conv_stored = sem("conv_stored")
        s_masks = sem("s_masks")
        s_setup = sem("s_setup")
        s_setup_used = sem("s_setup_used")
        s_ops = sem("s_ops")
        kt_turned = sem("kt_turned")
        kt_dve = sem("kt_dve")
        kt_act = sem("kt_act")
        kt_used = sem("kt_used")
        ss_ready = sem("ss_ready")
        smax_ready = sem("smax_ready")
        sp_ready = sem("sp_ready")
        sp_turned = sem("sp_turned")
        spt_ready = sem("spt_ready")
        so_ready = sem("so_ready")
        so_done = sem("so_done")
        om_ready = sem("om_ready")
        ys_ready = sem("ys_ready")
        ys_copied = sem("ys_copied")

        ALPHA = 2 ** 0.25
        NE, F = w_router.shape[1], w_exp_gate.shape[3]
        EG = 4
        layer = at(R_W, TILES, D)
        R_WO = R_W + TILES * D
        wo = at(R_WO, KD, D)
        x1T = at(R_X, KD, TOK)
        x_res = at(R_NR, 2, D)
        mix_T = at(R_NR + 2 * D, 2, 6, P)
        ln_row = [at(R_NR + 2 * D + 12 * P, 2, D), at(R_WO + 2 * KD * F + F // P * D, 2, D)]
        ln_s = sb("ln_s", [P, 2, 4])
        w_r = sb("w_r", [P, KD, NE])
        R_R = R_UV + 18 * P
        probs, gate, *r16 = [at(R_R + i * TILES * NE, TILES, NE) for i in range(5)]
        r4 = [at(R_R + 5 * TILES * NE + i * TILES * EG, TILES, EG) for i in range(4)]
        R_R1 = R_R + 5 * TILES * NE + 4 * TILES * EG
        r1 = [at(R_R1 + i * TILES, TILES) for i in range(3)]
        rank16 = at(R_R1 + 3 * TILES, NE)
        rank16_i = sb("rank16_i", [P, NE], I32)

        wo_in = sem("wo_in")
        x_res_in = [sem(f"x_res_in{i}") for i in range(2)]
        ln_in = sem("ln_in")
        router_in = sem("router_in")
        mix_turned = sem("mix_turned")
        mix_dve = sem("mix_dve")
        mix_act = sem("mix_act")
        r_done = sem("r_done")
        mean_ready = sem("mean_ready")
        rstd2_ready = sem("rstd2_ready")
        normed = sem("normed")
        x1_turned = sem("x1_turned")
        x1T_dve = sem("x1T_dve")
        x1T_act = sem("x1T_act")
        scaled = sem("scaled")
        logits_done = sem("logits_done")
        rmax_ready = sem("rmax_ready")
        rexp_ready = sem("rexp_ready")
        gate_ready = sem("gate_ready")

        R_EW = [R_WO, R_WO + KD * D]
        ew_g = [at(r, KD, F) for r in R_EW]
        ew_u = [at(r + KD * F, KD, F) for r in R_EW]
        ew_d = [at(r + 2 * KD * F, F // P, D) for r in R_EW]
        CH = [(0, 3), (3, 3), (6, 3)]
        sil = at(R_UV, 2, 3 * P)
        h_T = at(R_UV + 6 * P, 2, 2, 3 * P)
        ew_in = [sem(f"ew_in{i}") for i in range(2)]
        gu_done = sem("gu_done")
        sil_ready = sem("sil_ready")
        h_ready = sem("h_ready")
        ye_done = sem("ye_done")
        ye_added = sem("ye_added")

        consts_ready = sem("consts_ready")
        x_loaded = [sem(f"x_loaded{i}") for i in range(2)]
        w_loaded = [sem(f"w_loaded{i}") for i in range(2)]
        small_loaded = sem("small_loaded")
        turned = sem("turned")
        turn_copied = sem("turn_copied")
        proj_done = sem("proj_done")
        proj_copied = sem("proj_copied")
        dve_step = sem("dve_step")
        var_ready = sem("var_ready")
        lnv_ready = sem("lnv_ready")
        rstd_ready = sem("rstd_ready")
        v_ready = sem("v_ready")
        zg_done = sem("zg_done")
        zg_used = sem("zg_used")
        ws_turned = sem("ws_turned")
        ws_copied = sem("ws_copied")
        ws_masked = sem("ws_masked")
        z_used = sem("z_used")
        yd_ready = sem("yd_ready")
        out_sem = sem("out_stored")
        outs_n = [0]

        GROUPS = [(A_U, 512), (B_Q, 512), (B_V, GW + H), (C_Q, GW), (C_KV, 6 * DH + 12)]
        LOADS = [[(c, w)] for c, w in GROUPS] + [[(D_H + f * P, P), (D_C + f * P, P), (D_B + f * P, P)]
                                                 for f in range(2)]
        NRG = len(GROUPS)
        N_ROWJ = NRG * TILES
        CHUNKS = [(0, 512), (512, 512), (SEQ, NS)]

        def w_view(g):
            n = sum(w for _, w in LOADS[g])
            return w_buf[:, g % 2, 0:KD * n].rearrange("p (k n) -> p k n", k=KD)

        def tok0(t):
            return t * P

        def w_last_use(g):
            return (g + 1) * TILES if g < NRG else N_ROWJ + 9 * (g - NRG + 1)

        k_stored = [sem(f"k_stored{i}") for i in range(2)]
        lf_past_in = sem("lf_past_in")

        def tail(sp):
            sp.wait_ge(k_stored[0], 16 * ((TILES + 1) // 2))
            sp.wait_ge(k_stored[1], 16 * (TILES // 2))
            sp.wait_ge(out_sem, 16 * outs_n[0])
            sp.wait_ge(conv_stored, 16 * 2 * (1 + NB))

        pool_step = sem("pool_step")
        ws_s_ready = sem("ws_s_ready")

        ws_loaded = sem("ws_loaded")

        def gate_rows(pe, t):
            n = rows_of[t]
            bank = psum[4 + t % 2]
            pe.wait_ge(v_ready, t + 1)
            if t == 0:
                pe.wait_ge(ws_masked, 1)
                pe.wait_ge(turn_copied, 2 * TILES - 1)
            if t == NT:
                pe.wait_ge(ws_s_ready, 16 * NB)
            if t >= 2:
                pe.wait_ge(zg_used, t - 1)
            for h in range(H):
                w = ws_T[:, h, :] if t < NT else ws_s[:, h, :]
                ins = nc.tensor.matmul(bank[0:n, h * DH:(h + 1) * DH], w, uv[0:n, t, GW + h * DH:GW + (h + 1) * DH],
                                       start=True, stop=True)
            ins.then_inc(zg_done, 1)

        def w_count(g):
            return 16 * sum(len(LOADS[i]) for i in range(g % 2, g + 1, 2))

        def bank_free(pe, j):
            i = j - 4
            if i < N_ROWJ:
                pe.wait_ge(proj_copied, i + 1)
                return
            f, part, c = (i - N_ROWJ) // 9, (i - N_ROWJ) % 9 // 3, (i - N_ROWJ) % 3
            if part == 0:
                pe.wait_ge(proj_copied, N_ROWJ + 3 * f + c + 1)
            else:
                pe.wait_ge(z_used, 6 * f + 3 * (part - 1) + c + 1)

        def copy_units(copy, q):
            n = 512 // UNIT
            return copy(kcvc_T[:, :, q * n:(q + 1) * n],
                        psum[4 + q % 2][:].rearrange("p (u r) -> p r u", r=UNIT))

        def copy_keys(eng, copy, k):
            rows = P if sjobs[units[k][0]][0] == "fox" else DH
            eng.wait_ge(kt_turned, k + 1)
            if k >= 4:
                eng.wait_ge(kt_used, k - 3)
            return copy(KTs[0:rows, k % 4, :], psum[4 + k % 2][0:rows, :])

        act_step = sem("act_step")
        y_stored = sem("y_stored")

        def expert_loader(sp):
            def load(e):
                i = e % 2
                sp.dma_start(ew_g[i][:], w_exp_gate[0, e].rearrange("(k p) f -> p k f", p=P)).then_inc(ew_in[i], 16)
                sp.dma_start(ew_u[i][:], w_exp_up[0, e].rearrange("(k p) f -> p k f", p=P)).then_inc(ew_in[i], 16)
                sp.dma_start(ew_d[i][:], w_exp_down[0, e].rearrange("(k p) n -> p k n", p=P)).then_inc(ew_in[i], 16)
            return load

        block = ctx.enter_context(nc.Block())

        @block.sync
        def _(sp):
            def load_x(t):
                if t >= 2:
                    sp.wait_ge(turned, t - 1)
                src = x_prompt[0, tok0(t):tok0(t) + P, :] if t < NT else x_sample.rearrange("b t d -> (b t) d")
                sp.dma_start(x_rows[0:rows_of[t], t % 2, :], src).then_inc(x_loaded[t % 2], 16)

            def load_w(g):
                if g >= 2:
                    sp.wait_ge(proj_done, w_last_use(g - 2))
                v, at = w_view(g), 0
                for c, w in LOADS[g]:
                    sp.dma_start(v[:, :, at:at + w], w_in[0, :, c:c + w].rearrange("(k p) n -> p k n", p=P)
                                 ).then_inc(w_loaded[g % 2], 16)
                    at += w

            load_x(0)
            load_x(1)
            load_w(0)
            load_w(1)
            for t in range(2, TILES):
                load_x(t)

            def store(dst, src, sem_=out_sem):
                outs_n[0] += 1
                sp.dma_start(dst, src).then_inc(sem_, 16)

            def store_slow(dst, src):
                sp.dma_start(dst, src, allow_slow_non_contiguous=True).then_inc(conv_stored, 16)

            j = 0
            for g in range(NRG):
                if g >= 1:
                    load_w(g + 1)
                for t in range(TILES):
                    j += 1
                    n = rows_of[t]
                    if g == 1:
                        sp.wait_ge(proj_copied, j)
                        kr = qk_rows[0:n, t % 2, GW:2 * GW].rearrange("p (h d) -> p h d", h=H)
                        dst = (fox_kv_p[0, 0, tok0(t):tok0(t) + P, 0] if t < NT
                               else fox_kv_s[0, :, :, 0].rearrange("b t h d -> (b t) h d"))
                        sp.dma_start(dst, kr).then_inc(k_stored[t % 2], 16)
                if g == 2:
                    sp.wait_ge(proj_copied, j)
                    store(fox_kv_p[0, 0, :, 1].rearrange("(t p) h d -> p t (h d)", p=P), fox_v[:, 0:NT, :])
                    store(fox_kv_s[0, :, :, 1].rearrange("b t h d -> (b t) (h d)"), fox_v[0:NS, NT, :])
                if g == 4:
                    sp.wait_ge(lf_ready, 2)
                    sp.wait_ge(cT_copied, 1)
                    sp.dma_start(foxT_q[DH:DH + 1, :, :].rearrange("o h (t n) -> o (h t) n", n=P),
                                 cum_T[:, 0, :]).then_inc(c_rows, 16)
                    sp.dma_start(foxT_k[DH + 1:DH + 2, :, :].rearrange("o h (t n) -> o (h t) n", n=P),
                                 cum_T[:, 1, :]).then_inc(c_rows, 16)
                    sp.wait_ge(proj_copied, j)
                    store(nsa_kv_p[0, 0].rearrange("(t p) c d -> p t (c d)", p=P), nsa_rows[:, 0:NT, 0:4 * DH])
                    store(nsa_kv_s[0].rearrange("b t c d -> (b t) (c d)"), nsa_rows[0:NS, NT, 0:4 * DH])
                    keep = WINDOW // P
                    store(nsa_win_p[0, 0].rearrange("(t p) c d -> p t (c d)", p=P),
                          nsa_rows[:, NT - keep:NT, 4 * DH:6 * DH])
                    for b in range(NB):
                        store(nsa_win_s[0, b, PAST - TN:PAST].rearrange("t c d -> t (c d)"),
                              nsa_rows[TN * b:TN * b + TN, NT, 4 * DH:6 * DH])
                    store(nsa_win_s[0, :, 0:PAST - TN].rearrange("b t c d -> b (t c d)"),
                          state_nsa_win[0, :, TN:PAST].rearrange("b t c d -> b (t c d)"))

            load_w(NRG + 1)
            store(fox_lf_p[0, 0].rearrange("(t p) h -> p t h", p=P), lf_rows[:, 0:NT, :])
            store(fox_lf_s[0].rearrange("b t h -> (b t) h"), lf_rows[0:NS, NT, :])
            sp.wait_ge(v_ready, TILES)
            store(gmlp_v_s[0].rearrange("b t h d -> (b t) (h d)"), uv[0:NS, NT, GW:2 * GW])
            sp.wait_ge(z_used, 12)
            for f in range(2):
                fs = slice(f * P, f * P + P)
                store_slow(conv_p[0, 0, :, fs].rearrange("j p -> p j"), z_p[:, f, SEQ:SEQ + 2])
                for b in range(NB):
                    store_slow(conv_s[0, b, :, fs].rearrange("j p -> p j"), z_s[:, f, b, TN:TN + 2])

            def load_pages(cache, dst, n, first, done):
                with sp.Fori(0, n) as i:
                    page = sp.value_load(pages[0:1, bass.ds(i + first, 1)], min_val=0, max_val=NPOOL - 1)
                    sp.dma_start(dst[:, bass.ds(i, 1), :], cache[bass.ds(page, 1)]).then_inc(done, 16)

            sp.dma_start(pages[:], page_table.rearrange("(o b) n -> o (b n)", o=1)).then_inc(pages_loaded, 16)
            sp.wait_ge(z_used, 12)
            for c in range(2):
                sp.dma_start(cmp_w1[c * DH:(c + 1) * DH], nsa_cmp_w1[0, c].rearrange("(l d) n -> d l n", d=DH)
                             ).then_inc(cmp_w_in, 16)
                sp.dma_start(pe_rows[:, c * DH:(c + 1) * DH], nsa_cmp_pe[0, c]).then_inc(cmp_w_in, 16)
                sp.dma_start(cmp_w2[:, c, :], nsa_cmp_w2[0, c]).then_inc(cmp_w_in, 16)
            sp.wait_ge(pages_loaded, 16)
            load_pages(cache_fox_logf[0].rearrange("n p h -> n p h"), lf_past, NB * NPG, 0, lf_past_in)
            sp.wait_ge(s_ready, N_FOX)
            load_pages(cache_nsa_kv[0].rearrange("n p c d -> n p (c d)"), nsa_cache, NB * NPG, 0, nsa_cache_in)
            sp.wait_ge(comp_done, 2)
            fox_pages = cache_fox_kv[0].rearrange("n p c h d -> n p (c h d)")
            load_pages(fox_pages, fox_cache, 4 * NPG, 0, fox_cache_in)
            for b in range(NB):
                sp.dma_start(win_cache[:, b], state_nsa_win[0, b].rearrange("(n p) c d -> p n (c d)", p=P)
                             ).then_inc(win_cache_in, 16)
            sp.wait_ge(so_ready, 1)
            load_pages(fox_pages, fox_cache, 4 * NPG, 4 * NPG, fox_cache_in)
            sp.dma_start(w_r[:], w_router.rearrange("(k p) e -> p k e", p=P)).then_inc(router_in, 16)
            sp.wait_ge(so_ready, 3)
            sp.dma_start(wo[:], w_out[0].rearrange("(k p) n -> p k n", p=P)).then_inc(wo_in, 16)
            sp.wait_ge(so_ready, 5)
            sp.wait_ge(out_sem, 16 * outs_n[0])

            def rows_dram(x_p, x_s, t):
                return x_p[0, tok0(t):tok0(t) + P, :] if t < NT else x_s.rearrange("b t d -> (b t) d")

            sp.wait_ge(so_ready, len(sjobs))
            for i, row in enumerate((ln_g, ln_b)):
                sp.dma_start(ln_row[0][:, i, :], row[0, 0].partition_broadcast(P)).then_inc(ln_in, 16)
            for t in range(TILES):
                if t >= 2:
                    sp.wait_ge(mean_ready, t - 1)
                sp.dma_start(x_res[0:rows_of[t], t % 2, :], rows_dram(x_prompt, x_sample, t)
                             ).then_inc(x_res_in[t % 2], 16)
                if t == 2:
                    load_expert = expert_loader(sp)
                    sp.wait_ge(ys_ready, 1)
                    load_expert(1)
            sp.wait_ge(r_done, TILES)
            load_expert(0)
            for i, row in enumerate((ln_g, ln_b)):
                sp.dma_start(ln_row[1][:, i, :], row[0, 1].partition_broadcast(P)).then_inc(ln_in, 16)
            for e in range(2, NE):
                sp.wait_ge(ye_done, TILES * (e - 1))
                load_expert(e)
            for t in range(TILES):
                sp.wait_ge(normed, TILES + t + 1)
                sp.dma_start(rows_dram(y_prompt, y_sample, t), layer[0:rows_of[t], t, :]).then_inc(y_stored, 16)
            sp.wait_ge(y_stored, 16 * TILES)
            tail(sp)

        @block.gpsimd
        def _(pool):
            pool.memset(ident[:], 0.0).then_inc(pool_step, 1)
            pool.memset(ident_bf[:], 0.0).then_inc(pool_step, 1)
            pool.memset(ones[:], 1.0).then_inc(pool_step, 1)
            pool.memset(zeros_bf[:], 0.0).then_inc(pool_step, 1)
            pool.wait_ge(pool_step, 4)
            for m in (ident, ident_bf):
                pool.affine_select(out=m[:], in_=m[:], compare_op=ALU.not_equal, fill=1.0, base=0,
                                   pattern=[[-1, P]], channel_multiplier=1).then_inc(consts_ready, 1)
            pool.affine_select(out=tri_u[:], in_=ones[:], compare_op=ALU.is_ge, fill=0.0, base=0,
                               pattern=[[1, P]], channel_multiplier=-1).then_inc(consts_ready, 1)
            pool.affine_select(out=causal_m[:], in_=zeros_bf[:], compare_op=ALU.is_ge, fill=NEG, base=0,
                               pattern=[[-1, P]], channel_multiplier=1).then_inc(consts_ready, 1)
            pool.affine_select(out=far_m[:], in_=zeros_bf[:], compare_op=ALU.is_gt, fill=NEG, base=0,
                               pattern=[[1, P]], channel_multiplier=-1).then_inc(consts_ready, 1)
            pool.memset(cmp_m[:], 0.0).then_inc(pool_step, 1)
            pool.memset(same[:], 1.0).then_inc(pool_step, 1)
            pool.memset(later[:], 1.0).then_inc(pool_step, 1)
            pool.memset(spread[:], 0.0).then_inc(pool_step, 1)
            pool.memset(lf_new[:], 1.0).then_inc(pool_step, 1)
            pool.wait_ge(pool_step, 9)
            pool.affine_select(out=cmp_m[:], in_=cmp_m[:], compare_op=ALU.is_ge, fill=NEG, base=1 - CMP_LEN,
                               pattern=[[P, NT], [-UNIT, NC_P]], channel_multiplier=1).then_inc(masks_ready, 1)
            pool.affine_select(out=any_cmp[:], in_=ones[:, 0:1], compare_op=ALU.is_ge, fill=0.0, base=1 - CMP_LEN,
                               pattern=[[0, 1]], channel_multiplier=1).then_inc(masks_ready, 1)
            pool.affine_select(out=later[:, PAST - P:PAST], in_=later[:, PAST - P:PAST], compare_op=ALU.is_gt, fill=0.0,
                               base=0, pattern=[[-1, P]], channel_multiplier=1).then_inc(masks_ready, 1)
            pool.affine_select(out=same[:], in_=same[:], compare_op=ALU.is_ge, fill=0.0, base=0,
                               pattern=[[-TN, NB], [-1, TN]], channel_multiplier=1).then_inc(masks_ready, 1)
            for g in range(2):
                base = -4 * TN * g
                pool.affine_select(out=spread[:, g, :], in_=spread[:, g, :], compare_op=ALU.not_equal, fill=1.0,
                                   base=base, pattern=[[-TN, 4], [0, H], [-1, TN]], channel_multiplier=1
                                   ).then_inc(masks_ready, 1)
                pool.affine_select(out=lf_new[:, g, :], in_=lf_new[:, g, :], compare_op=ALU.is_ge, fill=0.0,
                                   base=base, pattern=[[-TN, 4], [0, H], [0, TN]], channel_multiplier=1
                                   ).then_inc(masks_ready, 1)
            pool.wait_ge(masks_ready, 8)
            pool.affine_select(out=same[:], in_=same[:], compare_op=ALU.is_ge, fill=0.0, base=TN - 1,
                               pattern=[[TN, NB], [0, TN]], channel_multiplier=-1).then_inc(masks_ready, 1)
            for g in range(2):
                pool.affine_select(out=lf_new[:, g, :], in_=lf_new[:, g, :], compare_op=ALU.is_ge, fill=0.0,
                                   base=4 * TN * g, pattern=[[TN, 4], [0, H], [1, TN]], channel_multiplier=-1
                                   ).then_inc(masks_ready, 1)
            pool.iota(rank16_i[:], pattern=[[-1, NE]], base=NE, channel_multiplier=0).then_inc(masks_ready, 1)
            pool.wait_ge(ws_copied, 1)
            pool.affine_select(out=ws_T[:], in_=ws_T[:], compare_op=ALU.is_ge, fill=0.0, base=0,
                               pattern=[[0, H], [1, P]], channel_multiplier=-1).then_inc(ws_masked, 1)
            pool.memset(ws_s[:], 0.0).then_inc(pool_step, 1)
            pool.wait_ge(pool_step, 10)
            pool.wait_ge(ws_masked, 1)
            for b in range(NB):
                pool.dma_start(ws_s[TN * b:TN * b + TN, :, TN * b:TN * b + TN], ws_T[0:TN, :, 0:TN]
                               ).then_inc(ws_s_ready, 16)

        @block.scalar
        def _(act):
            act.dma_start(ws_rows, gmlp_w_s[0].rearrange("h t s -> t h s")).then_inc(ws_loaded, 16)
            act.dma_start(bs[:, 0, :], gmlp_b_s[0].rearrange("h t -> t h"),
                          allow_slow_non_contiguous=True).then_inc(small_loaded, 16)
            for b in range(NB):
                act.dma_start(bs[TN * b:TN * b + TN, 1, :], gmlp_b_s[0, :, 0:TN].rearrange("h t -> t h"),
                              allow_slow_non_contiguous=True).then_inc(small_loaded, 16)
            act.dma_start(bias_f[:], fox_b_f[0].partition_broadcast(P)).then_inc(small_loaded, 16)
            for f in range(2):
                act.dma_start(cw[:, f, :], conv_w[0, :, f * P:(f + 1) * P].rearrange("j p -> p j"),
                              allow_slow_non_contiguous=True).then_inc(small_loaded, 16)
            for f in range(2):
                for b in range(NB):
                    act.dma_start(z_s[:, f, b, 0:2], state_conv[0, b, :, f * P:(f + 1) * P].rearrange("j p -> p j"),
                                  allow_slow_non_contiguous=True).then_inc(small_loaded, 16)
            for t in range(TILES):
                act.wait_ge(proj_done, t + 1)
                n = rows_of[t]
                nc.scalar.activation(uv[0:n, t, :], psum[t % 4][0:n, :], ACT.Gelu_apprx_tanh).then_inc(proj_copied, 1)
            act.wait_ge(var_ready, TILES + 1)
            nc.scalar.activation(ln_stat[:, :, :, 1], ln_stat[:, :, :, 1], ACT.Ln, bias=lnc[:, 0:1]).then_inc(lnv_ready, 1)
            act.wait_ge(lnv_ready, 1)
            nc.scalar.activation(ln_stat[:, :, :, 1], ln_stat[:, :, :, 1], ACT.Exp, scale=-0.5).then_inc(rstd_ready, 1)
            j = TILES
            for g in range(1, NRG):
                for t in range(TILES):
                    n, w = rows_of[t], GROUPS[g][1]
                    act.wait_ge(proj_done, j + 1)
                    if g == 1 and t >= 2:
                        act.wait_ge(turned, TILES + t - 1)
                        act.wait_ge(k_stored[t % 2], 16 * (t // 2))
                    if g == 1 and t < 2:
                        act.wait_ge(ws_turned, 1)
                    if g == 3:
                        act.wait_ge(turned, 2 * TILES + max(t - 1, 0))
                        if t < 2:
                            act.wait_ge(k_stored[t % 2], 16 * ((TILES + 1 - t) // 2))
                    ps = psum[j % 4]
                    if g == 1:
                        out = qk_rows[0:n, t % 2, :]
                    elif g == 2:
                        out = fox_v[0:n, t, :]
                    elif g == 3:
                        out = qk_rows[0:n, t % 2, 0:GW]
                    else:
                        out = nsa_rows[0:n, t, :]
                    w = out.shape[-1]
                    ins = nc.scalar.copy(out, ps[0:n, 0:w])
                    if g == 2:
                        nc.scalar.copy(b_f[0:n, :, t], ps[0:n, GW:GW + H]).then_inc(proj_copied, 1)
                    else:
                        ins.then_inc(proj_copied, 1)
                    j += 1
                    if (g, t) == (3, 0):
                        act.wait_ge(x_biased, 1)
                        nc.scalar.activation(lf_e[:], lf_x[:], ACT.Abs).then_inc(lf_parts, 1)
                        act.wait_ge(lf_parts, 1)
                        nc.scalar.activation(lf_e[:], lf_e[:], ACT.Exp, scale=-1.0).then_inc(lf_parts, 1)
                        act.wait_ge(lf_parts, 2)
                        nc.scalar.activation(lf_e[:], lf_e[:], ACT.Ln, bias=lnc[:, 1:2]).then_inc(lf_parts, 1)
            act.wait_ge(proj_copied, N_ROWJ)
            nc.scalar.activation(gates[:].rearrange("p t b h -> p t (b h)"), nsa_rows[:, :, 6 * DH:6 * DH + 12],
                                 ACT.Exp, scale=-1.0).then_inc(gate_x, 1)
            for f in range(2):
                if f:
                    act.wait_ge(z_used, 3)
                for c, (c0, cn) in enumerate(CHUNKS):
                    act.wait_ge(proj_done, N_ROWJ + 9 * f + c + 1)
                    nc.scalar.copy(dh_T[c], psum[(N_ROWJ + 9 * f + c) % 4][:, 0:cn]).then_inc(proj_copied, 1)

            def exp_scores(i):
                n = keys_of(i)[1]
                act.wait_ge(max_ready, i + 1)
                if i >= 2:
                    act.wait_ge(p_turned, i - 1)
                if i >= 4:
                    act.wait_ge(y_done, i - 3)
                nc.scalar.activation(P_buf[:, i % 2, 0:n * P], banks(2 * (i % 2), 2)[:, 0:n * P], ACT.Exp,
                                     bias=neg_max[:, i % 4:i % 4 + 1],
                                     accum_out=row_sum[:, i % 4:i % 4 + 1]).then_inc(p_ready, 1)

            def copy_pt_act(i):
                n = keys_of(i)[1]
                if n > 4:
                    act.wait_ge(p_turned, i + 1)
                    if i >= 2:
                        act.wait_ge(o_ready, i - 1)
                    nc.scalar.copy(PT_buf[:, i % 2, 512:n * P], psum[5][:, 0:(n - 4) * P]).then_inc(pt_act, 1)

            for i in range(J + 1):
                if i < J:
                    exp_scores(i)
                if i >= 1:
                    copy_pt_act(i - 1)

            for q in range(1, 2 + NB, 2):
                act.wait_ge(cc_turned, q + 1)
                copy_units(nc.scalar.copy, q).then_inc(cc_act, 1)
            act.wait_ge(comp_done, 2)
            act.wait_ge(conv_stored, 16 * 2 * (1 + NB))
            for c in range(2):
                ins = nc.scalar.copy(hid_bias[:, c:c + 1], psum[c][:, NU:NU + 1])
            ins.then_inc(act_step, 1)
            act.wait_ge(act_step, 1)
            for c in range(2):
                nc.scalar.activation(hid[:, c, 0:NCB], psum[c][:, 0:NCB], ACT.Gelu_apprx_tanh,
                                     bias=hid_bias[:, c:c + 1]).then_inc(hid_ready, 1)
            act.wait_ge(cmp_proj, 1)
            nc.scalar.copy(cmpT_k[:, 0:NCB], psum[2][0:DH, 0:NCB])
            nc.scalar.copy(cmp_v_p[0:NC_P, :], psum[3][0:NC_P, 0:DH])
            nc.scalar.copy(cmp_v_s[0:NC_S], psum[4][0:NC_S, 0:NB * DH].rearrange("p (b d) -> p b d", b=NB)
                           ).then_inc(cmp_kv, 1)
            for qt in range(NT + 1):
                if qt < NT:
                    act.wait_ge(c_shifted, qt + 1)
                    v = P_buf[:, qt % 2, 0:H * NC_P]
                    nc.scalar.activation(v, v, ACT.Exp).then_inc(c_exp, 1)
                if qt >= 1:
                    act.wait_ge(c_turned, qt)
                    if qt >= 3:
                        act.wait_ge(c_out, qt - 2)
                    nc.scalar.copy(PT_buf[0:NC_P, (qt - 1) % 2, 0:512], psum[4 + (qt - 1) % 2][0:NC_P, :]
                                   ).then_inc(c_pt, 1)
            k = 0
            for u, (br, g) in enumerate(sjobs):
                while k < len(units) and units[k][0] == u:
                    if k % 2:
                        copy_keys(act, nc.scalar.copy, k).then_inc(kt_act, 1)
                    k += 1
                act.wait_ge(smax_ready, u + 1)
                if u >= 2:
                    act.wait_ge(sp_turned, u - 1)
                    act.wait_ge(so_done, u - 1)
                w = NC_S if br == "cmp" else SW
                nc.scalar.activation(Ps[:, u % 2, 0:w], banks(2 * (u % 2), 2)[:, 0:w], ACT.Exp,
                                     bias=s_stat[:, u % 2, 0:1], accum_out=s_stat[:, u % 2, 1:2]).then_inc(sp_ready, 1)
            steps = [1]

            def link(ins):
                steps[0] += 1
                ins.then_inc(act_step, 1)
                act.wait_ge(act_step, steps[0])

            def copy_mix(t):
                n = rows_of[t]
                act.wait_ge(mix_turned, t + 1)
                if t >= 2:
                    act.wait_ge(r_done, t - 1)
                nc.scalar.copy(mix_T[:, t % 2, 4:6, 0:n], psum[5][:, 0:2 * P].rearrange("p (k n) -> p k n", k=2)[:, :, 0:n]
                               ).then_inc(mix_act, 1)

            def rstd(i, t):
                n, m = rows_of[t], TILES * i + t
                st = ln_s[0:n, m % 2, :]
                act.wait_ge(mean_ready, m + 1)
                link(nc.scalar.activation(banks(2 * (m % 2), 2)[0:n, :], layer[0:n, t, :], ACT.Square, bias=st[:, 1:2],
                                          accum_out=st[:, 2:3]))
                link(nc.scalar.activation(st[:, 3:4], st[:, 2:3], ACT.Ln, bias=lnc[0:n, 0:1], scale=1.0 / D))
                nc.scalar.activation(st[:, 3:4], st[:, 3:4], ACT.Exp, scale=-0.5).then_inc(rstd2_ready, 1)

            def after_turn(t):
                n = rows_of[t]
                act.wait_ge(x1_turned, t + 1)
                nc.scalar.copy(x1T[:, 0:4, tok0(t):tok0(t) + n],
                               psum[6][:].rearrange("p (k n) -> p k n", k=4)[:, :, 0:n]).then_inc(x1T_act, 1)
                nc.scalar.mul(layer[0:n, t, :], layer[0:n, t, :], ALPHA).then_inc(scaled, 1)

            act.wait_ge(ys_ready, 1)
            for t in range(TILES + 1):
                if t < TILES:
                    copy_mix(t)
                    rstd(0, t)
                if t >= 1:
                    after_turn(t - 1)
            act.wait_ge(rmax_ready, 1)
            pv = probs[:].rearrange("p t e -> p (t e)")
            nc.scalar.activation(pv, pv, ACT.Exp).then_inc(rexp_ready, 1)
            for e in range(NE):
                for c, (t0, tn) in enumerate(CH):
                    n = min(tn * P, TOK - t0 * P)
                    for f in range(2):
                        m = 2 * (3 * e + c) + f
                        act.wait_ge(gu_done, m + 1)
                        if m >= 2:
                            act.wait_ge(h_ready, m - 1)
                        nc.scalar.activation(sil[:, f, 0:n], psum[f][:, 0:n], ACT.Silu).then_inc(sil_ready, 1)
            for t in range(TILES):
                rstd(1, t)

        @block.tensor
        def _(pe):
            def turn_x(t):
                n = rows_of[t]
                pe.wait_ge(x_loaded[t % 2], 16 * (t // 2 + 1))
                if t >= 2:
                    pe.wait_ge(turn_copied, t - 1)
                for k in range(KD):
                    ins = nc.tensor.transpose(psum[4 + 2 * (t % 2) + k // 4][:, (k % 4) * P:(k % 4) * P + n],
                                              x_rows[0:n, t % 2, k * P:(k + 1) * P], ident[0:n, 0:n])
                ins.then_inc(turned, 1)

            def project_rows(g, t):
                j = g * TILES + t
                n, w = rows_of[t], GROUPS[g][1]
                if t == 0:
                    pe.wait_ge(w_loaded[g % 2], w_count(g))
                if g == 0:
                    pe.wait_ge(turn_copied, t + 1)
                if j >= 4:
                    pe.wait_ge(proj_copied, j - 3)
                wv = w_view(g)
                for k in range(KD):
                    ins = nc.tensor.matmul(psum[j % 4][0:n, 0:w], xT[:, k, tok0(t):tok0(t) + n], wv[:, k, 0:w],
                                           start=(k == 0), stop=(k == KD - 1))
                ins.then_inc(proj_done, 1)

            def turn_rows(g, t):
                e = {1: 1, 3: 2, 4: 3}[g] * TILES + t
                n = rows_of[t]
                pe.wait_ge(proj_copied, g * TILES + t + 1)
                pe.wait_ge(turn_copied, e - 1)
                if e == 2 * TILES:
                    pe.wait_ge(zg_used, TILES)
                A, B = psum[4 + 2 * (e % 2)], psum[5 + 2 * (e % 2)]
                I = ident[0:n, 0:n]
                if g == 1 and t < NT:
                    for h in range(H):
                        for bank, c in ((A, 0), (B, GW)):
                            ins = nc.tensor.transpose(bank[0:DH, h * P:(h + 1) * P],
                                                      qk_rows[:, t % 2, c + h * DH:c + (h + 1) * DH], I)
                elif g == 1:
                    for pair in range(2):
                        for bank, c in ((A, 0), (B, GW)):
                            ins = nc.tensor.transpose(bank[:, pair * P:pair * P + n],
                                                      qk_rows[0:n, t % 2, c + pair * P:c + (pair + 1) * P], I)
                elif g == 3:
                    for h in range(H):
                        ins = nc.tensor.transpose(A[0:DH, h * P:h * P + n],
                                                  qk_rows[0:n, t % 2, h * DH:(h + 1) * DH], I)
                else:
                    for i, c in enumerate((2, 4)):
                        ins = nc.tensor.transpose(A[0:DH, i * P:i * P + n], nsa_rows[0:n, t, c * DH:(c + 1) * DH], I)
                ins.then_inc(turned, 1)

            pe.wait_ge(consts_ready, 5)
            for t in range(TILES):
                turn_x(t)
                if t >= 1:
                    project_rows(0, t - 1)
            pe.wait_ge(ws_loaded, 16)
            pe.wait_ge(turn_copied, TILES)
            for h in range(H):
                ins = nc.tensor.transpose(psum[6][:, h * P:(h + 1) * P], ws_rows[:, h, :], ident[:])
            ins.then_inc(ws_turned, 1)
            project_rows(0, TILES - 1)
            pe.wait_ge(ws_copied, 1)
            for g in range(1, NRG):
                for t in range(TILES):
                    project_rows(g, t)
                    if g != 2 and t >= 1:
                        turn_rows(g, t - 1)
                    if g == 2:
                        gate_rows(pe, t)
                    if g in (2, 4) and t == 0:
                        turn_rows(g - 1, TILES - 1)
                    if (g, t) == (3, TILES - 1):
                        pe.wait_ge(lf_ready, 1)
                        lfp = lf[:, :, 0:NT]
                        nc.tensor.matmul(psum[5][:, 0:H * NT], tri_u[:], lfp, start=True, stop=True)
                        nc.tensor.matmul(psum[5][:, 64:64 + H * NT], ones[:], lfp, start=True, stop=True
                                         ).then_inc(cum_done, 1)
                    if (g, t) == (4, 1):
                        pe.wait_ge(c_ready, 1)
                        nc.tensor.transpose(psum[7][0:H * NT, 0:P], cum[:].rearrange("p h t -> p (h t)"), ident[:]
                                            ).then_inc(cT_done, 1)
            for f in range(2):
                g = NRG + f
                pe.wait_ge(w_loaded[g % 2], w_count(g))
                wv = w_view(g)
                for part in range(3):
                    for c, (c0, cn) in enumerate(CHUNKS):
                        j = N_ROWJ + 9 * f + 3 * part + c
                        bank_free(pe, j)
                        for k in range(KD):
                            ins = nc.tensor.matmul(psum[j % 4][:, 0:cn], wv[:, k, part * P:(part + 1) * P],
                                                   xT[:, k, c0:c0 + cn], start=(k == 0), stop=(k == KD - 1))
                        ins.then_inc(proj_done, 1)
                    if f == 0 and part == 0:
                        turn_rows(4, TILES - 1)

            def scores(i):
                br, qt, h = jobs[i]
                k0, n = keys_of(i)
                if i >= 2:
                    pe.wait_ge(p_ready, i - 1)
                elif i == 0:
                    pe.wait_ge(z_used, 12)
                    pe.wait_ge(turn_copied, 4 * TILES)
                    pe.wait_ge(c_rows, 32)
                q = (foxT_q if br == "fox" else nsaT_q)[:, h, qt * P:(qt + 1) * P]
                kT = foxT_k[:, h, :] if br == "fox" else selT_k if br == "sel" else winT_k
                S = banks(2 * (i % 2), 2)
                for c0 in range(0, n * P, 512):
                    cn = min(512, n * P - c0)
                    masks = []
                    if c0 + cn == n * P:
                        masks.append((n * P - P, causal_m))
                    if br == "win" and qt >= win_tiles and c0 == 0:
                        masks.append((0, far_m))
                    ins = nc.tensor.matmul(S[:, c0:c0 + cn], q, kT[:, k0 * P + c0:k0 * P + c0 + cn],
                                           start=True, stop=not masks, skip_group_check=True)
                    for k, (m0, m) in enumerate(masks):
                        ins = nc.tensor.matmul(S[:, m0:m0 + P], ident_bf[:], m[:], start=False,
                                               stop=(k == len(masks) - 1), skip_group_check=True)
                ins.then_inc(s_ready, 1)

            def turn_p(i):
                n = keys_of(i)[1]
                pe.wait_ge(p_ready, i + 1)
                if i >= 1:
                    pe.wait_ge(pt_dve, i)
                    if wide_jobs(i - 1):
                        pe.wait_ge(pt_act, wide_jobs(i - 1))
                for k in range(n):
                    ins = nc.tensor.transpose(psum[4 + k // 4][:, (k % 4) * P:(k % 4 + 1) * P],
                                              P_buf[:, i % 2, k * P:(k + 1) * P], ident[:])
                ins.then_inc(p_turned, 1)

            def p_times_v(i):
                br, qt, h = jobs[i]
                k0, n = keys_of(i)
                pe.wait_ge(pt_dve, i + 1)
                if wide_jobs(i):
                    pe.wait_ge(pt_act, wide_jobs(i))
                if i >= 2:
                    pe.wait_ge(y_done, i - 1)
                for k in range(n):
                    if br == "fox":
                        v = fox_v[:, k0 + k, h * DH:(h + 1) * DH]
                    else:
                        c = 3 if br == "sel" else 5
                        v = nsa_rows[:, k0 + k, c * DH:(c + 1) * DH]
                    ins = nc.tensor.matmul(psum[6 + i % 2][:, 0:DH], PT_buf[:, i % 2, k * P:(k + 1) * P], v,
                                           start=(k == 0), stop=(k == n - 1))
                ins.then_inc(o_ready, 1)

            for i in range(J + 2):
                if i < J:
                    scores(i)
                if 1 <= i <= J:
                    turn_p(i - 1)
                if i >= 2:
                    p_times_v(i - 2)

            pe.wait_ge(pt_dve, J)
            pe.wait_ge(pt_act, wide_jobs(J - 1))
            pe.wait_ge(y_done, J)
            pe.wait_ge(cmp_w_in, 16 * 6)
            nc.tensor.transpose(psum[6][:, 0:CMP_LEN], pe_rows[:], ident[0:CMP_LEN, 0:CMP_LEN]).then_inc(pe_turned, 1)
            for q in range(2 + NB):
                if q >= 2:
                    pe.wait_ge(cc_act if q % 2 else cc_dve, q // 2)
                if q == 2:
                    pe.wait_ge(nsa_cache_in, 16 * NB * NPG)
                for k in range(4):
                    src = nsa_rows[:, 4 * q + k, 0:2 * DH] if q < 2 else nsa_cache[:, (q - 2) * NPG + k, 0:2 * DH]
                    ins = nc.tensor.transpose(psum[4 + q % 2][:, k * P:(k + 1) * P], src, ident[:])
                ins.then_inc(cc_turned, 1)
            pe.wait_ge(pe_copied, 1)
            pe.wait_ge(cc_dve, 1 + NB // 2)
            pe.wait_ge(cc_act, 1 + NB // 2)
            for c in range(2):
                half = slice(c * DH, (c + 1) * DH)
                for l in range(CMP_LEN):
                    u0, r = l // UNIT, l % UNIT
                    ins = nc.tensor.matmul(psum[c][:, 0:NU + 1], cmp_w1[half, l, :], kcvc_T[half, r, u0:u0 + NU + 1],
                                           start=(l == 0), stop=(l == CMP_LEN - 1))
                ins.then_inc(comp_done, 1)
            pe.wait_ge(hid_ready, 2)
            nc.tensor.matmul(psum[2][0:DH, 0:NCB], cmp_w2[:, 0, :], hid[:, 0, 0:NCB], start=True, stop=True)
            nc.tensor.matmul(psum[3][0:NC_P, 0:DH], hid[:, 1, 0:NC_P], cmp_w2[:, 1, :], start=True, stop=True)
            for b in range(NB):
                u0 = U_P + U_S * b
                ins = nc.tensor.matmul(psum[4][0:NC_S, b * DH:(b + 1) * DH], hid[:, 1, u0:u0 + NC_S], cmp_w2[:, 1, :],
                                       start=True, stop=True)
            ins.then_inc(cmp_proj, 1)

            def cmp_scores(qt):
                if qt == 0:
                    pe.wait_ge(cmp_kv, 1)
                    pe.wait_ge(masks_ready, 11)
                if qt >= 2:
                    pe.wait_ge(c_shifted, qt - 1)
                S = psum[2 + qt % 2]
                for h in range(H):
                    nc.tensor.matmul(S[:, h * NC_P:(h + 1) * NC_P], nsaT_q[:, h, qt * P:(qt + 1) * P],
                                     cmpT_k[:, 0:NC_P], start=True, stop=False, skip_group_check=True)
                    ins = nc.tensor.matmul(S[:, h * NC_P:(h + 1) * NC_P], ident_bf[:], cmp_m[:, qt, :],
                                           start=False, stop=True, skip_group_check=True)
                ins.then_inc(c_scored, 1)

            def cmp_turn(qt):
                pe.wait_ge(c_exp, qt + 1)
                if qt >= 2:
                    pe.wait_ge(c_pt, qt - 1)
                for h in range(H):
                    ins = nc.tensor.transpose(psum[4 + qt % 2][0:NC_P, h * P:(h + 1) * P],
                                              P_buf[:, qt % 2, h * NC_P:(h + 1) * NC_P], ident[:])
                ins.then_inc(c_turned, 1)

            def cmp_out(qt):
                pe.wait_ge(c_pt, qt + 1)
                if qt >= 2:
                    pe.wait_ge(c_added, qt - 1)
                for h in range(H):
                    ins = nc.tensor.matmul(psum[6 + qt % 2][:, h * DH:(h + 1) * DH],
                                           PT_buf[0:NC_P, qt % 2, h * P:(h + 1) * P], cmp_v_p[0:NC_P, :],
                                           start=True, stop=True)
                ins.then_inc(c_out, 1)

            for qt in range(NT + 2):
                if qt < NT:
                    cmp_scores(qt)
                if 1 <= qt <= NT:
                    cmp_turn(qt - 1)
                if qt >= 2:
                    cmp_out(qt - 2)

            pe.wait_ge(c_added, NT)
            for g in range(2):
                nc.tensor.transpose(psum[6][:, g * NS:(g + 1) * NS], spread[:, g, :], ident[0:NS, 0:NS])
                ins = nc.tensor.matmul(psum[7][:, 16 * g:16 * g + 12], spread[:, g, :],
                                       gates[0:NS, NT].rearrange("p b h -> p (b h)"), start=True, stop=True)
            ins.then_inc(s_ops, 1)

            def turn_keys(k):
                u, b, pr = units[k]
                br, g = sjobs[u]
                if k < 2:
                    pe.wait_ge(c_pt, NT)
                else:
                    pe.wait_ge(kt_act if k % 2 else kt_dve, k // 2)
                if b == 0 and pr == 0:
                    if br == "fox":
                        pe.wait_ge(fox_cache_in, 16 * 4 * NPG * (g + 1))
                    if br == "win":
                        pe.wait_ge(win_cache_in, 16 * NB)
                bs_ = 4 * g + b
                for n in range(NPG):
                    if br == "fox":
                        src, rows = fox_cache[:, b * NPG + n, pr * P:(pr + 1) * P], P
                    elif br == "sel":
                        src, rows = nsa_cache[:, bs_ * NPG + n, 2 * DH:3 * DH], DH
                    else:
                        src, rows = win_cache[:, bs_, n, 0:DH], DH
                    ins = nc.tensor.transpose(psum[4 + k % 2][0:rows, n * P:(n + 1) * P], src, ident[:])
                ins.then_inc(kt_turned, 1)

            def score_keys(k):
                u, b, pr = units[k]
                br, g = sjobs[u]
                S = psum[2 * (u % 2)][32 * b:32 * b + 32, :]
                pe.wait_ge(kt_act if k % 2 else kt_dve, k // 2 + 1)
                if br == "fox":
                    ins = nc.tensor.matmul(S, foxS_q[:, pr, 4 * g + b].rearrange("p h t -> p (h t)"), KTs[:, k % 4, :],
                                           start=False, stop=(pr == 1), skip_group_check=True, tile_position=(0, 32 * b))
                else:
                    ins = nc.tensor.matmul(S, nsaS_q[:, 4 * g + b].rearrange("p h t -> p (h t)"), KTs[0:DH, k % 4, :],
                                           start=True, stop=(br == "sel"), skip_group_check=True,
                                           tile_position=(0, 32 * b))
                ins.then_inc(kt_used, 1)

            def new_scores(u):
                br, g = sjobs[u]
                S, Sn = psum[2 * (u % 2)], psum[2 * (u % 2) + 1][:, 0:NS]
                if u >= 2:
                    pe.wait_ge(sp_ready, u - 1)
                rows = slice(4 * g, 4 * g + 4)
                if br == "fox":
                    for n in range(NPG - 1, -1, -1):
                        w = (n + 1) * P
                        nc.tensor.matmul(S[:, 0:w], lf_rep[:, g, n, :], later[:, PAST - w:PAST],
                                         start=(n == NPG - 1), stop=False, skip_group_check=True)
                    for c in range(0, PAST, P):
                        nc.tensor.matmul(S[:, c:c + P], lf_new[:, g, :], ones[0:NS, :],
                                         start=False, stop=False, skip_group_check=True)
                    nc.tensor.matmul(Sn, lf_new[:, g, :], later[0:NS, PAST - P:PAST - P + NS], start=True, stop=False,
                                     skip_group_check=True)
                    for pr in range(2):
                        nc.tensor.matmul(Sn, foxS_q[:, pr, rows].rearrange("p b h t -> p (b h t)"), foxS_k[:, pr, :],
                                         start=False, stop=False, skip_group_check=True)
                else:
                    kT = selT_k if br == "sel" else winT_k
                    nc.tensor.matmul(Sn, nsaS_q[:, rows].rearrange("p b h t -> p (b h t)"), kT[:, SEQ:SEQ + NS],
                                     start=True, stop=False, skip_group_check=True)

            def cmp_sample_scores(u):
                g = sjobs[u][1]
                if u >= 2:
                    pe.wait_ge(sp_ready, u - 1)
                for b in range(4):
                    u0 = U_P + U_S * (4 * g + b)
                    ins = nc.tensor.matmul(psum[2 * (u % 2)][32 * b:32 * b + 32, 0:NC_S],
                                           nsaS_q[:, 4 * g + b].rearrange("p h t -> p (h t)"),
                                           cmpT_k[:, u0:u0 + NC_S], start=True, stop=True, tile_position=(0, 32 * b))
                ins.then_inc(ss_ready, 1)

            def turn_sample_p(u):
                br = sjobs[u][0]
                pe.wait_ge(sp_ready, u + 1)
                if u >= 1:
                    pe.wait_ge(spt_ready, u)
                    pe.wait_ge(so_done, u)
                if u == 0:
                    pe.wait_ge(s_setup, 2)
                if br == "cmp":
                    ins = nc.tensor.transpose(psum[6][0:NC_S, 0:P], Ps[:, u % 2, 0:NC_S], ident[:])
                else:
                    for n in range(NPG):
                        nc.tensor.transpose(psum[6][:, n * P:(n + 1) * P], Ps[:, u % 2, n * P:(n + 1) * P], ident[:])
                    ins = nc.tensor.transpose(psum[7][0:NS, 0:P], Ps[:, u % 2, PAST:SW], ident[:])
                ins.then_inc(sp_turned, 1)

            def sample_p_times_v(u):
                br, g = sjobs[u]
                pe.wait_ge(spt_ready, u + 1)
                if u >= 1:
                    pe.wait_ge(so_done, u)
                w = GW if br == "fox" else DH
                O = psum[7][:, 256:256 + w]
                if br != "cmp":
                    v = fox_v[0:NS, NT, :] if br == "fox" else nsa_rows[0:NS, NT, (3 if br == "sel" else 5) * DH:][:, 0:DH]
                    nc.tensor.matmul(O, PTs[0:NS, NPG, :], v, start=True, stop=False, skip_group_check=True)
                for b in range(4):
                    Ob, bs_ = O[32 * b:32 * b + 32, :], 4 * g + b
                    if br == "cmp":
                        ins = nc.tensor.matmul(Ob, PTs[0:NC_S, 0, 32 * b:32 * b + 32], cmp_v_s[0:NC_S, bs_, :],
                                               start=True, stop=True, tile_position=(0, 32 * b))
                        continue
                    for n in range(NPG):
                        if br == "fox":
                            v = fox_cache[:, b * NPG + n, GW:2 * GW]
                        elif br == "sel":
                            v = nsa_cache[:, bs_ * NPG + n, 3 * DH:4 * DH]
                        else:
                            v = win_cache[:, bs_, n, DH:2 * DH]
                        ins = nc.tensor.matmul(Ob, PTs[:, n, 32 * b:32 * b + 32], v, start=False, stop=(n == NPG - 1),
                                               skip_group_check=True, tile_position=(0, 32 * b))
                ins.then_inc(so_ready, 1)

            k = 0
            for u, (br, g) in enumerate(sjobs):
                mine = [i for i, x in enumerate(units) if x[0] == u]
                if br == "cmp":
                    cmp_sample_scores(u)
                else:
                    if u == 0:
                        pe.wait_ge(s_setup, 2)
                    turn_keys(mine[0])
                    new_scores(u)
                    for i in mine:
                        if i + 1 in mine:
                            turn_keys(i + 1)
                        score_keys(i)
                    if br == "win":
                        nc.tensor.matmul(psum[2 * (u % 2)][:, 0:TN], spread_bf[:, g, :], left_m[:],
                                         start=False, stop=True, skip_group_check=True)
                    nc.tensor.matmul(psum[2 * (u % 2) + 1][:, 0:NS], spread_bf[:, g, :], new_m[:],
                                     start=False, stop=True, skip_group_check=True).then_inc(ss_ready, 1)
                if u >= 1:
                    turn_sample_p(u - 1)
                    sample_p_times_v(u - 1)
            turn_sample_p(len(sjobs) - 1)
            sample_p_times_v(len(sjobs) - 1)
            pe.wait_ge(om_ready, 2)
            pe.wait_ge(so_done, len(sjobs))
            for i in range(2):
                for g in range(2):
                    ins = nc.tensor.matmul(psum[i][0:NS, 0:GW], gather[:, g, :], o_m[:, 2 * i + g, :],
                                           start=(g == 0), stop=(g == 1))
            ins.then_inc(ys_ready, 1)

            def turn_mix(t):
                n = rows_of[t]
                if t == 0:
                    pe.wait_ge(kt_act, len(units) // 2)
                    pe.wait_ge(kt_dve, len(units) // 2)
                else:
                    pe.wait_ge(mix_dve, t)
                    pe.wait_ge(mix_act, t)
                if t == NT:
                    pe.wait_ge(ys_copied, 1)
                srcs = [uv[0:n, t, i * P:(i + 1) * P] for i in range(4)] + [fox_v[0:n, t, i * P:(i + 1) * P] for i in range(2)]
                for k, src in enumerate(srcs):
                    ins = nc.tensor.transpose(psum[4 + k // 4][:, (k % 4) * P:(k % 4) * P + n], src, ident[0:n, 0:n])
                ins.then_inc(mix_turned, 1)

            def mix_out(t):
                n = rows_of[t]
                if t == 0:
                    pe.wait_ge(wo_in, 16)
                    pe.wait_ge(ys_copied, 1)
                pe.wait_ge(mix_dve, t + 1)
                pe.wait_ge(mix_act, t + 1)
                if t >= 2:
                    pe.wait_ge(rstd2_ready, t - 1)
                for i in range(2):
                    for k in range(KD):
                        lhs = mix_T[:, t % 2, k, 0:n] if k < 6 else yd_T[:, k - 6, tok0(t):tok0(t) + n]
                        ins = nc.tensor.matmul(psum[2 * (t % 2) + i][0:n, :], lhs, wo[:, k, i * 512:(i + 1) * 512],
                                               start=(k == 0), stop=(k == KD - 1))
                ins.then_inc(r_done, 1)

            def turn_x1(t):
                n = rows_of[t]
                pe.wait_ge(normed, t + 1)
                if t:
                    pe.wait_ge(x1T_dve, t)
                    pe.wait_ge(x1T_act, t)
                for k in range(KD):
                    ins = nc.tensor.transpose(psum[6 + k // 4][:, (k % 4) * P:(k % 4) * P + n],
                                              layer[0:n, t, k * P:(k + 1) * P], ident[0:n, 0:n])
                ins.then_inc(x1_turned, 1)

            turn_mix(0)
            for t in range(TILES):
                if t + 1 < TILES:
                    turn_mix(t + 1)
                mix_out(t)
                if t >= 1:
                    turn_x1(t - 1)
            turn_x1(TILES - 1)
            pe.wait_ge(router_in, 16)
            pe.wait_ge(mix_dve, TILES)
            pe.wait_ge(x1T_dve, TILES)
            pe.wait_ge(x1T_act, TILES)
            for t in range(TILES):
                n = rows_of[t]
                for k in range(KD):
                    ins = nc.tensor.matmul(psum[4][0:n, t * NE:(t + 1) * NE], x1T[:, k, tok0(t):tok0(t) + n], w_r[:, k, :],
                                           start=(k == 0), stop=(k == KD - 1))
            ins.then_inc(logits_done, 1)

            def hidden(e, c):
                t0, tn = CH[c]
                n = min(tn * P, TOK - t0 * P)
                i = e % 2
                if c == 0:
                    pe.wait_ge(ew_in[i], 48 * (e // 2 + 1))
                if e == 0 and c == 0:
                    pe.wait_ge(rstd2_ready, TILES)
                for f in range(2):
                    m = 2 * (3 * e + c) + f
                    if m >= 2:
                        pe.wait_ge(h_ready, m - 1)
                    for bank, w in ((f, ew_g[i]), (2 + f, ew_u[i])):
                        for k in range(KD):
                            ins = nc.tensor.matmul(psum[bank][:, 0:n], w[:, k, f * P:(f + 1) * P],
                                                   x1T[:, k, t0 * P:t0 * P + n], start=(k == 0), stop=(k == KD - 1))
                    ins.then_inc(gu_done, 1)

            def down(e, c):
                t0, tn = CH[c]
                j = (3 * e + c) % 2
                pe.wait_ge(h_ready, 2 * (3 * e + c) + 2)
                for t in range(t0, t0 + tn):
                    y = TILES * e + t
                    n = rows_of[t]
                    if y >= 2:
                        pe.wait_ge(ye_added, y - 1)
                    elif y == 0:
                        pe.wait_ge(rmax_ready, 1)
                    for half in range(2):
                        for f in range(2):
                            ins = nc.tensor.matmul(psum[4 + 2 * (y % 2) + half][0:n, :],
                                                   h_T[:, j, f, (t - t0) * P:(t - t0) * P + n],
                                                   ew_d[e % 2][:, f, half * 512:(half + 1) * 512],
                                                   start=(f == 0), stop=(f == 1))
                    ins.then_inc(ye_done, 1)

            todo = [(e, c) for e in range(NE) for c in range(len(CH))]
            for i in range(len(todo) + 1):
                if i < len(todo):
                    hidden(*todo[i])
                if i:
                    down(*todo[i - 1])

        @block.vector
        def _(dve):
            steps = [0]

            def link(ins):
                steps[0] += 1
                ins.then_inc(dve_step, 1)
                dve.wait_ge(dve_step, steps[0])

            nc.vector.memset(lnc[:, 0:1], LN_EPS).then_inc(var_ready, 1)
            nc.vector.memset(lnc[:, 1:2], 1.0)
            nc.vector.memset(foxT_q[DH:DH + 2, :, :], 1.0)
            nc.vector.memset(foxT_k[DH:DH + 2, :, :], 1.0)
            nc.vector.memset(foxS_q[:], 0.0)
            nc.vector.memset(ln_stat[:], 1.0)
            nc.vector.memset(b_f[:], 0.0)
            nc.vector.memset(nsa_rows[NS:P, NT, :], 0.0)

            def center_v(t):
                n = rows_of[t]
                dve.wait_ge(proj_copied, t + 1)
                v = uv[0:n, t, GW:2 * GW].rearrange("p (h d) -> p h d", h=H)
                sq = ln_sq[0:n, :].rearrange("p (h d) -> p h d", h=H)
                m = ln_stat[0:n, t, :, 0]
                link(nc.vector.tensor_reduce(m, v, AX.X, ALU.add))
                link(nc.vector.tensor_scalar(m, m, 1.0 / DH, None, ALU.mult))
                link(nc.vector.tensor_tensor(v, v, m.unsqueeze(2).to_broadcast([n, H, DH]), ALU.subtract))
                link(nc.vector.tensor_tensor(sq, v, v, ALU.mult))
                link(nc.vector.tensor_reduce(ln_stat[0:n, t, :, 1], sq, AX.X, ALU.add))
                nc.vector.tensor_scalar(ln_stat[0:n, t, :, 1], ln_stat[0:n, t, :, 1], 1.0 / DH, None,
                                        ALU.mult).then_inc(var_ready, 1)

            def scale_v(t):
                n = rows_of[t]
                v = uv[0:n, t, GW:2 * GW].rearrange("p (h d) -> p h d", h=H)
                r = ln_stat[0:n, t, :, 1]
                nc.vector.tensor_tensor(v, v, r.unsqueeze(2).to_broadcast([n, H, DH]), ALU.mult).then_inc(v_ready, 1)

            def copy_x(t):
                n = rows_of[t]
                dve.wait_ge(turned, t + 1)
                for i in range(2):
                    ins = nc.vector.tensor_copy(
                        xT[:, 4 * i:4 * i + 4, tok0(t):tok0(t) + n],
                        psum[4 + 2 * (t % 2) + i][:].rearrange("p (k n) -> p k n", k=4)[:, :, 0:n])
                ins.then_inc(turn_copied, 1)

            def copy_turned(g, t):
                e = {1: 1, 3: 2, 4: 3}[g] * TILES + t
                A, B = psum[4 + 2 * (e % 2)], psum[5 + 2 * (e % 2)]
                dve.wait_ge(turned, e + 1)
                ts = slice(tok0(t), tok0(t) + rows_of[t])
                av = A[0:DH, :].rearrange("p (h n) -> p h n", h=H)
                if g == 1 and t < NT:
                    nc.vector.tensor_scalar(foxT_q[0:DH, :, ts], av, SCALE, None, ALU.mult)
                    ins = nc.vector.tensor_copy(foxT_k[0:DH, :, ts], B[0:DH, :].rearrange("p (h n) -> p h n", h=H))
                elif g == 1:
                    for pair in range(2):
                        for i in range(2):
                            q = slice(DH * i, DH * i + DH)
                            nc.vector.tensor_scalar(foxS_q[q, pair, :, 2 * pair + i, :],
                                                    A[q, pair * P:pair * P + NS].rearrange("p (b t) -> p b t", b=NB),
                                                    SCALE, None, ALU.mult)
                    ins = nc.vector.tensor_copy(foxS_k[:], B[:, 0:2 * P].rearrange("p (i n) -> p i n", i=2)[:, :, 0:NS])
                elif g == 3 and t < NT:
                    ins = nc.vector.tensor_scalar(nsaT_q[:, :, ts], av, SCALE, None, ALU.mult)
                elif g == 3:
                    ins = nc.vector.tensor_scalar(nsaS_q[:].rearrange("p b h t -> p h b t"),
                                                  av[:, :, 0:NS].rearrange("p h (b t) -> p h b t", b=NB),
                                                  SCALE, None, ALU.mult)
                else:
                    nc.vector.tensor_copy(selT_k[:, ts], A[0:DH, 0:rows_of[t]])
                    ins = nc.vector.tensor_copy(winT_k[:, ts], A[0:DH, P:P + rows_of[t]])
                ins.then_inc(turn_copied, 1)

            def gate_u(t):
                n = rows_of[t]
                i = 0 if t < NT else 1
                dve.wait_ge(zg_done, t + 1)
                if t:
                    dve.wait_ge(zg_used, t)
                z = psum[4 + t % 2][0:n, 0:GW].rearrange("p (h d) -> p h d", h=H)
                b = bs[0:n, i, :].unsqueeze(2).to_broadcast([n, H, DH])
                sq = ln_sq[0:n, :].rearrange("p (h d) -> p h d", h=H)
                link(nc.vector.tensor_tensor(sq, z, b, ALU.add))
                u = uv[0:n, t, 0:GW]
                nc.vector.tensor_tensor(u, u, ln_sq[0:n, :], ALU.mult).then_inc(zg_used, 1)

            for t in range(TILES):
                copy_x(t)
                if t >= 2:
                    center_v(t - 2)
            dve.wait_ge(ws_turned, 1)
            nc.vector.tensor_copy(ws_T[:], psum[6][:].rearrange("p (h n) -> p h n", h=H)).then_inc(ws_copied, 1)
            center_v(TILES - 2)
            center_v(TILES - 1)
            copy_turned(1, 0)
            dve.wait_ge(rstd_ready, 1)
            dve.wait_ge(small_loaded, 16 * (1 + NB + 1 + 2 + 2 * NB))
            for t in range(TILES):
                scale_v(t)
                if t + 1 < TILES:
                    copy_turned(1, t + 1)
            for t in range(TILES):
                gate_u(t)
            for t in range(TILES):
                if t == 1:
                    dve.wait_ge(proj_copied, 3 * TILES)
                    nc.vector.tensor_tensor(lf_x[:], b_f[:], bias_f[:].unsqueeze(2).to_broadcast([P, H, TILES]),
                                            ALU.add).then_inc(x_biased, 1)
                if t == 3:
                    dve.wait_ge(lf_parts, 3)
                    dve.wait_ge(x_biased, 1)
                    nc.vector.scalar_tensor_tensor(out=lf[:], in0=lf_x[:], scalar=0.0, in1=lf_e[:],
                                                   op0=ALU.min, op1=ALU.subtract).then_inc(lf_ready, 1)
                    dve.wait_ge(lf_ready, 1)
                    nc.vector.tensor_copy(lf_rows[:].rearrange("p t h -> p h t"), lf[:]).then_inc(lf_ready, 1)
                if t == TILES - 1:
                    link(nc.vector.memset(carry[:, :, 0], 0.0))
                    dve.wait_ge(cum_done, 1)
                    tot = psum[5][:, 64:64 + H * NT].rearrange("p (h t) -> p h t", h=H)
                    for i in range(1, NT):
                        link(nc.vector.tensor_tensor(carry[:, :, i], carry[:, :, i - 1], tot[:, :, i - 1], ALU.add))
                    nc.vector.tensor_tensor(cum[:], psum[5][:, 0:H * NT].rearrange("p (h t) -> p h t", h=H),
                                            carry[:], ALU.add).then_inc(c_ready, 1)
                copy_turned(3, t)
            for t in range(TILES):
                copy_turned(4, t)
                if t == 0:
                    dve.wait_ge(cT_done, 1)
                    nc.vector.tensor_copy(cum_T[:, 0, :], psum[7][0:H * NT, 0:P])
                    nc.vector.tensor_scalar(cum_T[:, 1, :], psum[7][0:H * NT, 0:P], -1.0, None,
                                            ALU.mult).then_inc(cT_copied, 1)
            gv = gates[:].rearrange("p t b h -> p (t b h)")
            dve.wait_ge(gate_x, 1)
            link(nc.vector.tensor_scalar(gv, gv, 1.0, None, ALU.add))
            nc.vector.reciprocal(gv, gv).then_inc(gates_ready, 1)
            dve.wait_ge(turned, 3 * TILES)
            dve.wait_ge(k_stored[0], 16 * ((TILES + 1) // 2))
            dve.wait_ge(k_stored[1], 16 * (TILES // 2))
            link(nc.vector.memset(z_p[:, :, 0:2], 0.0))
            for f in range(2):
                j0 = N_ROWJ + 9 * f
                for c, (c0, cn) in enumerate(CHUNKS):
                    dve.wait_ge(proj_copied, N_ROWJ + 3 * f + c + 1)
                    dve.wait_ge(proj_done, j0 + 4 + c)
                    src = psum[(j0 + 3 + c) % 4][:, 0:cn]
                    dh = dh_T[c]
                    if c0 < SEQ:
                        dst = z_p[:, f, 2 + c0:2 + c0 + cn]
                    else:
                        dst = z_s[:, f, :, 2:2 + TN]
                        src = src.rearrange("p (b t) -> p b t", b=NB)
                        dh = dh.rearrange("p (b t) -> p b t", b=NB)
                    ins = nc.vector.tensor_tensor(dst, src, dh, ALU.mult)
                    ins.then_inc(z_used, 1)
                dve.wait_ge(z_used, 6 * f + 3)
                for c, (c0, cn) in enumerate(CHUNKS):
                    dve.wait_ge(proj_done, j0 + 7 + c)
                    dve.wait_ge(z_used, 6 * f + 3 + c)
                    if c0 < SEQ:
                        sh = [z_p[:, f, c0 + i:c0 + i + cn] for i in range(3)]
                        y, out = conv_y[:, 0:cn], yd_T[:, f, c0:c0 + cn]
                        ps = psum[(j0 + 6 + c) % 4][:, 0:cn]
                    else:
                        sh = [z_s[:, f, :, i:i + TN] for i in range(3)]
                        y, out, ps = [a.rearrange("p (b t) -> p b t", b=NB) for a in (
                            conv_y[:, 0:cn], yd_T[:, f, c0:c0 + cn], psum[(j0 + 6 + c) % 4][:, 0:cn])]
                    link(nc.vector.tensor_scalar(y, sh[0], cw[:, f, 0:1], None, ALU.mult))
                    link(nc.vector.scalar_tensor_tensor(out=y, in0=sh[1], scalar=cw[:, f, 1:2], in1=y,
                                                        op0=ALU.mult, op1=ALU.add))
                    link(nc.vector.scalar_tensor_tensor(out=y, in0=sh[2], scalar=cw[:, f, 2:3], in1=y,
                                                        op0=ALU.mult, op1=ALU.add))
                    nc.vector.tensor_tensor(out, ps, y, ALU.mult).then_inc(z_used, 1)
                dve.wait_ge(z_used, 6 * f + 6)

            dve.wait_ge(gates_ready, 1)

            def row_max(i):
                n = keys_of(i)[1]
                dve.wait_ge(s_ready, i + 1)
                if i >= 4:
                    dve.wait_ge(p_ready, i - 3)
                nc.vector.tensor_reduce(neg_max[:, i % 4:i % 4 + 1], banks(2 * (i % 2), 2)[:, 0:n * P], AX.X,
                                        ALU.max, negate=True).then_inc(max_ready, 1)

            def copy_pt_dve(i):
                n = min(4, keys_of(i)[1])
                dve.wait_ge(p_turned, i + 1)
                if i >= 2:
                    dve.wait_ge(o_ready, i - 1)
                nc.vector.tensor_copy(PT_buf[:, i % 2, 0:n * P], psum[4][:, 0:n * P]).then_inc(pt_dve, 1)

            def finish(i):
                br, qt, h = jobs[i]
                dve.wait_ge(o_ready, i + 1)
                s = slice(i % 4, i % 4 + 1)
                link(nc.vector.reciprocal(recip[:, s], row_sum[:, s]))
                O = psum[6 + i % 2][:, 0:DH]
                if br == "fox":
                    ins = nc.vector.tensor_scalar(uv[:, qt, GW + h * DH:GW + (h + 1) * DH], O, recip[:, s], None, ALU.mult)
                else:
                    b = 1 if br == "sel" else 2
                    link(nc.vector.tensor_tensor(coef[:, s], recip[:, s], gates[:, qt, b, h:h + 1], ALU.mult))
                    y = fox_v[:, qt, h * DH:(h + 1) * DH]
                    if br == "sel":
                        ins = nc.vector.tensor_scalar(y, O, coef[:, s], None, ALU.mult)
                    else:
                        ins = nc.vector.scalar_tensor_tensor(out=y, in0=O, scalar=coef[:, s], in1=y,
                                                             op0=ALU.mult, op1=ALU.add)
                ins.then_inc(y_done, 1)

            for i in range(J + 2):
                if i < J:
                    row_max(i)
                if 1 <= i <= J:
                    copy_pt_dve(i - 1)
                if i >= 2:
                    finish(i - 2)

            dve.wait_ge(pe_turned, 1)
            nc.vector.tensor_copy(kcvc_T[:, :, NU:NU + 2], psum[6][:, 0:CMP_LEN].rearrange("p (o r) -> p r o", r=UNIT)
                                  ).then_inc(pe_copied, 1)
            for q in range(0, 2 + NB, 2):
                dve.wait_ge(cc_turned, q + 1)
                copy_units(nc.vector.tensor_copy, q).then_inc(cc_dve, 1)

            def by_head(v):
                return v.unsqueeze(2)

            def cmp_shift(qt):
                dve.wait_ge(c_scored, qt + 1)
                if qt >= 2:
                    dve.wait_ge(c_turned, qt - 1)
                S = psum[2 + qt % 2][:, 0:H * NC_P].rearrange("p (h n) -> p h n", h=H)
                m = head_v[:, 0, :]
                if qt:
                    dve.wait_ge(c_shifted, qt)
                link(nc.vector.tensor_reduce(m, S, AX.X, ALU.max, negate=True))
                nc.vector.tensor_tensor(P_buf[:, qt % 2, 0:H * NC_P].rearrange("p (h n) -> p h n", h=H), S,
                                        by_head(m).to_broadcast([P, H, NC_P]), ALU.add).then_inc(c_shifted, 1)

            def cmp_sum(qt):
                dve.wait_ge(c_exp, qt + 1)
                if qt >= 2:
                    dve.wait_ge(c_added, qt - 1)
                s, r = head_v[:, 1, :], head_v[:, 2 + qt % 2, :]
                link(nc.vector.tensor_reduce(s, P_buf[:, qt % 2, 0:H * NC_P].rearrange("p (h n) -> p h n", h=H), AX.X, ALU.add))
                link(nc.vector.reciprocal(s, s))
                link(nc.vector.tensor_tensor(r, s, gates[:, qt, 0, :], ALU.mult))
                if qt == 0:
                    link(nc.vector.tensor_scalar(r, r, any_cmp[:, 0:1], None, ALU.mult))

            def cmp_add(qt):
                dve.wait_ge(c_out, qt + 1)
                if qt:
                    dve.wait_ge(c_added, qt)
                t = P_buf[:, 0, 512:512 + GW]
                O = psum[6 + qt % 2][:, 0:GW].rearrange("p (h d) -> p h d", h=H)
                link(nc.vector.tensor_tensor(t.rearrange("p (h d) -> p h d", h=H), O,
                                             by_head(head_v[:, 2 + qt % 2, :]).to_broadcast([P, H, DH]), ALU.mult))
                nc.vector.tensor_tensor(fox_v[:, qt, :], fox_v[:, qt, :], t, ALU.add).then_inc(c_added, 1)

            dve.wait_ge(masks_ready, 11)
            for qt in range(NT + 2):
                if qt < NT:
                    cmp_shift(qt)
                if 1 <= qt <= NT:
                    cmp_sum(qt - 1)
                if qt >= 2:
                    cmp_add(qt - 2)

            nc.vector.tensor_scalar(new_m[:], same[:], -NEG, NEG, ALU.mult, ALU.add)
            link(nc.vector.tensor_reduce(left_f[:], same[:].rearrange("p (b t) -> p t b", b=NB), AX.X, ALU.add))
            nc.vector.tensor_scalar(left_m[:], left_f[:], NEG, None, ALU.mult)
            nc.vector.tensor_copy(spread_bf[:], spread[:])
            link(nc.vector.tensor_reduce(head_m[:], ident[:].rearrange("p (b h t) -> p h b t", b=4, h=H), AX.XY, ALU.add))
            dve.wait_ge(lf_ready, 2)
            for g in range(2):
                v = lf_new[:, g, :].rearrange("p (b h t) -> p b h t", b=4, h=H)
                for b in range(4):
                    nc.vector.tensor_tensor(v[:, b], v[:, b], lf[0:NS, :, NT:NT + 1].to_broadcast([NS, H, TN]), ALU.mult)
            dve.wait_ge(lf_past_in, 16 * NB * NPG)
            dve.wait_ge(conv_stored, 16 * 2 * (1 + NB))
            for g in range(2):
                for n in range(NPG):
                    for b in range(4):
                        nc.vector.tensor_copy(
                            lf_rep[:, g, n, 32 * b:32 * b + 32].rearrange("p (h t) -> p h t", h=H),
                            lf_past[:, (4 * g + b) * NPG + n, :].unsqueeze(2).to_broadcast([P, H, TN]))
            dve.wait_ge(s_ops, 1)
            link(nc.vector.tensor_copy(gather[:], psum[6][:, 0:2 * NS].rearrange("p (g n) -> p g n", g=2)))
            for g in range(2):
                link(nc.vector.tensor_tensor(gate_t[:], psum[7][:, 16 * g:16 * g + 12].rearrange("p (b h) -> p b h", b=3),
                                             head_m[:].unsqueeze(1).to_broadcast([P, 3, H]), ALU.mult))
                nc.vector.tensor_reduce(gate_s[:, g, :], gate_t[:], AX.X, ALU.add).then_inc(s_setup, 1)
                dve.wait_ge(s_setup, g + 1)

            def sample_finish(u):
                br, g = sjobs[u]
                dve.wait_ge(so_ready, u + 1)
                st = s_stat[:, u % 2, :]
                link(nc.vector.reciprocal(st[:, 2:3], st[:, 1:2]))
                if br == "fox":
                    c = o_coef[:, g, :]
                    link(nc.vector.tensor_scalar(c, head_m[:], st[:, 2:3], None, ALU.mult))
                    nc.vector.tensor_tensor(o_m[:, g, :].rearrange("p (h d) -> p h d", h=H),
                                            psum[7][:, 256:512].rearrange("p (h d) -> p h d", h=H),
                                            c.unsqueeze(2).to_broadcast([P, H, DH]), ALU.mult).then_inc(so_done, 1)
                    return
                i = {"cmp": 0, "sel": 1, "win": 2}[br]
                link(nc.vector.tensor_tensor(st[:, 3:4], st[:, 2:3], gate_s[:, g, i:i + 1], ALU.mult))
                O, y = psum[7][:, 256:256 + DH], o_nsa[:, g, :]
                if br == "sel":
                    nc.vector.tensor_scalar(y, O, st[:, 3:4], None, ALU.mult).then_inc(so_done, 1)
                else:
                    nc.vector.scalar_tensor_tensor(out=y, in0=O, scalar=st[:, 3:4], in1=y, op0=ALU.mult, op1=ALU.add
                                                   ).then_inc(so_done, 1)
                dve.wait_ge(so_done, u + 1)
                if br == "cmp":
                    nc.vector.tensor_tensor(o_m[:, 2 + g, :].rearrange("p (h d) -> p h d", h=H),
                                            y.unsqueeze(1).to_broadcast([P, H, DH]),
                                            head_m[:].unsqueeze(2).to_broadcast([P, H, DH]), ALU.mult
                                            ).then_inc(om_ready, 1)

            def copy_sample_pt(u):
                dve.wait_ge(sp_turned, u + 1)
                if u >= 1:
                    dve.wait_ge(so_ready, u)
                if sjobs[u][0] == "cmp":
                    nc.vector.tensor_copy(PTs[0:NC_S, 0, :], psum[6][0:NC_S, 0:P]).then_inc(spt_ready, 1)
                else:
                    nc.vector.tensor_copy(PTs[:, 0:NPG, :], psum[6][:].rearrange("p (n k) -> p n k", n=NPG))
                    nc.vector.tensor_copy(PTs[0:NS, NPG, :], psum[7][0:NS, 0:P]).then_inc(spt_ready, 1)

            k = 0
            for u, (br, g) in enumerate(sjobs):
                while k < len(units) and units[k][0] == u:
                    if k % 2 == 0:
                        copy_keys(dve, nc.vector.tensor_copy, k).then_inc(kt_dve, 1)
                    k += 1
                dve.wait_ge(ss_ready, u + 1)
                if u >= 2:
                    dve.wait_ge(sp_ready, u - 1)
                w = NC_S if br == "cmp" else SW
                nc.vector.tensor_reduce(s_stat[:, u % 2, 0:1], banks(2 * (u % 2), 2)[:, 0:w], AX.X, ALU.max, negate=True
                                        ).then_inc(smax_ready, 1)
                if u >= 1:
                    copy_sample_pt(u - 1)
                    sample_finish(u - 1)
            copy_sample_pt(len(sjobs) - 1)
            sample_finish(len(sjobs) - 1)
            dve.wait_ge(ys_ready, 1)
            nc.vector.tensor_copy(uv[0:NS, NT, GW:2 * GW], psum[0][0:NS, 0:GW])
            nc.vector.tensor_copy(fox_v[0:NS, NT, :], psum[1][0:NS, 0:GW]).then_inc(ys_copied, 1)

            def add_residual(t):
                n = rows_of[t]
                dve.wait_ge(r_done, t + 1)
                dve.wait_ge(x_res_in[t % 2], 16 * (t // 2 + 1))
                st = ln_s[0:n, t % 2, :]
                if t >= 2:
                    dve.wait_ge(normed, t - 1)
                link(nc.vector.scalar_tensor_tensor(out=layer[0:n, t, :], in0=x_res[0:n, t % 2, :], scalar=ALPHA,
                                                    in1=banks(2 * (t % 2), 2)[0:n, :], op0=ALU.mult, op1=ALU.add,
                                                    accum_out=st[:, 0:1]))
                nc.vector.tensor_scalar(st[:, 1:2], st[:, 0:1], -1.0 / D, None, ALU.mult).then_inc(mean_ready, 1)

            def norm(i, t):
                n, m = rows_of[t], TILES * i + t
                st, v = ln_s[0:n, m % 2, :], layer[0:n, t, :]
                dve.wait_ge(rstd2_ready, m + 1)
                if t == 0:
                    dve.wait_ge(ln_in, 32 * (i + 1))
                link(nc.vector.scalar_tensor_tensor(out=v, in0=v, scalar=st[:, 1:2], in1=ln_row[i][0:n, 0, :],
                                                    op0=ALU.add, op1=ALU.mult))
                nc.vector.scalar_tensor_tensor(out=v, in0=v, scalar=st[:, 3:4], in1=ln_row[i][0:n, 1, :],
                                               op0=ALU.mult, op1=ALU.add).then_inc(normed, 1)

            def copy_mix(t):
                n = rows_of[t]
                dve.wait_ge(mix_turned, t + 1)
                if t >= 2:
                    dve.wait_ge(r_done, t - 1)
                nc.vector.tensor_copy(mix_T[:, t % 2, 0:4, 0:n], psum[4][:].rearrange("p (k n) -> p k n", k=4)[:, :, 0:n]
                                      ).then_inc(mix_dve, 1)

            def copy_x1T(t):
                n = rows_of[t]
                dve.wait_ge(x1_turned, t + 1)
                nc.vector.tensor_copy(x1T[:, 4:8, tok0(t):tok0(t) + n],
                                      psum[7][:].rearrange("p (k n) -> p k n", k=4)[:, :, 0:n]).then_inc(x1T_dve, 1)

            copy_mix(0)
            for t in range(TILES):
                if t + 1 < TILES:
                    copy_mix(t + 1)
                add_residual(t)
                norm(0, t)
                if t:
                    copy_x1T(t - 1)
            copy_x1T(TILES - 1)

            V = nc.vector
            full = [P, TILES, NE]
            t16 = lambda v: v.unsqueeze(2).to_broadcast(full)
            g44 = lambda v: v.rearrange("p t (g e) -> p (t g) e", g=EG)
            f4 = lambda v: v[:].rearrange("p t g -> p (t g)")
            in_group = lambda v: f4(v).unsqueeze(2).to_broadcast([P, TILES * EG, EG])
            dve.wait_ge(logits_done, 1)
            dve.wait_ge(masks_ready, 12)
            link(V.tensor_copy(rank16[:], rank16_i[:]))
            link(V.memset(probs[:], 0.0))
            link(V.tensor_copy(probs[:, 0:NT, :], psum[4][:, 0:NT * NE].rearrange("p (t e) -> p t e", t=NT)))
            link(V.tensor_copy(probs[0:NS, NT, :], psum[4][0:NS, NT * NE:TILES * NE]))
            link(V.tensor_reduce(r1[0][:], probs[:], AX.X, ALU.max, negate=True))
            V.tensor_tensor(probs[:], probs[:], t16(r1[0][:]), ALU.add).then_inc(rmax_ready, 1)
            dve.wait_ge(rexp_ready, 1)
            link(V.tensor_reduce(r1[0][:], probs[:], AX.X, ALU.add))
            link(V.reciprocal(r1[0][:], r1[0][:]))
            link(V.tensor_tensor(probs[:], probs[:], t16(r1[0][:]), ALU.mult))
            m1, cnt, m2, sel = r4
            link(V.tensor_reduce(f4(m1), g44(probs[:]), AX.X, ALU.max))
            link(V.tensor_tensor(g44(r16[0][:]), g44(probs[:]), in_group(m1), ALU.is_equal))
            link(V.tensor_reduce(f4(cnt), g44(r16[0][:]), AX.X, ALU.add))
            link(V.tensor_scalar(r16[1][:], r16[0][:], -2.0, None, ALU.mult))
            link(V.tensor_tensor(r16[1][:], r16[1][:], probs[:], ALU.add))
            link(V.tensor_reduce(f4(m2), g44(r16[1][:]), AX.X, ALU.max))
            link(V.tensor_scalar(cnt[:], cnt[:], 2.0, None, ALU.is_ge))
            link(V.tensor_tensor(cnt[:], cnt[:], m1[:], ALU.mult))
            link(V.tensor_tensor(m2[:], m2[:], cnt[:], ALU.max))
            link(V.tensor_tensor(m1[:], m1[:], m2[:], ALU.add))
            link(V.tensor_reduce(r1[0][:], m1[:], AX.X, ALU.max))
            t4 = lambda v: v.unsqueeze(2).to_broadcast([P, TILES, EG])
            rank4 = rank16[:, NE - EG:NE].unsqueeze(1).to_broadcast([P, TILES, EG])
            link(V.tensor_tensor(sel[:], m1[:], t4(r1[0][:]), ALU.is_equal))
            link(V.tensor_tensor(sel[:], sel[:], rank4, ALU.mult))
            link(V.tensor_reduce(r1[0][:], sel[:], AX.X, ALU.max))
            link(V.tensor_tensor(sel[:], sel[:], t4(r1[0][:]), ALU.is_equal))
            pm, hot = r16[0], r16[1]
            link(V.tensor_tensor(g44(pm[:]), g44(probs[:]), in_group(sel), ALU.mult))
            link(V.tensor_scalar(sel[:], sel[:], -1.0, None, ALU.add))
            link(V.tensor_tensor(g44(pm[:]), g44(pm[:]), in_group(sel), ALU.add))
            rank = rank16[:].unsqueeze(1).to_broadcast(full)
            for k in range(2):
                link(V.tensor_reduce(r1[k][:], pm[:], AX.X, ALU.max))
                link(V.tensor_tensor(hot[:], pm[:], t16(r1[k][:]), ALU.is_equal))
                link(V.tensor_tensor(hot[:], hot[:], rank, ALU.mult))
                link(V.tensor_reduce(r1[2][:], hot[:], AX.X, ALU.max))
                link(V.tensor_tensor(hot[:], hot[:], t16(r1[2][:]), ALU.is_equal))
                link(V.tensor_tensor((gate if k == 0 else r16[2])[:], hot[:], t16(r1[k][:]), ALU.mult))
                if k == 0:
                    link(V.tensor_scalar(hot[:], hot[:], -4.0, None, ALU.mult))
                    link(V.tensor_tensor(pm[:], pm[:], hot[:], ALU.add))
            link(V.tensor_tensor(gate[:], gate[:], r16[2][:], ALU.add))
            link(V.tensor_tensor(r1[0][:], r1[0][:], r1[1][:], ALU.add))
            link(V.reciprocal(r1[0][:], r1[0][:]))
            link(V.tensor_tensor(gate[:], gate[:], t16(r1[0][:]), ALU.mult))

            dve.wait_ge(scaled, TILES)

            def gated(e, c):
                t0, tn = CH[c]
                n = min(tn * P, TOK - t0 * P)
                j = (3 * e + c) % 2
                for f in range(2):
                    m = 2 * (3 * e + c) + f
                    dve.wait_ge(sil_ready, m + 1)
                    if m >= 4:
                        dve.wait_ge(ye_done, TILES * ((m // 2 - 2) // 3) + 3 * ((m // 2 - 2) % 3) + 3)
                    nc.vector.tensor_tensor(h_T[:, j, f, 0:n], psum[2 + f][:, 0:n], sil[:, f, 0:n], ALU.mult
                                            ).then_inc(h_ready, 1)

            def add_expert(e, c):
                t0, tn = CH[c]
                for t in range(t0, t0 + tn):
                    y, n = TILES * e + t, rows_of[t]
                    dve.wait_ge(ye_done, y + 1)
                    if y >= TILES:
                        dve.wait_ge(ye_added, y - TILES + 1)
                    v = layer[0:n, t, :]
                    nc.vector.scalar_tensor_tensor(out=v, in0=banks(4 + 2 * (y % 2), 2)[0:n, :],
                                                   scalar=gate[0:n, t, e:e + 1], in1=v,
                                                   op0=ALU.mult, op1=ALU.add).then_inc(ye_added, 1)

            todo = [(e, c) for e in range(NE) for c in range(len(CH))]
            for i in range(len(todo) + 1):
                if i < len(todo):
                    gated(*todo[i])
                if i:
                    add_expert(*todo[i - 1])
            dve.wait_ge(ye_added, NE * TILES)
            for t in range(TILES + 1):
                if t < TILES:
                    n, m = rows_of[t], TILES + t
                    st = ln_s[0:n, m % 2, :]
                    if t >= 2:
                        dve.wait_ge(normed, m - 1)
                    link(nc.vector.tensor_reduce(st[:, 0:1], layer[0:n, t, :], AX.X, ALU.add))
                    nc.vector.tensor_scalar(st[:, 1:2], st[:, 0:1], -1.0 / D, None, ALU.mult).then_inc(mean_ready, 1)
                if t >= 1:
                    norm(1, t - 1)


_INS = ['x_prompt', 'x_sample', 'cache_fox_kv', 'cache_fox_logf', 'cache_nsa_kv', 'state_nsa_win', 'state_conv',
        'page_table', 'w_in', 'fox_b_f', 'gmlp_w_s', 'gmlp_b_s', 'nsa_cmp_pe', 'nsa_cmp_w1', 'nsa_cmp_w2', 'conv_w',
        'w_out', 'ln_g', 'ln_b', 'w_router', 'w_exp_gate', 'w_exp_up', 'w_exp_down']

_OUTS = [(1, 1024, 1024), (8, 8, 1024), (1, 1, 1024, 2, 4, 64), (1, 8, 8, 2, 4, 64), (1, 1, 1024, 4), (1, 8, 8, 4),
         (1, 1, 1024, 4, 64), (1, 8, 8, 4, 64), (1, 1, 512, 2, 64), (1, 8, 512, 2, 64), (1, 1, 2, 256), (1, 8, 2, 256),
         (1, 8, 8, 4, 64)]


def kernel(**inputs):
    import numpy as np
    import concourse.bacc as bacc
    from concourse.bass_utils import run_bass_kernel_spmd as run

    nc = bacc.Bacc("TRN2", target_bir_lowering=False, num_devices=1)
    arrays, args = {}, []
    for name in _INS:
        a = np.ascontiguousarray(inputs[name])
        arrays[f"in_{name}"] = a
        args.append(nc.dram_tensor(f"in_{name}", a.shape, mybir.dt.from_np(a.dtype), kind="ExternalInput").ap())
    for i, shape in enumerate(_OUTS):
        args.append(nc.dram_tensor(f"out_{i}", shape, F32, kind="ExternalOutput").ap())
    build(nc, *args)
    r = run(nc, [arrays], core_ids=[0])
    return tuple(r.results[0][f"out_{i}"] for i in range(len(_OUTS)))
```

```python
from contextlib import ExitStack

import concourse.bass as bass
from concourse import mybir

ALU = mybir.AluOpType
ACT = mybir.ActivationFunctionType
F32 = mybir.dt.float32
BF16 = mybir.dt.bfloat16
I32 = mybir.dt.int32
AX = mybir.AxisListType

P = 128
NEG = -1e30
LN_EPS = 1e-5


def build(nc, x_prompt, x_sample, cache_fox_kv, cache_fox_logf, cache_nsa_kv, state_nsa_win, state_conv,
          page_table, w_in, fox_b_f, gmlp_w_s, gmlp_b_s, nsa_cmp_pe, nsa_cmp_w1, nsa_cmp_w2, conv_w, w_out,
          ln_g, ln_b, w_router, w_exp_gate, w_exp_up, w_exp_down, *outs):
    (y_prompt, y_sample, fox_kv_p, fox_kv_s, fox_lf_p, fox_lf_s, nsa_kv_p, nsa_kv_s, nsa_win_p, nsa_win_s,
     conv_p, conv_s, gmlp_v_s) = outs

    SEQ, D = x_prompt.shape[1], x_prompt.shape[2]
    NB, TN = x_sample.shape[0], x_sample.shape[1]
    H, DH = 4, 64
    GW = H * DH
    KD = D // P
    NT = SEQ // P
    TILES = NT + 1
    NS = NB * TN
    TOK = SEQ + NS
    PAST = state_nsa_win.shape[2]
    PAGE = cache_nsa_kv.shape[2]
    NPG = PAST // PAGE
    NPOOL = cache_nsa_kv.shape[1]
    WINDOW = 512
    assert PAGE == P and NS == 64 and PAST == WINDOW
    SCALE = DH ** -0.5
    rows_of = [P] * NT + [NS]

    A_U, A_V, B_Q, B_K, B_V, B_F = 0, GW, 2 * GW, 3 * GW, 4 * GW, 5 * GW
    C_Q = B_F + H
    C_KV = C_Q + GW
    C_G = C_KV + 6 * DH
    D_H = C_G + 3 * H
    D_B, D_C = D_H + GW, D_H + 2 * GW

    ctx = ExitStack()
    with ctx:
        def sb(name, shape, dt=F32):
            return ctx.enter_context(nc.sbuf_tensor(name, shape, dt))

        def sem(name):
            return ctx.enter_context(nc.semaphore(name))

        psum_all = ctx.enter_context(nc.psum_tensor("psum_all", [P, 8, 512], F32))
        psum = [psum_all[:, i, :] for i in range(8)]

        def banks(i, n):
            return psum_all[:, i:i + n, :].rearrange("p i n -> p (i n)")

        arena = sb("arena", [P, 47084])

        def at(off, *dims, part=P):
            n = 1
            for d in dims:
                n *= d
            v = arena[0:part, off:off + n]
            names = " ".join(f"d{i}" for i in range(len(dims)))
            return v.rearrange(f"p ({names}) -> p {names}", **{f"d{i}": d for i, d in enumerate(dims)}) if len(dims) > 1 else v

        R_X = 0
        R_W = R_X + KD * TOK
        R_FOX = R_W + 2 * KD * 512
        R_NQ = R_FOX + 2 * H * SEQ
        R_XR = R_NQ + H * SEQ
        R_UV = R_XR + 2 * D + 2 * 512
        R_FV = R_UV + TILES * 2 * GW
        R_NR = R_FV + TILES * GW
        R_SK = R_NR + TILES * (6 * DH + 12)
        R_YD = R_SK + 2 * TOK

        ident = sb("ident", [P, P])
        ident_bf = sb("ident_bf", [P, P], BF16)
        ones = sb("ones", [P, P])
        tri_u = sb("tri_u", [P, P])

        causal_m = sb("causal_m", [P, P], BF16)
        far_m = sb("far_m", [P, P], BF16)
        zeros_bf = sb("zeros_bf", [P, P], BF16)

        x_rows = at(R_XR, 2, D)
        xT = at(R_X, KD, TOK)
        w_buf = at(R_W, 2, KD * 512)
        uv = at(R_UV, TILES, 2 * GW)
        qk_rows = at(R_XR + 2 * D, 2, 2 * GW)
        foxT_q = at(R_FOX, H, SEQ, part=DH + 2)
        foxT_k = at(R_FOX + H * SEQ, H, SEQ, part=DH + 2)
        nsaT_q = at(R_NQ, H, SEQ, part=DH)
        fox_v = at(R_FV, TILES, GW)
        nsa_rows = at(R_NR, TILES, 6 * DH + 12)
        b_f = sb("b_f", [P, H, TILES])
        selT_k = at(R_SK, TOK, part=DH)
        winT_k = at(R_SK + TOK, TOK, part=DH)
        yd_T = at(R_YD, 2, TOK)

        ws_T = sb("ws_T", [P, H, P])
        ws_rows = qk_rows[:, 0, :].rearrange("p (h s) -> p h s", h=H)
        ws_s = sb("ws_s", [NS, H, NS])
        bs = sb("bs", [P, 2, H])
        ln_stat = sb("ln_stat", [P, TILES, H, 2])
        ln_sq = sb("ln_sq", [P, GW])
        lnc = sb("lnc", [P, 4])
        cw = sb("cw", [P, 2, 3])
        tail_w = R_W + KD * 512 + KD * 3 * P
        conv_y = at(tail_w, 512)
        dh_T = [at(tail_w + 512, 512), at(R_XR + 2 * (2 + SEQ), 512), at(R_XR + 2 * (2 + SEQ) + 512, NS)]
        z_p = at(R_XR, 2, 2 + SEQ)
        z_s = sb("z_s", [P, 2, NB, 2 + TN])

        foxS_q = sb("foxS_q", [P, 2, NB, H, TN])
        foxS_k = sb("foxS_k", [P, 2, NS])
        nsaS_q = sb("nsaS_q", [DH, NB, H, TN])

        bias_f = sb("bias_f", [P, H])
        lf_x = sb("lf_x", [P, H, TILES])
        lf_e = sb("lf_e", [P, H, TILES])
        lf = sb("lf", [P, H, TILES])
        lf_rows = sb("lf_rows", [P, TILES, H])
        carry = sb("carry", [P, H, NT])
        cum = sb("cum", [P, H, NT])
        cum_T = sb("cum_T", [H * NT, 2, P])

        P_buf = at(R_W, 2, SEQ)
        PT_buf = at(R_W + 2 * SEQ, 2, SEQ)
        gates = sb("gates", [P, TILES, 3, H])
        neg_max = sb("neg_max", [P, 4])
        row_sum = sb("row_sum", [P, 4])
        recip = sb("recip", [P, 4])
        coef = sb("coef", [P, 4])
        win_tiles = WINDOW // P
        jobs = [("fox", qt, h) for qt in range(NT) for h in range(H)]
        N_FOX = len(jobs)
        jobs += [(br, qt, h) for qt in range(NT) for h in range(H) for br in ("sel", "win")]
        J = len(jobs)

        def keys_of(i):
            br, qt, _ = jobs[i]
            k0 = max(0, qt - win_tiles) if br == "win" else 0
            return k0, qt + 1 - k0

        def wide_jobs(i):
            return sum(keys_of(n)[1] > 4 for n in range(i + 1))

        x_biased = sem("x_biased")
        lf_parts = sem("lf_parts")
        lf_ready = sem("lf_ready")
        cum_done = sem("cum_done")
        c_ready = sem("c_ready")
        cT_done = sem("cT_done")
        cT_copied = sem("cT_copied")
        c_rows = sem("c_rows")
        gate_x = sem("gate_x")
        gates_ready = sem("gates_ready")
        s_ready = sem("s_ready")
        max_ready = sem("max_ready")
        p_ready = sem("p_ready")
        p_turned = sem("p_turned")
        pt_dve = sem("pt_dve")
        pt_act = sem("pt_act")
        o_ready = sem("o_ready")
        y_done = sem("y_done")

        CMP_LEN, UNIT = nsa_cmp_pe.shape[2], 16
        HID = nsa_cmp_w1.shape[3]
        U_P, U_S = SEQ // UNIT, PAST // UNIT
        NU = U_P + NB * U_S
        NC_P, NC_S = U_P - 1, U_S - 1
        NCB = NU - 1
        kcvc_T = at(R_X, UNIT, NU + 2)
        cmp_w1 = at(R_W + 4 * SEQ, CMP_LEN, HID)
        cmp_w2 = sb("cmp_w2", [HID, 2, DH])
        pe_rows = sb("pe_rows", [CMP_LEN, 2 * DH])
        hid_bias = sb("hid_bias", [HID, 2])
        hid = at(R_XR, 2, NU)
        cmpT_k = at(R_XR + 2 * NU, NU, part=DH)
        cmp_v_p = at(R_XR + 3 * NU, DH)
        cmp_v_s = at(R_XR + 3 * NU + DH, NB, DH)
        lf_rep = at(R_XR + 3 * NU + DH + NB * DH, 2, NPG, P)
        nsa_cache = at(R_FOX, NB * NPG, 4 * DH)
        fox_cache = at(R_X, 4 * NPG, 2 * GW)
        win_cache = at(R_W + 4 * SEQ, NB, NPG, 2 * DH)
        lf_past = sb("lf_past", [P, NB * NPG, H])
        pages = sb("pages", [1, NB * NPG], I32)
        cmp_m = sb("cmp_m", [P, NT, NC_P], BF16)
        any_cmp = sb("any_cmp", [P, 1])
        head_v = sb("head_v", [P, 4, H])

        sjobs = [("fox", 0), ("sel", 0), ("sel", 1), ("win", 0), ("win", 1), ("cmp", 0), ("cmp", 1), ("fox", 1)]
        units = []
        for u, (br, g) in enumerate(sjobs):
            if br != "cmp":
                units += [(u, b, pr) for b in range(4) for pr in range(2 if br == "fox" else 1)]
        SW = PAST + NS
        Ps = at(R_W, 2, SW)
        PTs = at(R_W + 2 * SW, NPG + 1, P)
        KTs = at(R_W + 2 * SW + (NPG + 1) * P, 4, PAST)
        o_m = at(R_NQ + D, 4, GW)
        o_nsa = at(R_NQ + D + 4 * GW, 2, DH)
        o_coef = at(R_NQ + D + 4 * GW + 2 * DH, 2, H)
        later = sb("later", [P, PAST])
        same = sb("same", [NS, NS])
        new_m = sb("new_m", [NS, NS], BF16)
        left_m = sb("left_m", [NS, TN], BF16)
        left_f = sb("left_f", [NS, TN])
        spread = sb("spread", [NS, 2, P])
        spread_bf = sb("spread_bf", [NS, 2, P], BF16)
        gather = sb("gather", [P, 2, NS])
        lf_new = sb("lf_new", [NS, 2, P])
        head_m = sb("head_m", [P, H])
        gate_s = sb("gate_s", [P, 2, 3])
        gate_t = sb("gate_t", [P, 3, H])
        s_stat = sb("s_stat", [P, 2, 4])

        pages_loaded = sem("pages_loaded")
        nsa_cache_in = sem("nsa_cache_in")
        cmp_w_in = sem("cmp_w_in")
        fox_cache_in = sem("fox_cache_in")
        win_cache_in = sem("win_cache_in")
        masks_ready = sem("masks_ready")
        cc_turned = sem("cc_turned")
        cc_dve = sem("cc_dve")
        cc_act = sem("cc_act")
        pe_turned = sem("pe_turned")
        pe_copied = sem("pe_copied")
        comp_done = sem("comp_done")
        hid_ready = sem("hid_ready")
        cmp_proj = sem("cmp_proj")
        cmp_kv = sem("cmp_kv")
        c_scored = sem("c_scored")
        c_shifted = sem("c_shifted")
        c_exp = sem("c_exp")
        c_turned = sem("c_turned")
        c_pt = sem("c_pt")
        c_out = sem("c_out")
        c_added = sem("c_added")
        conv_stored = sem("conv_stored")
        s_masks = sem("s_masks")
        s_setup = sem("s_setup")
        s_setup_used = sem("s_setup_used")
        s_ops = sem("s_ops")
        kt_turned = sem("kt_turned")
        kt_dve = sem("kt_dve")
        kt_act = sem("kt_act")
        kt_used = sem("kt_used")
        ss_ready = sem("ss_ready")
        smax_ready = sem("smax_ready")
        sp_ready = sem("sp_ready")
        sp_turned = sem("sp_turned")
        spt_ready = sem("spt_ready")
        so_ready = sem("so_ready")
        so_done = sem("so_done")
        om_ready = sem("om_ready")
        ys_ready = sem("ys_ready")
        ys_copied = sem("ys_copied")

        ALPHA = 2 ** 0.25
        NE, F = w_router.shape[1], w_exp_gate.shape[3]
        EG = 4
        layer = at(R_W, TILES, D)
        R_WO = R_W + TILES * D
        wo = at(R_WO, KD, D)
        x1T = at(R_X, KD, TOK)
        x_res = at(R_NR, 2, D)
        mix_T = at(R_NR + 2 * D, 2, 6, P)
        ln_row = [at(R_NR + 2 * D + 12 * P, 2, D), at(R_WO + 2 * KD * F + F // P * D, 2, D)]
        ln_s = sb("ln_s", [P, 2, 4])
        w_r = sb("w_r", [P, KD, NE])
        R_R = R_UV + 18 * P
        probs, *r16 = [at(R_R + i * TILES * NE, TILES, NE) for i in range(3)]
        r4 = [at(R_R + 5 * TILES * NE + i * TILES * EG, TILES, EG) for i in range(4)]
        R_R1 = R_R + 5 * TILES * NE + 4 * TILES * EG
        r1 = [at(R_R1 + i * TILES, TILES) for i in range(3)]
        rank16 = at(R_R1 + 3 * TILES, NE)
        iota_i = sb("iota_i", [P, P], I32)
        tok_i = sb("tok_i", [P, TILES], I32)

        wo_in = sem("wo_in")
        x_res_in = [sem(f"x_res_in{i}") for i in range(2)]
        ln_in = sem("ln_in")
        router_in = sem("router_in")
        mix_turned = sem("mix_turned")
        mix_dve = sem("mix_dve")
        mix_act = sem("mix_act")
        r_done = sem("r_done")
        mean_ready = sem("mean_ready")
        std_ready = sem("std_ready")
        normed = sem("normed")
        x1_turned = sem("x1_turned")
        x1T_dve = sem("x1T_dve")
        x1T_act = sem("x1T_act")
        logits_done = sem("logits_done")
        rmax_ready = sem("rmax_ready")
        rexp_ready = sem("rexp_ready")
        gate_ready = sem("gate_ready")

        TOP_K = 2
        MAX_SLOTS = (TOP_K * TOK + NE * (P - 1)) // P
        MIN_SLOTS = -(-TOP_K * TOK // P)
        PAIRS_MAX = (MAX_SLOTS + 1) // 2
        NSL = 2 * PAIRS_MAX + 2
        x1_dram = nc.dram_tensor("x1_scratch", [TOK, D], F32, kind="Internal").ap()
        y_dram = nc.dram_tensor("slot_rows", [NSL, P, D], F32, kind="Internal").ap()
        slot_tok = sb("slot_tok", [P, NSL], I32)
        slot_gate = sb("slot_gate", [P, NSL])
        slot_of = sb("slot_of", [P, TOP_K * TILES], I32)
        T_UPTO, T_PAIRS, T_E1 = NSL, NSL + NE, NSL + NE + 2
        table = sb("table", [1, 2 * NSL + NE + 2], I32)
        free = [R_R1 + 3 * TILES + NE]

        def more(*dims):
            off = free[0]
            n = 1
            for d in dims:
                n *= d
            free[0] += n
            assert free[0] <= R_SK
            return at(off, *dims)

        no_rows = at(R_UV, D)
        no_rows_ready = sem("no_rows_ready")
        rest_cleared = sem("rest_cleared")
        lo_hot = at(R_UV, TOP_K * TILES, P)
        hot = more(TOP_K, TILES, NE)
        picked = more(TILES + 1, NE)
        le16 = more(NE, NE)
        le16_x = more(NE, NE)
        over = more(NE, TILES)
        n_tiles, upto, alt16 = more(NE), more(NE), more(NE)
        pos16 = more(TILES, NE)
        pos_x = more(TOP_K * TILES, NE)
        pos, lo_pos, hi_cnt = [more(TOP_K * TILES) for _ in range(3)]
        ge_tile = more(TOP_K * TILES, NSL + 1)
        hi_hot = more(TOP_K * TILES, NSL)
        slot_vals = more(TOP_K * TILES, 2 * NSL)
        iota_f = more(P)
        iota_p = more(NSL + 1)
        tok_f = more(TILES)
        gate2 = more(TOP_K, TILES)
        e_cmp = more(NSL, NE - 1)[0:1]
        e_f = more(2 * NSL + NE + 2)[0:1]

        EW = KD * 2 * F + F // P * D
        R_EW = [R_WO, R_WO + KD * D]
        x_slot = at(R_X, 2, D)
        xT_slot = at(R_X + 2 * D, 2, KD, P)
        y_slot = at(R_X + 4 * D, 2, D)
        sil = at(R_X + 6 * D, F)
        h_row = at(R_X + 6 * D + F, F)
        h_T = at(R_X + 6 * D + 2 * F, F // P, P)
        y_pair = at(R_WO, 3, TOP_K, D)
        ew_in = [sem(f"ew_in{i}") for i in range(2)]
        picked_ready = sem("picked_ready")
        ranked = sem("ranked")
        hots_ready = sem("hots_ready")
        slots_done = sem("slots_done")
        slots_ready = sem("slots_ready")
        x1_stored = sem("x1_stored")
        xs_in = [sem(f"xs_in{i}") for i in range(2)]
        tok_now = sb("tok_now", [P, 2], I32)
        tok_set = sem("tok_set")
        xs_turned = sem("xs_turned")
        xs_dve = sem("xs_dve")
        xs_act = sem("xs_act")
        hid_done = sem("hid_done")
        sil_ready = sem("sil_ready")
        h_ready = sem("h_ready")
        h_turned = sem("h_turned")
        hT_ready = sem("hT_ready")
        down_done = sem("down_done")
        y_dve = sem("y_dve")
        y_act = sem("y_act")
        ys_stored = [sem(f"ys_stored{i}") for i in range(2)]
        yp_in = [sem(f"yp_in{i}") for i in range(3)]

        def pairs_of(eng):
            return eng.value_load(table[0:1, T_PAIRS:T_PAIRS + 1], min_val=(MIN_SLOTS + 1) // 2,
                                  max_val=PAIRS_MAX)

        consts_ready = sem("consts_ready")
        x_loaded = [sem(f"x_loaded{i}") for i in range(2)]
        w_loaded = [sem(f"w_loaded{i}") for i in range(2)]
        small_loaded = sem("small_loaded")
        turned = sem("turned")
        turn_copied = sem("turn_copied")
        proj_done = sem("proj_done")
        proj_copied = sem("proj_copied")
        dve_step = sem("dve_step")
        var_ready = sem("var_ready")
        lnv_ready = sem("lnv_ready")
        rstd_ready = sem("rstd_ready")
        v_ready = sem("v_ready")
        zg_done = sem("zg_done")
        zg_used = sem("zg_used")
        ws_turned = sem("ws_turned")
        ws_copied = sem("ws_copied")
        ws_masked = sem("ws_masked")
        z_used = sem("z_used")
        yd_ready = sem("yd_ready")
        out_sem = sem("out_stored")
        outs_n = [0]

        GROUPS = [(A_U, 512), (B_Q, 512), (B_V, GW + H), (C_Q, GW), (C_KV, 6 * DH + 12)]
        LOADS = [[(c, w)] for c, w in GROUPS] + [[(D_H + f * P, P), (D_C + f * P, P), (D_B + f * P, P)]
                                                 for f in range(2)]
        NRG = len(GROUPS)
        N_ROWJ = NRG * TILES
        CHUNKS = [(0, 512), (512, 512), (SEQ, NS)]

        def w_view(g):
            n = sum(w for _, w in LOADS[g])
            return w_buf[:, g % 2, 0:KD * n].rearrange("p (k n) -> p k n", k=KD)

        def tok0(t):
            return t * P

        def w_last_use(g):
            return (g + 1) * TILES if g < NRG else N_ROWJ + 9 * (g - NRG + 1)

        k_stored = [sem(f"k_stored{i}") for i in range(2)]
        lf_past_in = sem("lf_past_in")

        def tail(sp):
            sp.wait_ge(k_stored[0], 16 * ((TILES + 1) // 2))
            sp.wait_ge(k_stored[1], 16 * (TILES // 2))
            sp.wait_ge(out_sem, 16 * outs_n[0])
            sp.wait_ge(conv_stored, 16 * 2 * (1 + NB))

        pool_step = sem("pool_step")
        ws_s_ready = sem("ws_s_ready")

        ws_loaded = sem("ws_loaded")

        def gate_rows(pe, t):
            n = rows_of[t]
            bank = psum[4 + t % 2]
            pe.wait_ge(v_ready, t + 1)
            if t == 0:
                pe.wait_ge(ws_masked, 1)
                pe.wait_ge(turn_copied, 2 * TILES - 1)
            if t == NT:
                pe.wait_ge(ws_s_ready, 16 * NB)
            if t >= 2:
                pe.wait_ge(zg_used, t - 1)
            for h in range(H):
                w = ws_T[:, h, :] if t < NT else ws_s[:, h, :]
                ins = nc.tensor.matmul(bank[0:n, h * DH:(h + 1) * DH], w, uv[0:n, t, GW + h * DH:GW + (h + 1) * DH],
                                       start=True, stop=True)
            ins.then_inc(zg_done, 1)

        def w_count(g):
            return 16 * sum(len(LOADS[i]) for i in range(g % 2, g + 1, 2))

        def bank_free(pe, j):
            i = j - 4
            if i < N_ROWJ:
                pe.wait_ge(proj_copied, i + 1)
                return
            f, part, c = (i - N_ROWJ) // 9, (i - N_ROWJ) % 9 // 3, (i - N_ROWJ) % 3
            if part == 0:
                pe.wait_ge(proj_copied, N_ROWJ + 3 * f + c + 1)
            else:
                pe.wait_ge(z_used, 6 * f + 3 * (part - 1) + c + 1)

        def copy_units(copy, q):
            n = 512 // UNIT
            return copy(kcvc_T[:, :, q * n:(q + 1) * n],
                        psum[4 + q % 2][:].rearrange("p (u r) -> p r u", r=UNIT))

        def copy_keys(eng, copy, k):
            rows = P if sjobs[units[k][0]][0] == "fox" else DH
            eng.wait_ge(kt_turned, k + 1)
            if k >= 4:
                eng.wait_ge(kt_used, k - 3)
            return copy(KTs[0:rows, k % 4, :], psum[4 + k % 2][0:rows, :])

        act_step = sem("act_step")
        y_stored = sem("y_stored")

        def load_expert(sp, e, i):
            def src(w):
                return (w[0, e] if isinstance(e, int) else w[0, bass.ds(e, 1)].rearrange("o a b -> (o a) b")
                        ).rearrange("(k p) n -> p k n", p=P)
            gu = at(R_EW[i], KD, 2, F)
            sp.dma_start(gu[:, :, 0, :], src(w_exp_gate)).then_inc(ew_in[i], 16)
            sp.dma_start(gu[:, :, 1, :], src(w_exp_up)).then_inc(ew_in[i], 16)
            sp.dma_start(at(R_EW[i] + KD * 2 * F, F // P, D), src(w_exp_down)).then_inc(ew_in[i], 16)

        block = ctx.enter_context(nc.Block())

        @block.sync
        def _(sp):
            def load_x(t):
                if t >= 2:
                    sp.wait_ge(turned, t - 1)
                src = x_prompt[0, tok0(t):tok0(t) + P, :] if t < NT else x_sample.rearrange("b t d -> (b t) d")
                sp.dma_start(x_rows[0:rows_of[t], t % 2, :], src).then_inc(x_loaded[t % 2], 16)

            def load_w(g):
                if g >= 2:
                    sp.wait_ge(proj_done, w_last_use(g - 2))
                v, at = w_view(g), 0
                for c, w in LOADS[g]:
                    sp.dma_start(v[:, :, at:at + w], w_in[0, :, c:c + w].rearrange("(k p) n -> p k n", p=P)
                                 ).then_inc(w_loaded[g % 2], 16)
                    at += w

            load_x(0)
            load_x(1)
            load_w(0)
            load_w(1)
            for t in range(2, TILES):
                load_x(t)

            def store(dst, src, sem_=out_sem):
                outs_n[0] += 1
                sp.dma_start(dst, src).then_inc(sem_, 16)

            def store_slow(dst, src):
                sp.dma_start(dst, src, allow_slow_non_contiguous=True).then_inc(conv_stored, 16)

            j = 0
            for g in range(NRG):
                if g >= 1:
                    load_w(g + 1)
                for t in range(TILES):
                    j += 1
                    n = rows_of[t]
                    if g == 1:
                        sp.wait_ge(proj_copied, j)
                        kr = qk_rows[0:n, t % 2, GW:2 * GW].rearrange("p (h d) -> p h d", h=H)
                        dst = (fox_kv_p[0, 0, tok0(t):tok0(t) + P, 0] if t < NT
                               else fox_kv_s[0, :, :, 0].rearrange("b t h d -> (b t) h d"))
                        sp.dma_start(dst, kr).then_inc(k_stored[t % 2], 16)
                if g == 2:
                    sp.wait_ge(proj_copied, j)
                    store(fox_kv_p[0, 0, :, 1].rearrange("(t p) h d -> p t (h d)", p=P), fox_v[:, 0:NT, :])
                    store(fox_kv_s[0, :, :, 1].rearrange("b t h d -> (b t) (h d)"), fox_v[0:NS, NT, :])
                if g == 4:
                    sp.wait_ge(lf_ready, 2)
                    sp.wait_ge(cT_copied, 1)
                    sp.dma_start(foxT_q[DH:DH + 1, :, :].rearrange("o h (t n) -> o (h t) n", n=P),
                                 cum_T[:, 0, :]).then_inc(c_rows, 16)
                    sp.dma_start(foxT_k[DH + 1:DH + 2, :, :].rearrange("o h (t n) -> o (h t) n", n=P),
                                 cum_T[:, 1, :]).then_inc(c_rows, 16)
                    sp.wait_ge(proj_copied, j)
                    store(nsa_kv_p[0, 0].rearrange("(t p) c d -> p t (c d)", p=P), nsa_rows[:, 0:NT, 0:4 * DH])
                    store(nsa_kv_s[0].rearrange("b t c d -> (b t) (c d)"), nsa_rows[0:NS, NT, 0:4 * DH])
                    keep = WINDOW // P
                    store(nsa_win_p[0, 0].rearrange("(t p) c d -> p t (c d)", p=P),
                          nsa_rows[:, NT - keep:NT, 4 * DH:6 * DH])
                    for b in range(NB):
                        store(nsa_win_s[0, b, PAST - TN:PAST].rearrange("t c d -> t (c d)"),
                              nsa_rows[TN * b:TN * b + TN, NT, 4 * DH:6 * DH])
                    store(nsa_win_s[0, :, 0:PAST - TN].rearrange("b t c d -> b (t c d)"),
                          state_nsa_win[0, :, TN:PAST].rearrange("b t c d -> b (t c d)"))

            load_w(NRG + 1)
            store(fox_lf_p[0, 0].rearrange("(t p) h -> p t h", p=P), lf_rows[:, 0:NT, :])
            store(fox_lf_s[0].rearrange("b t h -> (b t) h"), lf_rows[0:NS, NT, :])
            sp.wait_ge(v_ready, TILES)
            store(gmlp_v_s[0].rearrange("b t h d -> (b t) (h d)"), uv[0:NS, NT, GW:2 * GW])
            sp.wait_ge(z_used, 12)
            for f in range(2):
                fs = slice(f * P, f * P + P)
                store_slow(conv_p[0, 0, :, fs].rearrange("j p -> p j"), z_p[:, f, SEQ:SEQ + 2])
                for b in range(NB):
                    store_slow(conv_s[0, b, :, fs].rearrange("j p -> p j"), z_s[:, f, b, TN:TN + 2])

            def load_pages(cache, dst, n, first, done):
                with sp.Fori(0, n) as i:
                    page = sp.value_load(pages[0:1, bass.ds(i + first, 1)], min_val=0, max_val=NPOOL - 1)
                    sp.dma_start(dst[:, bass.ds(i, 1), :], cache[bass.ds(page, 1)]).then_inc(done, 16)

            sp.dma_start(pages[:], page_table.rearrange("(o b) n -> o (b n)", o=1)).then_inc(pages_loaded, 16)
            sp.wait_ge(z_used, 12)
            for c in range(2):
                sp.dma_start(cmp_w1[c * DH:(c + 1) * DH], nsa_cmp_w1[0, c].rearrange("(l d) n -> d l n", d=DH)
                             ).then_inc(cmp_w_in, 16)
                sp.dma_start(pe_rows[:, c * DH:(c + 1) * DH], nsa_cmp_pe[0, c]).then_inc(cmp_w_in, 16)
                sp.dma_start(cmp_w2[:, c, :], nsa_cmp_w2[0, c]).then_inc(cmp_w_in, 16)
            sp.wait_ge(pages_loaded, 16)
            load_pages(cache_fox_logf[0].rearrange("n p h -> n p h"), lf_past, NB * NPG, 0, lf_past_in)
            sp.wait_ge(s_ready, N_FOX)
            load_pages(cache_nsa_kv[0].rearrange("n p c d -> n p (c d)"), nsa_cache, NB * NPG, 0, nsa_cache_in)
            sp.wait_ge(comp_done, 2)
            fox_pages = cache_fox_kv[0].rearrange("n p c h d -> n p (c h d)")
            load_pages(fox_pages, fox_cache, 4 * NPG, 0, fox_cache_in)
            for b in range(NB):
                sp.dma_start(win_cache[:, b], state_nsa_win[0, b].rearrange("(n p) c d -> p n (c d)", p=P)
                             ).then_inc(win_cache_in, 16)
            sp.wait_ge(so_ready, 1)
            load_pages(fox_pages, fox_cache, 4 * NPG, 4 * NPG, fox_cache_in)
            sp.dma_start(w_r[:], w_router.rearrange("(k p) e -> p k e", p=P)).then_inc(router_in, 16)
            sp.wait_ge(so_ready, 3)
            sp.dma_start(wo[:], w_out[0].rearrange("(k p) n -> p k n", p=P)).then_inc(wo_in, 16)
            sp.wait_ge(so_ready, 5)
            sp.wait_ge(out_sem, 16 * outs_n[0])

            def rows_dram(x_p, x_s, t):
                return x_p[0, tok0(t):tok0(t) + P, :] if t < NT else x_s.rearrange("b t d -> (b t) d")

            sp.wait_ge(so_ready, len(sjobs))
            for i, row in enumerate((ln_g, ln_b)):
                sp.dma_start(ln_row[0][:, i, :], row[0, 0].partition_broadcast(P)).then_inc(ln_in, 16)

            def store_x1(t):
                sp.wait_ge(normed, t + 1)
                sp.dma_start(x1_dram[tok0(t):tok0(t) + rows_of[t]], layer[0:rows_of[t], t, :]).then_inc(x1_stored, 16)

            for t in range(TILES):
                if t >= 2:
                    sp.wait_ge(mean_ready, t - 1)
                sp.dma_start(x_res[0:rows_of[t], t % 2, :], rows_dram(x_prompt, x_sample, t)
                             ).then_inc(x_res_in[t % 2], 16)
                if t == 2:
                    sp.wait_ge(ys_ready, 1)
                    load_expert(sp, 1, 1)
                if t >= 2:
                    store_x1(t - 2)
            store_x1(TILES - 2)
            store_x1(TILES - 1)
            sp.wait_ge(r_done, TILES)
            load_expert(sp, 0, 0)
            for i, row in enumerate((ln_g, ln_b)):
                sp.dma_start(ln_row[1][:, i, :], row[0, 1].partition_broadcast(P)).then_inc(ln_in, 16)
            sp.wait_ge(slots_ready, 1)
            with sp.Fori(0, (NE - 2) // 2) as pair:
                for i in range(2):
                    done = sp.value_load(table[0:1, bass.ds(pair * 2 + (T_UPTO + i), 1)], min_val=0, max_val=MAX_SLOTS)
                    sp.wait_ge(down_done, done + 1)
                    sp.wait_ge(ew_in[i], pair * 48 + 48)
                    load_expert(sp, pair * 2 + (i + 2), i)
            sp.wait_ge(no_rows_ready, 1)
            pairs = pairs_of(sp)
            with sp.Fori(pairs, PAIRS_MAX + 1) as pair:
                for p in range(2):
                    sp.dma_start(y_dram[bass.ds(pair * 2 + p, 1)].rearrange("s p d -> (s p) d"), no_rows[:]
                                 ).then_inc(rest_cleared, 16)
            for t in range(TILES):
                sp.wait_ge(normed, TILES + t + 1)
                sp.dma_start(rows_dram(y_prompt, y_sample, t), layer[0:rows_of[t], t, :]).then_inc(y_stored, 16)
            sp.wait_ge(y_stored, 16 * TILES)
            tail(sp)

        @block.gpsimd
        def _(pool):
            pool.memset(ident[:], 0.0).then_inc(pool_step, 1)
            pool.memset(ident_bf[:], 0.0).then_inc(pool_step, 1)
            pool.memset(ones[:], 1.0).then_inc(pool_step, 1)
            pool.memset(zeros_bf[:], 0.0).then_inc(pool_step, 1)
            pool.wait_ge(pool_step, 4)
            for m in (ident, ident_bf):
                pool.affine_select(out=m[:], in_=m[:], compare_op=ALU.not_equal, fill=1.0, base=0,
                                   pattern=[[-1, P]], channel_multiplier=1).then_inc(consts_ready, 1)
            pool.affine_select(out=tri_u[:], in_=ones[:], compare_op=ALU.is_ge, fill=0.0, base=0,
                               pattern=[[1, P]], channel_multiplier=-1).then_inc(consts_ready, 1)
            pool.affine_select(out=causal_m[:], in_=zeros_bf[:], compare_op=ALU.is_ge, fill=NEG, base=0,
                               pattern=[[-1, P]], channel_multiplier=1).then_inc(consts_ready, 1)
            pool.affine_select(out=far_m[:], in_=zeros_bf[:], compare_op=ALU.is_gt, fill=NEG, base=0,
                               pattern=[[1, P]], channel_multiplier=-1).then_inc(consts_ready, 1)
            pool.memset(cmp_m[:], 0.0).then_inc(pool_step, 1)
            pool.memset(same[:], 1.0).then_inc(pool_step, 1)
            pool.memset(later[:], 1.0).then_inc(pool_step, 1)
            pool.memset(spread[:], 0.0).then_inc(pool_step, 1)
            pool.memset(lf_new[:], 1.0).then_inc(pool_step, 1)
            pool.wait_ge(pool_step, 9)
            pool.affine_select(out=cmp_m[:], in_=cmp_m[:], compare_op=ALU.is_ge, fill=NEG, base=1 - CMP_LEN,
                               pattern=[[P, NT], [-UNIT, NC_P]], channel_multiplier=1).then_inc(masks_ready, 1)
            pool.affine_select(out=any_cmp[:], in_=ones[:, 0:1], compare_op=ALU.is_ge, fill=0.0, base=1 - CMP_LEN,
                               pattern=[[0, 1]], channel_multiplier=1).then_inc(masks_ready, 1)
            pool.affine_select(out=later[:, PAST - P:PAST], in_=later[:, PAST - P:PAST], compare_op=ALU.is_gt, fill=0.0,
                               base=0, pattern=[[-1, P]], channel_multiplier=1).then_inc(masks_ready, 1)
            pool.affine_select(out=same[:], in_=same[:], compare_op=ALU.is_ge, fill=0.0, base=0,
                               pattern=[[-TN, NB], [-1, TN]], channel_multiplier=1).then_inc(masks_ready, 1)
            for g in range(2):
                base = -4 * TN * g
                pool.affine_select(out=spread[:, g, :], in_=spread[:, g, :], compare_op=ALU.not_equal, fill=1.0,
                                   base=base, pattern=[[-TN, 4], [0, H], [-1, TN]], channel_multiplier=1
                                   ).then_inc(masks_ready, 1)
                pool.affine_select(out=lf_new[:, g, :], in_=lf_new[:, g, :], compare_op=ALU.is_ge, fill=0.0,
                                   base=base, pattern=[[-TN, 4], [0, H], [0, TN]], channel_multiplier=1
                                   ).then_inc(masks_ready, 1)
            pool.wait_ge(masks_ready, 8)
            pool.affine_select(out=same[:], in_=same[:], compare_op=ALU.is_ge, fill=0.0, base=TN - 1,
                               pattern=[[TN, NB], [0, TN]], channel_multiplier=-1).then_inc(masks_ready, 1)
            for g in range(2):
                pool.affine_select(out=lf_new[:, g, :], in_=lf_new[:, g, :], compare_op=ALU.is_ge, fill=0.0,
                                   base=4 * TN * g, pattern=[[TN, 4], [0, H], [1, TN]], channel_multiplier=-1
                                   ).then_inc(masks_ready, 1)
            pool.iota(iota_i[:], pattern=[[1, P]], base=0, channel_multiplier=0).then_inc(masks_ready, 1)
            pool.iota(tok_i[:], pattern=[[P, TILES]], base=0, channel_multiplier=1).then_inc(masks_ready, 1)
            pool.wait_ge(ws_copied, 1)
            pool.affine_select(out=ws_T[:], in_=ws_T[:], compare_op=ALU.is_ge, fill=0.0, base=0,
                               pattern=[[0, H], [1, P]], channel_multiplier=-1).then_inc(ws_masked, 1)
            pool.memset(ws_s[:], 0.0).then_inc(pool_step, 1)
            pool.wait_ge(pool_step, 10)
            pool.wait_ge(ws_masked, 1)
            for b in range(NB):
                pool.dma_start(ws_s[TN * b:TN * b + TN, :, TN * b:TN * b + TN], ws_T[0:TN, :, 0:TN]
                               ).then_inc(ws_s_ready, 16)

            def gather_x1(col, n, p):
                pool.tensor_copy(tok_now[:, p:p + 1], slot_tok[:, col]).then_inc(tok_set, 1)
                pool.wait_ge(x1_stored, 16 * TILES)
                pool.wait_ge(tok_set, n)
                pool.indirect_dma_start(x_slot[:, p, :], None, x1_dram,
                                        bass.IndirectOffsetOnAxis(ap=tok_now[:, p:p + 1], axis=0)).then_inc(xs_in[p], 16)

            pool.wait_ge(slots_ready, 1)
            pool.memset(no_rows[:], 0.0).then_inc(no_rows_ready, 1)
            pairs = pairs_of(pool)
            rest = pool.value_load(table[0:1, T_PAIRS + 1:T_PAIRS + 2], min_val=1,
                                   max_val=PAIRS_MAX + 1 - (MIN_SLOTS + 1) // 2)
            gather_x1(slice(0, 1), 1, 0)
            gather_x1(slice(1, 2), 2, 1)
            with pool.Fori(0, pairs) as pair:
                for p in range(2):
                    pool.wait_ge(xs_turned, pair * 4 + (2 * p + 2))
                    gather_x1(bass.ds(pair * 2 + (p + 2), 1), pool.to_reg(pair * 2 + (p + 3)), p)
            for p in range(2):
                pool.wait_ge(xs_in[p], pairs * 16 + 16)
            stored, cleared = pool.to_reg(pairs * 16), pool.to_reg(rest * 32)
            pool.wait_ge(ew_in[0], 48 * (NE // 2))
            pool.wait_ge(ew_in[1], 48 * (NE // 2))
            pool.wait_ge(ys_stored[0], stored)
            pool.wait_ge(ys_stored[1], stored)
            pool.wait_ge(rest_cleared, cleared)
            rows = y_dram.rearrange("s p d -> (s p) d")
            for t in range(TILES):
                n = rows_of[t]
                if t >= 3:
                    pool.wait_ge(mean_ready, TILES + t - 2)
                for k in range(TOP_K):
                    c = k * TILES + t
                    pool.indirect_dma_start(y_pair[0:n, t % 3, k, :], None, rows,
                                            bass.IndirectOffsetOnAxis(ap=slot_of[0:n, c:c + 1], axis=0)
                                            ).then_inc(yp_in[t % 3], 16)

        @block.scalar
        def _(act):
            act.dma_start(ws_rows, gmlp_w_s[0].rearrange("h t s -> t h s")).then_inc(ws_loaded, 16)
            act.dma_start(bs[:, 0, :], gmlp_b_s[0].rearrange("h t -> t h"),
                          allow_slow_non_contiguous=True).then_inc(small_loaded, 16)
            for b in range(NB):
                act.dma_start(bs[TN * b:TN * b + TN, 1, :], gmlp_b_s[0, :, 0:TN].rearrange("h t -> t h"),
                              allow_slow_non_contiguous=True).then_inc(small_loaded, 16)
            act.dma_start(bias_f[:], fox_b_f[0].partition_broadcast(P)).then_inc(small_loaded, 16)
            for f in range(2):
                act.dma_start(cw[:, f, :], conv_w[0, :, f * P:(f + 1) * P].rearrange("j p -> p j"),
                              allow_slow_non_contiguous=True).then_inc(small_loaded, 16)
            for f in range(2):
                for b in range(NB):
                    act.dma_start(z_s[:, f, b, 0:2], state_conv[0, b, :, f * P:(f + 1) * P].rearrange("j p -> p j"),
                                  allow_slow_non_contiguous=True).then_inc(small_loaded, 16)
            for t in range(TILES):
                act.wait_ge(proj_done, t + 1)
                n = rows_of[t]
                nc.scalar.activation(uv[0:n, t, :], psum[t % 4][0:n, :], ACT.Gelu_apprx_tanh).then_inc(proj_copied, 1)
            act.wait_ge(var_ready, TILES + 1)
            nc.scalar.activation(ln_stat[:, :, :, 1], ln_stat[:, :, :, 1], ACT.Ln, bias=lnc[:, 0:1]).then_inc(lnv_ready, 1)
            act.wait_ge(lnv_ready, 1)
            nc.scalar.activation(ln_stat[:, :, :, 1], ln_stat[:, :, :, 1], ACT.Exp, scale=-0.5).then_inc(rstd_ready, 1)
            j = TILES
            for g in range(1, NRG):
                for t in range(TILES):
                    n, w = rows_of[t], GROUPS[g][1]
                    act.wait_ge(proj_done, j + 1)
                    if g == 1 and t >= 2:
                        act.wait_ge(turned, TILES + t - 1)
                        act.wait_ge(k_stored[t % 2], 16 * (t // 2))
                    if g == 1 and t < 2:
                        act.wait_ge(ws_turned, 1)
                    if g == 3:
                        act.wait_ge(turned, 2 * TILES + max(t - 1, 0))
                        if t < 2:
                            act.wait_ge(k_stored[t % 2], 16 * ((TILES + 1 - t) // 2))
                    ps = psum[j % 4]
                    if g == 1:
                        out = qk_rows[0:n, t % 2, :]
                    elif g == 2:
                        out = fox_v[0:n, t, :]
                    elif g == 3:
                        out = qk_rows[0:n, t % 2, 0:GW]
                    else:
                        out = nsa_rows[0:n, t, :]
                    w = out.shape[-1]
                    ins = nc.scalar.copy(out, ps[0:n, 0:w])
                    if g == 2:
                        nc.scalar.copy(b_f[0:n, :, t], ps[0:n, GW:GW + H]).then_inc(proj_copied, 1)
                    else:
                        ins.then_inc(proj_copied, 1)
                    j += 1
                    if (g, t) == (3, 0):
                        act.wait_ge(x_biased, 1)
                        nc.scalar.activation(lf_e[:], lf_x[:], ACT.Abs).then_inc(lf_parts, 1)
                        act.wait_ge(lf_parts, 1)
                        nc.scalar.activation(lf_e[:], lf_e[:], ACT.Exp, scale=-1.0).then_inc(lf_parts, 1)
                        act.wait_ge(lf_parts, 2)
                        nc.scalar.activation(lf_e[:], lf_e[:], ACT.Ln, bias=lnc[:, 1:2]).then_inc(lf_parts, 1)
            act.wait_ge(proj_copied, N_ROWJ)
            nc.scalar.activation(gates[:].rearrange("p t b h -> p t (b h)"), nsa_rows[:, :, 6 * DH:6 * DH + 12],
                                 ACT.Exp, scale=-1.0).then_inc(gate_x, 1)
            for f in range(2):
                if f:
                    act.wait_ge(z_used, 3)
                for c, (c0, cn) in enumerate(CHUNKS):
                    act.wait_ge(proj_done, N_ROWJ + 9 * f + c + 1)
                    nc.scalar.copy(dh_T[c], psum[(N_ROWJ + 9 * f + c) % 4][:, 0:cn]).then_inc(proj_copied, 1)

            def exp_scores(i):
                n = keys_of(i)[1]
                act.wait_ge(max_ready, i + 1)
                if i >= 2:
                    act.wait_ge(p_turned, i - 1)
                if i >= 4:
                    act.wait_ge(y_done, i - 3)
                nc.scalar.activation(P_buf[:, i % 2, 0:n * P], banks(2 * (i % 2), 2)[:, 0:n * P], ACT.Exp,
                                     bias=neg_max[:, i % 4:i % 4 + 1],
                                     accum_out=row_sum[:, i % 4:i % 4 + 1]).then_inc(p_ready, 1)

            def copy_pt_act(i):
                n = keys_of(i)[1]
                if n > 4:
                    act.wait_ge(p_turned, i + 1)
                    if i >= 2:
                        act.wait_ge(o_ready, i - 1)
                    nc.scalar.copy(PT_buf[:, i % 2, 512:n * P], psum[5][:, 0:(n - 4) * P]).then_inc(pt_act, 1)

            for i in range(J + 1):
                if i < J:
                    exp_scores(i)
                if i >= 1:
                    copy_pt_act(i - 1)

            for q in range(1, 2 + NB, 2):
                act.wait_ge(cc_turned, q + 1)
                copy_units(nc.scalar.copy, q).then_inc(cc_act, 1)
            act.wait_ge(comp_done, 2)
            act.wait_ge(conv_stored, 16 * 2 * (1 + NB))
            for c in range(2):
                ins = nc.scalar.copy(hid_bias[:, c:c + 1], psum[c][:, NU:NU + 1])
            ins.then_inc(act_step, 1)
            act.wait_ge(act_step, 1)
            for c in range(2):
                nc.scalar.activation(hid[:, c, 0:NCB], psum[c][:, 0:NCB], ACT.Gelu_apprx_tanh,
                                     bias=hid_bias[:, c:c + 1]).then_inc(hid_ready, 1)
            act.wait_ge(cmp_proj, 1)
            nc.scalar.copy(cmpT_k[:, 0:NCB], psum[2][0:DH, 0:NCB])
            nc.scalar.copy(cmp_v_p[0:NC_P, :], psum[3][0:NC_P, 0:DH])
            nc.scalar.copy(cmp_v_s[0:NC_S], psum[4][0:NC_S, 0:NB * DH].rearrange("p (b d) -> p b d", b=NB)
                           ).then_inc(cmp_kv, 1)
            for qt in range(NT + 1):
                if qt < NT:
                    act.wait_ge(c_shifted, qt + 1)
                    v = P_buf[:, qt % 2, 0:H * NC_P]
                    nc.scalar.activation(v, v, ACT.Exp).then_inc(c_exp, 1)
                if qt >= 1:
                    act.wait_ge(c_turned, qt)
                    if qt >= 3:
                        act.wait_ge(c_out, qt - 2)
                    nc.scalar.copy(PT_buf[0:NC_P, (qt - 1) % 2, 0:512], psum[4 + (qt - 1) % 2][0:NC_P, :]
                                   ).then_inc(c_pt, 1)
            k = 0
            for u, (br, g) in enumerate(sjobs):
                while k < len(units) and units[k][0] == u:
                    if k % 2:
                        copy_keys(act, nc.scalar.copy, k).then_inc(kt_act, 1)
                    k += 1
                act.wait_ge(smax_ready, u + 1)
                if u >= 2:
                    act.wait_ge(sp_turned, u - 1)
                    act.wait_ge(so_done, u - 1)
                w = NC_S if br == "cmp" else SW
                nc.scalar.activation(Ps[:, u % 2, 0:w], banks(2 * (u % 2), 2)[:, 0:w], ACT.Exp,
                                     bias=s_stat[:, u % 2, 0:1], accum_out=s_stat[:, u % 2, 1:2]).then_inc(sp_ready, 1)
            steps = [1]

            def link(ins):
                steps[0] += 1
                ins.then_inc(act_step, 1)
                act.wait_ge(act_step, steps[0])

            def copy_mix(t):
                n = rows_of[t]
                act.wait_ge(mix_turned, t + 1)
                if t >= 2:
                    act.wait_ge(r_done, t - 1)
                nc.scalar.copy(mix_T[:, t % 2, 4:6, 0:n], psum[5][:, 0:2 * P].rearrange("p (k n) -> p k n", k=2)[:, :, 0:n]
                               ).then_inc(mix_act, 1)

            def deviation(i, t):
                n, m = rows_of[t], TILES * i + t
                st = ln_s[0:n, m % 2, :]
                act.wait_ge(mean_ready, m + 1)
                link(nc.scalar.activation(banks(2 * (m % 2), 2)[0:n, :], layer[0:n, t, :], ACT.Square, bias=st[:, 1:2],
                                          accum_out=st[:, 2:3]))
                nc.scalar.activation(st[:, 2:3], st[:, 2:3], ACT.Sqrt, bias=lnc[0:n, 0:1], scale=1.0 / D).then_inc(std_ready, 1)

            def after_turn(t):
                n = rows_of[t]
                act.wait_ge(x1_turned, t + 1)
                nc.scalar.copy(x1T[:, 0:4, tok0(t):tok0(t) + n],
                               psum[6][:].rearrange("p (k n) -> p k n", k=4)[:, :, 0:n]).then_inc(x1T_act, 1)

            act.wait_ge(ys_ready, 1)
            copy_mix(0)
            for t in range(TILES + 1):
                if t + 1 < TILES:
                    copy_mix(t + 1)
                if t < TILES:
                    deviation(0, t)
                if t >= 1:
                    after_turn(t - 1)
            act.wait_ge(rmax_ready, 1)
            pv = probs[:].rearrange("p t e -> p (t e)")
            nc.scalar.activation(pv, pv, ACT.Exp).then_inc(rexp_ready, 1)
            def copy_x(n_turned, p):
                act.wait_ge(xs_turned, n_turned)
                nc.scalar.copy(xT_slot[:, p, 4:8, :], psum[5][:].rearrange("p (k n) -> p k n", k=4)).then_inc(xs_act, 1)

            act.wait_ge(slots_ready, 1)
            pairs = pairs_of(act)
            copy_x(2, 0)

            def slot_pair(pair):
                for p in range(2):
                    t1 = pair * 2 + (p + 1)
                    act.wait_ge(hid_done, t1)
                    nc.scalar.activation(sil[:], psum[p][:, 0:F], ACT.Silu).then_inc(sil_ready, 1)
                    copy_x(pair * 4 + (2 * p + 4), 1 - p)
                    if not isinstance(pair, int):
                        act.wait_ge(ys_stored[p], pair * 16)
                    act.wait_ge(down_done, t1 + 1)
                    nc.scalar.copy(y_slot[:, p, 512:1024], psum[3][:]).then_inc(y_act, 1)
                    act.wait_ge(y_act, t1)
                    act.wait_ge(y_dve, t1)
                    act.dma_start(y_dram[bass.ds(pair * 2 + p, 1)].rearrange("s p d -> (s p) d"), y_slot[:, p, :]
                                  ).then_inc(ys_stored[p], 16)

            slot_pair(0)
            with act.Fori(1, pairs) as pair:
                slot_pair(pair)
            for t in range(TILES):
                deviation(1, t)

        @block.tensor
        def _(pe):
            def turn_x(t):
                n = rows_of[t]
                pe.wait_ge(x_loaded[t % 2], 16 * (t // 2 + 1))
                if t >= 2:
                    pe.wait_ge(turn_copied, t - 1)
                for k in range(KD):
                    ins = nc.tensor.transpose(psum[4 + 2 * (t % 2) + k // 4][:, (k % 4) * P:(k % 4) * P + n],
                                              x_rows[0:n, t % 2, k * P:(k + 1) * P], ident[0:n, 0:n])
                ins.then_inc(turned, 1)

            def project_rows(g, t):
                j = g * TILES + t
                n, w = rows_of[t], GROUPS[g][1]
                if t == 0:
                    pe.wait_ge(w_loaded[g % 2], w_count(g))
                if g == 0:
                    pe.wait_ge(turn_copied, t + 1)
                if j >= 4:
                    pe.wait_ge(proj_copied, j - 3)
                wv = w_view(g)
                for k in range(KD):
                    ins = nc.tensor.matmul(psum[j % 4][0:n, 0:w], xT[:, k, tok0(t):tok0(t) + n], wv[:, k, 0:w],
                                           start=(k == 0), stop=(k == KD - 1))
                ins.then_inc(proj_done, 1)

            def turn_rows(g, t):
                e = {1: 1, 3: 2, 4: 3}[g] * TILES + t
                n = rows_of[t]
                pe.wait_ge(proj_copied, g * TILES + t + 1)
                pe.wait_ge(turn_copied, e - 1)
                if e == 2 * TILES:
                    pe.wait_ge(zg_used, TILES)
                A, B = psum[4 + 2 * (e % 2)], psum[5 + 2 * (e % 2)]
                I = ident[0:n, 0:n]
                if g == 1 and t < NT:
                    for h in range(H):
                        for bank, c in ((A, 0), (B, GW)):
                            ins = nc.tensor.transpose(bank[0:DH, h * P:(h + 1) * P],
                                                      qk_rows[:, t % 2, c + h * DH:c + (h + 1) * DH], I)
                elif g == 1:
                    for pair in range(2):
                        for bank, c in ((A, 0), (B, GW)):
                            ins = nc.tensor.transpose(bank[:, pair * P:pair * P + n],
                                                      qk_rows[0:n, t % 2, c + pair * P:c + (pair + 1) * P], I)
                elif g == 3:
                    for h in range(H):
                        ins = nc.tensor.transpose(A[0:DH, h * P:h * P + n],
                                                  qk_rows[0:n, t % 2, h * DH:(h + 1) * DH], I)
                else:
                    for i, c in enumerate((2, 4)):
                        ins = nc.tensor.transpose(A[0:DH, i * P:i * P + n], nsa_rows[0:n, t, c * DH:(c + 1) * DH], I)
                ins.then_inc(turned, 1)

            pe.wait_ge(consts_ready, 5)
            for t in range(TILES):
                turn_x(t)
                if t >= 1:
                    project_rows(0, t - 1)
            pe.wait_ge(ws_loaded, 16)
            pe.wait_ge(turn_copied, TILES)
            for h in range(H):
                ins = nc.tensor.transpose(psum[6][:, h * P:(h + 1) * P], ws_rows[:, h, :], ident[:])
            ins.then_inc(ws_turned, 1)
            project_rows(0, TILES - 1)
            pe.wait_ge(ws_copied, 1)
            for g in range(1, NRG):
                for t in range(TILES):
                    project_rows(g, t)
                    if g != 2 and t >= 1:
                        turn_rows(g, t - 1)
                    if g == 2:
                        gate_rows(pe, t)
                    if g in (2, 4) and t == 0:
                        turn_rows(g - 1, TILES - 1)
                    if (g, t) == (3, TILES - 1):
                        pe.wait_ge(lf_ready, 1)
                        lfp = lf[:, :, 0:NT]
                        nc.tensor.matmul(psum[5][:, 0:H * NT], tri_u[:], lfp, start=True, stop=True)
                        nc.tensor.matmul(psum[5][:, 64:64 + H * NT], ones[:], lfp, start=True, stop=True
                                         ).then_inc(cum_done, 1)
                    if (g, t) == (4, 1):
                        pe.wait_ge(c_ready, 1)
                        nc.tensor.transpose(psum[7][0:H * NT, 0:P], cum[:].rearrange("p h t -> p (h t)"), ident[:]
                                            ).then_inc(cT_done, 1)
            for f in range(2):
                g = NRG + f
                pe.wait_ge(w_loaded[g % 2], w_count(g))
                wv = w_view(g)
                for part in range(3):
                    for c, (c0, cn) in enumerate(CHUNKS):
                        j = N_ROWJ + 9 * f + 3 * part + c
                        bank_free(pe, j)
                        for k in range(KD):
                            ins = nc.tensor.matmul(psum[j % 4][:, 0:cn], wv[:, k, part * P:(part + 1) * P],
                                                   xT[:, k, c0:c0 + cn], start=(k == 0), stop=(k == KD - 1))
                        ins.then_inc(proj_done, 1)
                    if f == 0 and part == 0:
                        turn_rows(4, TILES - 1)

            def scores(i):
                br, qt, h = jobs[i]
                k0, n = keys_of(i)
                if i >= 2:
                    pe.wait_ge(p_ready, i - 1)
                elif i == 0:
                    pe.wait_ge(z_used, 12)
                    pe.wait_ge(turn_copied, 4 * TILES)
                    pe.wait_ge(c_rows, 32)
                q = (foxT_q if br == "fox" else nsaT_q)[:, h, qt * P:(qt + 1) * P]
                kT = foxT_k[:, h, :] if br == "fox" else selT_k if br == "sel" else winT_k
                S = banks(2 * (i % 2), 2)
                for c0 in range(0, n * P, 512):
                    cn = min(512, n * P - c0)
                    masks = []
                    if c0 + cn == n * P:
                        masks.append((n * P - P, causal_m))
                    if br == "win" and qt >= win_tiles and c0 == 0:
                        masks.append((0, far_m))
                    ins = nc.tensor.matmul(S[:, c0:c0 + cn], q, kT[:, k0 * P + c0:k0 * P + c0 + cn],
                                           start=True, stop=not masks, skip_group_check=True)
                    for k, (m0, m) in enumerate(masks):
                        ins = nc.tensor.matmul(S[:, m0:m0 + P], ident_bf[:], m[:], start=False,
                                               stop=(k == len(masks) - 1), skip_group_check=True)
                ins.then_inc(s_ready, 1)

            def turn_p(i):
                n = keys_of(i)[1]
                pe.wait_ge(p_ready, i + 1)
                if i >= 1:
                    pe.wait_ge(pt_dve, i)
                    if wide_jobs(i - 1):
                        pe.wait_ge(pt_act, wide_jobs(i - 1))
                for k in range(n):
                    ins = nc.tensor.transpose(psum[4 + k // 4][:, (k % 4) * P:(k % 4 + 1) * P],
                                              P_buf[:, i % 2, k * P:(k + 1) * P], ident[:])
                ins.then_inc(p_turned, 1)

            def p_times_v(i):
                br, qt, h = jobs[i]
                k0, n = keys_of(i)
                pe.wait_ge(pt_dve, i + 1)
                if wide_jobs(i):
                    pe.wait_ge(pt_act, wide_jobs(i))
                if i >= 2:
                    pe.wait_ge(y_done, i - 1)
                for k in range(n):
                    if br == "fox":
                        v = fox_v[:, k0 + k, h * DH:(h + 1) * DH]
                    else:
                        c = 3 if br == "sel" else 5
                        v = nsa_rows[:, k0 + k, c * DH:(c + 1) * DH]
                    ins = nc.tensor.matmul(psum[6 + i % 2][:, 0:DH], PT_buf[:, i % 2, k * P:(k + 1) * P], v,
                                           start=(k == 0), stop=(k == n - 1))
                ins.then_inc(o_ready, 1)

            for i in range(J + 2):
                if i < J:
                    scores(i)
                if 1 <= i <= J:
                    turn_p(i - 1)
                if i >= 2:
                    p_times_v(i - 2)

            pe.wait_ge(pt_dve, J)
            pe.wait_ge(pt_act, wide_jobs(J - 1))
            pe.wait_ge(y_done, J)
            pe.wait_ge(cmp_w_in, 16 * 6)
            nc.tensor.transpose(psum[6][:, 0:CMP_LEN], pe_rows[:], ident[0:CMP_LEN, 0:CMP_LEN]).then_inc(pe_turned, 1)
            for q in range(2 + NB):
                if q >= 2:
                    pe.wait_ge(cc_act if q % 2 else cc_dve, q // 2)
                if q == 2:
                    pe.wait_ge(nsa_cache_in, 16 * NB * NPG)
                for k in range(4):
                    src = nsa_rows[:, 4 * q + k, 0:2 * DH] if q < 2 else nsa_cache[:, (q - 2) * NPG + k, 0:2 * DH]
                    ins = nc.tensor.transpose(psum[4 + q % 2][:, k * P:(k + 1) * P], src, ident[:])
                ins.then_inc(cc_turned, 1)
            pe.wait_ge(pe_copied, 1)
            pe.wait_ge(cc_dve, 1 + NB // 2)
            pe.wait_ge(cc_act, 1 + NB // 2)
            for c in range(2):
                half = slice(c * DH, (c + 1) * DH)
                for l in range(CMP_LEN):
                    u0, r = l // UNIT, l % UNIT
                    ins = nc.tensor.matmul(psum[c][:, 0:NU + 1], cmp_w1[half, l, :], kcvc_T[half, r, u0:u0 + NU + 1],
                                           start=(l == 0), stop=(l == CMP_LEN - 1))
                ins.then_inc(comp_done, 1)
            pe.wait_ge(hid_ready, 2)
            nc.tensor.matmul(psum[2][0:DH, 0:NCB], cmp_w2[:, 0, :], hid[:, 0, 0:NCB], start=True, stop=True)
            nc.tensor.matmul(psum[3][0:NC_P, 0:DH], hid[:, 1, 0:NC_P], cmp_w2[:, 1, :], start=True, stop=True)
            for b in range(NB):
                u0 = U_P + U_S * b
                ins = nc.tensor.matmul(psum[4][0:NC_S, b * DH:(b + 1) * DH], hid[:, 1, u0:u0 + NC_S], cmp_w2[:, 1, :],
                                       start=True, stop=True)
            ins.then_inc(cmp_proj, 1)

            def cmp_scores(qt):
                if qt == 0:
                    pe.wait_ge(cmp_kv, 1)
                    pe.wait_ge(masks_ready, 11)
                if qt >= 2:
                    pe.wait_ge(c_shifted, qt - 1)
                S = psum[2 + qt % 2]
                for h in range(H):
                    nc.tensor.matmul(S[:, h * NC_P:(h + 1) * NC_P], nsaT_q[:, h, qt * P:(qt + 1) * P],
                                     cmpT_k[:, 0:NC_P], start=True, stop=False, skip_group_check=True)
                    ins = nc.tensor.matmul(S[:, h * NC_P:(h + 1) * NC_P], ident_bf[:], cmp_m[:, qt, :],
                                           start=False, stop=True, skip_group_check=True)
                ins.then_inc(c_scored, 1)

            def cmp_turn(qt):
                pe.wait_ge(c_exp, qt + 1)
                if qt >= 2:
                    pe.wait_ge(c_pt, qt - 1)
                for h in range(H):
                    ins = nc.tensor.transpose(psum[4 + qt % 2][0:NC_P, h * P:(h + 1) * P],
                                              P_buf[:, qt % 2, h * NC_P:(h + 1) * NC_P], ident[:])
                ins.then_inc(c_turned, 1)

            def cmp_out(qt):
                pe.wait_ge(c_pt, qt + 1)
                if qt >= 2:
                    pe.wait_ge(c_added, qt - 1)
                for h in range(H):
                    ins = nc.tensor.matmul(psum[6 + qt % 2][:, h * DH:(h + 1) * DH],
                                           PT_buf[0:NC_P, qt % 2, h * P:(h + 1) * P], cmp_v_p[0:NC_P, :],
                                           start=True, stop=True)
                ins.then_inc(c_out, 1)

            for qt in range(NT + 2):
                if qt < NT:
                    cmp_scores(qt)
                if 1 <= qt <= NT:
                    cmp_turn(qt - 1)
                if qt >= 2:
                    cmp_out(qt - 2)

            pe.wait_ge(c_added, NT)
            for g in range(2):
                nc.tensor.transpose(psum[6][:, g * NS:(g + 1) * NS], spread[:, g, :], ident[0:NS, 0:NS])
                ins = nc.tensor.matmul(psum[7][:, 16 * g:16 * g + 12], spread[:, g, :],
                                       gates[0:NS, NT].rearrange("p b h -> p (b h)"), start=True, stop=True)
            ins.then_inc(s_ops, 1)

            def turn_keys(k):
                u, b, pr = units[k]
                br, g = sjobs[u]
                if k < 2:
                    pe.wait_ge(c_pt, NT)
                else:
                    pe.wait_ge(kt_act if k % 2 else kt_dve, k // 2)
                if b == 0 and pr == 0:
                    if br == "fox":
                        pe.wait_ge(fox_cache_in, 16 * 4 * NPG * (g + 1))
                    if br == "win":
                        pe.wait_ge(win_cache_in, 16 * NB)
                bs_ = 4 * g + b
                for n in range(NPG):
                    if br == "fox":
                        src, rows = fox_cache[:, b * NPG + n, pr * P:(pr + 1) * P], P
                    elif br == "sel":
                        src, rows = nsa_cache[:, bs_ * NPG + n, 2 * DH:3 * DH], DH
                    else:
                        src, rows = win_cache[:, bs_, n, 0:DH], DH
                    ins = nc.tensor.transpose(psum[4 + k % 2][0:rows, n * P:(n + 1) * P], src, ident[:])
                ins.then_inc(kt_turned, 1)

            def score_keys(k):
                u, b, pr = units[k]
                br, g = sjobs[u]
                S = psum[2 * (u % 2)][32 * b:32 * b + 32, :]
                pe.wait_ge(kt_act if k % 2 else kt_dve, k // 2 + 1)
                if br == "fox":
                    ins = nc.tensor.matmul(S, foxS_q[:, pr, 4 * g + b].rearrange("p h t -> p (h t)"), KTs[:, k % 4, :],
                                           start=False, stop=(pr == 1), skip_group_check=True, tile_position=(0, 32 * b))
                else:
                    ins = nc.tensor.matmul(S, nsaS_q[:, 4 * g + b].rearrange("p h t -> p (h t)"), KTs[0:DH, k % 4, :],
                                           start=True, stop=(br == "sel"), skip_group_check=True,
                                           tile_position=(0, 32 * b))
                ins.then_inc(kt_used, 1)

            def new_scores(u):
                br, g = sjobs[u]
                S, Sn = psum[2 * (u % 2)], psum[2 * (u % 2) + 1][:, 0:NS]
                if u >= 2:
                    pe.wait_ge(sp_ready, u - 1)
                rows = slice(4 * g, 4 * g + 4)
                if br == "fox":
                    for n in range(NPG - 1, -1, -1):
                        w = (n + 1) * P
                        nc.tensor.matmul(S[:, 0:w], lf_rep[:, g, n, :], later[:, PAST - w:PAST],
                                         start=(n == NPG - 1), stop=False, skip_group_check=True)
                    for c in range(0, PAST, P):
                        nc.tensor.matmul(S[:, c:c + P], lf_new[:, g, :], ones[0:NS, :],
                                         start=False, stop=False, skip_group_check=True)
                    nc.tensor.matmul(Sn, lf_new[:, g, :], later[0:NS, PAST - P:PAST - P + NS], start=True, stop=False,
                                     skip_group_check=True)
                    for pr in range(2):
                        nc.tensor.matmul(Sn, foxS_q[:, pr, rows].rearrange("p b h t -> p (b h t)"), foxS_k[:, pr, :],
                                         start=False, stop=False, skip_group_check=True)
                else:
                    kT = selT_k if br == "sel" else winT_k
                    nc.tensor.matmul(Sn, nsaS_q[:, rows].rearrange("p b h t -> p (b h t)"), kT[:, SEQ:SEQ + NS],
                                     start=True, stop=False, skip_group_check=True)

            def cmp_sample_scores(u):
                g = sjobs[u][1]
                if u >= 2:
                    pe.wait_ge(sp_ready, u - 1)
                for b in range(4):
                    u0 = U_P + U_S * (4 * g + b)
                    ins = nc.tensor.matmul(psum[2 * (u % 2)][32 * b:32 * b + 32, 0:NC_S],
                                           nsaS_q[:, 4 * g + b].rearrange("p h t -> p (h t)"),
                                           cmpT_k[:, u0:u0 + NC_S], start=True, stop=True, tile_position=(0, 32 * b))
                ins.then_inc(ss_ready, 1)

            def turn_sample_p(u):
                br = sjobs[u][0]
                pe.wait_ge(sp_ready, u + 1)
                if u >= 1:
                    pe.wait_ge(spt_ready, u)
                    pe.wait_ge(so_done, u)
                if u == 0:
                    pe.wait_ge(s_setup, 2)
                if br == "cmp":
                    ins = nc.tensor.transpose(psum[6][0:NC_S, 0:P], Ps[:, u % 2, 0:NC_S], ident[:])
                else:
                    for n in range(NPG):
                        nc.tensor.transpose(psum[6][:, n * P:(n + 1) * P], Ps[:, u % 2, n * P:(n + 1) * P], ident[:])
                    ins = nc.tensor.transpose(psum[7][0:NS, 0:P], Ps[:, u % 2, PAST:SW], ident[:])
                ins.then_inc(sp_turned, 1)

            def sample_p_times_v(u):
                br, g = sjobs[u]
                pe.wait_ge(spt_ready, u + 1)
                if u >= 1:
                    pe.wait_ge(so_done, u)
                w = GW if br == "fox" else DH
                O = psum[7][:, 256:256 + w]
                if br != "cmp":
                    v = fox_v[0:NS, NT, :] if br == "fox" else nsa_rows[0:NS, NT, (3 if br == "sel" else 5) * DH:][:, 0:DH]
                    nc.tensor.matmul(O, PTs[0:NS, NPG, :], v, start=True, stop=False, skip_group_check=True)
                for b in range(4):
                    Ob, bs_ = O[32 * b:32 * b + 32, :], 4 * g + b
                    if br == "cmp":
                        ins = nc.tensor.matmul(Ob, PTs[0:NC_S, 0, 32 * b:32 * b + 32], cmp_v_s[0:NC_S, bs_, :],
                                               start=True, stop=True, tile_position=(0, 32 * b))
                        continue
                    for n in range(NPG):
                        if br == "fox":
                            v = fox_cache[:, b * NPG + n, GW:2 * GW]
                        elif br == "sel":
                            v = nsa_cache[:, bs_ * NPG + n, 3 * DH:4 * DH]
                        else:
                            v = win_cache[:, bs_, n, DH:2 * DH]
                        ins = nc.tensor.matmul(Ob, PTs[:, n, 32 * b:32 * b + 32], v, start=False, stop=(n == NPG - 1),
                                               skip_group_check=True, tile_position=(0, 32 * b))
                ins.then_inc(so_ready, 1)

            k = 0
            for u, (br, g) in enumerate(sjobs):
                mine = [i for i, x in enumerate(units) if x[0] == u]
                if br == "cmp":
                    cmp_sample_scores(u)
                else:
                    if u == 0:
                        pe.wait_ge(s_setup, 2)
                    turn_keys(mine[0])
                    new_scores(u)
                    for i in mine:
                        if i + 1 in mine:
                            turn_keys(i + 1)
                        score_keys(i)
                    if br == "win":
                        nc.tensor.matmul(psum[2 * (u % 2)][:, 0:TN], spread_bf[:, g, :], left_m[:],
                                         start=False, stop=True, skip_group_check=True)
                    nc.tensor.matmul(psum[2 * (u % 2) + 1][:, 0:NS], spread_bf[:, g, :], new_m[:],
                                     start=False, stop=True, skip_group_check=True).then_inc(ss_ready, 1)
                if u >= 1:
                    turn_sample_p(u - 1)
                    sample_p_times_v(u - 1)
            turn_sample_p(len(sjobs) - 1)
            sample_p_times_v(len(sjobs) - 1)
            pe.wait_ge(om_ready, 2)
            pe.wait_ge(so_done, len(sjobs))
            for i in range(2):
                for g in range(2):
                    ins = nc.tensor.matmul(psum[i][0:NS, 0:GW], gather[:, g, :], o_m[:, 2 * i + g, :],
                                           start=(g == 0), stop=(g == 1))
            ins.then_inc(ys_ready, 1)

            def logits(t):
                n = rows_of[t]
                if t == 0:
                    pe.wait_ge(router_in, 16)
                pe.wait_ge(x1T_dve, t + 1)
                pe.wait_ge(x1T_act, t + 1)
                for k in range(KD):
                    ins = nc.tensor.matmul(psum[5][0:n, 2 * P + t * NE:2 * P + (t + 1) * NE], x1T[:, k, tok0(t):tok0(t) + n],
                                           w_r[:, k, :], start=(k == 0), stop=(k == KD - 1))
                if t == TILES - 1:
                    ins.then_inc(logits_done, 1)

            def turn_mix(t):
                n = rows_of[t]
                if t == 0:
                    pe.wait_ge(kt_act, len(units) // 2)
                    pe.wait_ge(kt_dve, len(units) // 2)
                else:
                    pe.wait_ge(mix_dve, t)
                    pe.wait_ge(mix_act, t)
                if t == NT:
                    pe.wait_ge(ys_copied, 1)
                if t >= 4:
                    logits(t - 4)
                srcs = [uv[0:n, t, i * P:(i + 1) * P] for i in range(4)] + [fox_v[0:n, t, i * P:(i + 1) * P] for i in range(2)]
                for k, src in enumerate(srcs):
                    ins = nc.tensor.transpose(psum[4 + k // 4][:, (k % 4) * P:(k % 4) * P + n], src, ident[0:n, 0:n])
                ins.then_inc(mix_turned, 1)

            def mix_out(t):
                n = rows_of[t]
                if t == 0:
                    pe.wait_ge(wo_in, 16)
                    pe.wait_ge(ys_copied, 1)
                pe.wait_ge(mix_dve, t + 1)
                pe.wait_ge(mix_act, t + 1)
                if t >= 2:
                    pe.wait_ge(std_ready, t - 1)
                for i in range(2):
                    for k in range(KD):
                        lhs = mix_T[:, t % 2, k, 0:n] if k < 6 else yd_T[:, k - 6, tok0(t):tok0(t) + n]
                        ins = nc.tensor.matmul(psum[2 * (t % 2) + i][0:n, :], lhs, wo[:, k, i * 512:(i + 1) * 512],
                                               start=(k == 0), stop=(k == KD - 1))
                ins.then_inc(r_done, 1)

            def turn_x1(t):
                n = rows_of[t]
                pe.wait_ge(normed, t + 1)
                if t:
                    pe.wait_ge(x1T_dve, t)
                    pe.wait_ge(x1T_act, t)
                for k in range(KD):
                    ins = nc.tensor.transpose(psum[6 + k // 4][:, (k % 4) * P:(k % 4) * P + n],
                                              layer[0:n, t, k * P:(k + 1) * P], ident[0:n, 0:n])
                ins.then_inc(x1_turned, 1)

            turn_mix(0)
            for t in range(TILES):
                if t + 1 < TILES:
                    turn_mix(t + 1)
                mix_out(t)
                if t >= 1:
                    turn_x1(t - 1)
            pe.wait_ge(mix_act, TILES)
            for t in range(TILES - 4, TILES - 1):
                logits(t)
            turn_x1(TILES - 1)
            logits(TILES - 1)

            pe.wait_ge(picked_ready, 1)
            nc.tensor.matmul(psum[5][:, 0:(TILES + 1) * NE], tri_u[:], picked[:].rearrange("p t e -> p (t e)"),
                             start=True, stop=False)
            for t in range(TILES):
                ins = nc.tensor.matmul(psum[5][:, (t + 1) * NE:(TILES + 1) * NE].rearrange("p (t e) -> p t e", e=NE), ones[:],
                                       picked[:, t:t + 1, :].to_broadcast([P, TILES - t, NE]),
                                       start=False, stop=(t == TILES - 1))
            ins.then_inc(ranked, 1)
            pe.wait_ge(hots_ready, 1)
            for j in range(TOP_K * TILES):
                ins = nc.tensor.matmul(psum[6][:, 0:2 * NSL], lo_hot[:, j, :], slot_vals[:, j, :],
                                       start=(j == 0), stop=(j == TOP_K * TILES - 1))
                if j == 0:
                    ins.then_inc(down_done, 1)
            ins.then_inc(slots_done, 1)

            def turn_slots(p, k0, k1):
                for k in range(k0, k1):
                    ins = nc.tensor.transpose(psum[4 + k // 4][:, (k % 4) * P:(k % 4 + 1) * P],
                                              x_slot[:, p, k * P:(k + 1) * P], ident[:])
                    if k % 4 == 3:
                        ins.then_inc(xs_turned, 1)

            pe.wait_ge(slots_ready, 1)
            pairs = pairs_of(pe)
            pe.wait_ge(xs_in[0], 16)
            turn_slots(0, 0, 8)
            with pe.Fori(0, pairs) as pair:
                for p in range(2):
                    t1 = pair * 2 + (p + 1)
                    e = pe.value_load(table[0:1, bass.ds(pair * 2 + p, 1)], min_val=0, max_val=NE - 1)
                    e1 = pe.value_load(table[0:1, bass.ds(pair * 2 + (T_E1 + p), 1)], min_val=1, max_val=NE - 1)
                    w_at = (e % 2) * (R_EW[1] - R_EW[0]) + R_EW[0]
                    pe.wait_ge(ew_in[0], (e // 2) * 48 + 48)
                    pe.wait_ge(ew_in[1], ((e1 + 1) // 2) * 48)
                    pe.wait_ge(xs_dve, t1)
                    pe.wait_ge(xs_act, t1)
                    for k in range(KD):
                        ins = nc.tensor.matmul(psum[p][:], xT_slot[:, p, k, :], arena[:, bass.ds(w_at + k * 2 * F, 2 * F)],
                                               start=(k == 0), stop=(k == KD - 1))
                    ins.then_inc(hid_done, 1)
                    pe.wait_ge(xs_in[1 - p], pair * 16 + 16 * (p + 1))
                    turn_slots(1 - p, 0, 6)
                    pe.wait_ge(h_ready, t1)
                    for f in range(F // P):
                        ins = nc.tensor.transpose(psum[6][:, f * P:(f + 1) * P], h_row[:, f * P:(f + 1) * P], ident[:])
                    ins.then_inc(h_turned, 1)
                    turn_slots(1 - p, 6, 8)
                    pe.wait_ge(hT_ready, t1)
                    for half in range(2):
                        for f in range(F // P):
                            ins = nc.tensor.matmul(psum[2 + half][:], h_T[:, f, :],
                                                   arena[:, bass.ds(w_at + (KD * 2 * F + f * D + half * 512), 512)],
                                                   start=(f == 0), stop=(f == F // P - 1))
                    ins.then_inc(down_done, 1)

        @block.vector
        def _(dve):
            steps = [0]

            def link(ins):
                steps[0] += 1
                ins.then_inc(dve_step, 1)
                dve.wait_ge(dve_step, steps[0])

            nc.vector.memset(lnc[:, 0:1], LN_EPS).then_inc(var_ready, 1)
            nc.vector.memset(lnc[:, 1:2], 1.0)
            nc.vector.memset(foxT_q[DH:DH + 2, :, :], 1.0)
            nc.vector.memset(foxT_k[DH:DH + 2, :, :], 1.0)
            nc.vector.memset(foxS_q[:], 0.0)
            nc.vector.memset(ln_stat[:], 1.0)
            nc.vector.memset(b_f[:], 0.0)
            nc.vector.memset(nsa_rows[NS:P, NT, :], 0.0)

            def center_v(t):
                n = rows_of[t]
                dve.wait_ge(proj_copied, t + 1)
                v = uv[0:n, t, GW:2 * GW].rearrange("p (h d) -> p h d", h=H)
                sq = ln_sq[0:n, :].rearrange("p (h d) -> p h d", h=H)
                m = ln_stat[0:n, t, :, 0]
                link(nc.vector.tensor_reduce(m, v, AX.X, ALU.add))
                link(nc.vector.tensor_scalar(m, m, 1.0 / DH, None, ALU.mult))
                link(nc.vector.tensor_tensor(v, v, m.unsqueeze(2).to_broadcast([n, H, DH]), ALU.subtract))
                link(nc.vector.tensor_tensor(sq, v, v, ALU.mult))
                link(nc.vector.tensor_reduce(ln_stat[0:n, t, :, 1], sq, AX.X, ALU.add))
                nc.vector.tensor_scalar(ln_stat[0:n, t, :, 1], ln_stat[0:n, t, :, 1], 1.0 / DH, None,
                                        ALU.mult).then_inc(var_ready, 1)

            def scale_v(t):
                n = rows_of[t]
                v = uv[0:n, t, GW:2 * GW].rearrange("p (h d) -> p h d", h=H)
                r = ln_stat[0:n, t, :, 1]
                nc.vector.tensor_tensor(v, v, r.unsqueeze(2).to_broadcast([n, H, DH]), ALU.mult).then_inc(v_ready, 1)

            def copy_x(t):
                n = rows_of[t]
                dve.wait_ge(turned, t + 1)
                for i in range(2):
                    ins = nc.vector.tensor_copy(
                        xT[:, 4 * i:4 * i + 4, tok0(t):tok0(t) + n],
                        psum[4 + 2 * (t % 2) + i][:].rearrange("p (k n) -> p k n", k=4)[:, :, 0:n])
                ins.then_inc(turn_copied, 1)

            def copy_turned(g, t):
                e = {1: 1, 3: 2, 4: 3}[g] * TILES + t
                A, B = psum[4 + 2 * (e % 2)], psum[5 + 2 * (e % 2)]
                dve.wait_ge(turned, e + 1)
                ts = slice(tok0(t), tok0(t) + rows_of[t])
                av = A[0:DH, :].rearrange("p (h n) -> p h n", h=H)
                if g == 1 and t < NT:
                    nc.vector.tensor_scalar(foxT_q[0:DH, :, ts], av, SCALE, None, ALU.mult)
                    ins = nc.vector.tensor_copy(foxT_k[0:DH, :, ts], B[0:DH, :].rearrange("p (h n) -> p h n", h=H))
                elif g == 1:
                    for pair in range(2):
                        for i in range(2):
                            q = slice(DH * i, DH * i + DH)
                            nc.vector.tensor_scalar(foxS_q[q, pair, :, 2 * pair + i, :],
                                                    A[q, pair * P:pair * P + NS].rearrange("p (b t) -> p b t", b=NB),
                                                    SCALE, None, ALU.mult)
                    ins = nc.vector.tensor_copy(foxS_k[:], B[:, 0:2 * P].rearrange("p (i n) -> p i n", i=2)[:, :, 0:NS])
                elif g == 3 and t < NT:
                    ins = nc.vector.tensor_scalar(nsaT_q[:, :, ts], av, SCALE, None, ALU.mult)
                elif g == 3:
                    ins = nc.vector.tensor_scalar(nsaS_q[:].rearrange("p b h t -> p h b t"),
                                                  av[:, :, 0:NS].rearrange("p h (b t) -> p h b t", b=NB),
                                                  SCALE, None, ALU.mult)
                else:
                    nc.vector.tensor_copy(selT_k[:, ts], A[0:DH, 0:rows_of[t]])
                    ins = nc.vector.tensor_copy(winT_k[:, ts], A[0:DH, P:P + rows_of[t]])
                ins.then_inc(turn_copied, 1)

            def gate_u(t):
                n = rows_of[t]
                i = 0 if t < NT else 1
                dve.wait_ge(zg_done, t + 1)
                if t:
                    dve.wait_ge(zg_used, t)
                z = psum[4 + t % 2][0:n, 0:GW].rearrange("p (h d) -> p h d", h=H)
                b = bs[0:n, i, :].unsqueeze(2).to_broadcast([n, H, DH])
                sq = ln_sq[0:n, :].rearrange("p (h d) -> p h d", h=H)
                link(nc.vector.tensor_tensor(sq, z, b, ALU.add))
                u = uv[0:n, t, 0:GW]
                nc.vector.tensor_tensor(u, u, ln_sq[0:n, :], ALU.mult).then_inc(zg_used, 1)

            for t in range(TILES):
                copy_x(t)
                if t >= 2:
                    center_v(t - 2)
            dve.wait_ge(ws_turned, 1)
            nc.vector.tensor_copy(ws_T[:], psum[6][:].rearrange("p (h n) -> p h n", h=H)).then_inc(ws_copied, 1)
            center_v(TILES - 2)
            center_v(TILES - 1)
            copy_turned(1, 0)
            dve.wait_ge(rstd_ready, 1)
            dve.wait_ge(small_loaded, 16 * (1 + NB + 1 + 2 + 2 * NB))
            for t in range(TILES):
                scale_v(t)
                if t + 1 < TILES:
                    copy_turned(1, t + 1)
            for t in range(TILES):
                gate_u(t)
            for t in range(TILES):
                if t == 1:
                    dve.wait_ge(proj_copied, 3 * TILES)
                    nc.vector.tensor_tensor(lf_x[:], b_f[:], bias_f[:].unsqueeze(2).to_broadcast([P, H, TILES]),
                                            ALU.add).then_inc(x_biased, 1)
                if t == 3:
                    dve.wait_ge(lf_parts, 3)
                    dve.wait_ge(x_biased, 1)
                    nc.vector.scalar_tensor_tensor(out=lf[:], in0=lf_x[:], scalar=0.0, in1=lf_e[:],
                                                   op0=ALU.min, op1=ALU.subtract).then_inc(lf_ready, 1)
                    dve.wait_ge(lf_ready, 1)
                    nc.vector.tensor_copy(lf_rows[:].rearrange("p t h -> p h t"), lf[:]).then_inc(lf_ready, 1)
                if t == TILES - 1:
                    link(nc.vector.memset(carry[:, :, 0], 0.0))
                    dve.wait_ge(cum_done, 1)
                    tot = psum[5][:, 64:64 + H * NT].rearrange("p (h t) -> p h t", h=H)
                    for i in range(1, NT):
                        link(nc.vector.tensor_tensor(carry[:, :, i], carry[:, :, i - 1], tot[:, :, i - 1], ALU.add))
                    nc.vector.tensor_tensor(cum[:], psum[5][:, 0:H * NT].rearrange("p (h t) -> p h t", h=H),
                                            carry[:], ALU.add).then_inc(c_ready, 1)
                copy_turned(3, t)
            for t in range(TILES):
                copy_turned(4, t)
                if t == 0:
                    dve.wait_ge(cT_done, 1)
                    nc.vector.tensor_copy(cum_T[:, 0, :], psum[7][0:H * NT, 0:P])
                    nc.vector.tensor_scalar(cum_T[:, 1, :], psum[7][0:H * NT, 0:P], -1.0, None,
                                            ALU.mult).then_inc(cT_copied, 1)
            gv = gates[:].rearrange("p t b h -> p (t b h)")
            dve.wait_ge(gate_x, 1)
            link(nc.vector.tensor_scalar(gv, gv, 1.0, None, ALU.add))
            nc.vector.reciprocal(gv, gv).then_inc(gates_ready, 1)
            dve.wait_ge(turned, 3 * TILES)
            dve.wait_ge(k_stored[0], 16 * ((TILES + 1) // 2))
            dve.wait_ge(k_stored[1], 16 * (TILES // 2))
            link(nc.vector.memset(z_p[:, :, 0:2], 0.0))
            for f in range(2):
                j0 = N_ROWJ + 9 * f
                for c, (c0, cn) in enumerate(CHUNKS):
                    dve.wait_ge(proj_copied, N_ROWJ + 3 * f + c + 1)
                    dve.wait_ge(proj_done, j0 + 4 + c)
                    src = psum[(j0 + 3 + c) % 4][:, 0:cn]
                    dh = dh_T[c]
                    if c0 < SEQ:
                        dst = z_p[:, f, 2 + c0:2 + c0 + cn]
                    else:
                        dst = z_s[:, f, :, 2:2 + TN]
                        src = src.rearrange("p (b t) -> p b t", b=NB)
                        dh = dh.rearrange("p (b t) -> p b t", b=NB)
                    ins = nc.vector.tensor_tensor(dst, src, dh, ALU.mult)
                    ins.then_inc(z_used, 1)
                dve.wait_ge(z_used, 6 * f + 3)
                for c, (c0, cn) in enumerate(CHUNKS):
                    dve.wait_ge(proj_done, j0 + 7 + c)
                    dve.wait_ge(z_used, 6 * f + 3 + c)
                    if c0 < SEQ:
                        sh = [z_p[:, f, c0 + i:c0 + i + cn] for i in range(3)]
                        y, out = conv_y[:, 0:cn], yd_T[:, f, c0:c0 + cn]
                        ps = psum[(j0 + 6 + c) % 4][:, 0:cn]
                    else:
                        sh = [z_s[:, f, :, i:i + TN] for i in range(3)]
                        y, out, ps = [a.rearrange("p (b t) -> p b t", b=NB) for a in (
                            conv_y[:, 0:cn], yd_T[:, f, c0:c0 + cn], psum[(j0 + 6 + c) % 4][:, 0:cn])]
                    link(nc.vector.tensor_scalar(y, sh[0], cw[:, f, 0:1], None, ALU.mult))
                    link(nc.vector.scalar_tensor_tensor(out=y, in0=sh[1], scalar=cw[:, f, 1:2], in1=y,
                                                        op0=ALU.mult, op1=ALU.add))
                    link(nc.vector.scalar_tensor_tensor(out=y, in0=sh[2], scalar=cw[:, f, 2:3], in1=y,
                                                        op0=ALU.mult, op1=ALU.add))
                    nc.vector.tensor_tensor(out, ps, y, ALU.mult).then_inc(z_used, 1)
                dve.wait_ge(z_used, 6 * f + 6)

            dve.wait_ge(gates_ready, 1)

            def row_max(i):
                n = keys_of(i)[1]
                dve.wait_ge(s_ready, i + 1)
                if i >= 4:
                    dve.wait_ge(p_ready, i - 3)
                nc.vector.tensor_reduce(neg_max[:, i % 4:i % 4 + 1], banks(2 * (i % 2), 2)[:, 0:n * P], AX.X,
                                        ALU.max, negate=True).then_inc(max_ready, 1)

            def copy_pt_dve(i):
                n = min(4, keys_of(i)[1])
                dve.wait_ge(p_turned, i + 1)
                if i >= 2:
                    dve.wait_ge(o_ready, i - 1)
                nc.vector.tensor_copy(PT_buf[:, i % 2, 0:n * P], psum[4][:, 0:n * P]).then_inc(pt_dve, 1)

            def finish(i):
                br, qt, h = jobs[i]
                dve.wait_ge(o_ready, i + 1)
                s = slice(i % 4, i % 4 + 1)
                link(nc.vector.reciprocal(recip[:, s], row_sum[:, s]))
                O = psum[6 + i % 2][:, 0:DH]
                if br == "fox":
                    ins = nc.vector.tensor_scalar(uv[:, qt, GW + h * DH:GW + (h + 1) * DH], O, recip[:, s], None, ALU.mult)
                else:
                    b = 1 if br == "sel" else 2
                    link(nc.vector.tensor_tensor(coef[:, s], recip[:, s], gates[:, qt, b, h:h + 1], ALU.mult))
                    y = fox_v[:, qt, h * DH:(h + 1) * DH]
                    if br == "sel":
                        ins = nc.vector.tensor_scalar(y, O, coef[:, s], None, ALU.mult)
                    else:
                        ins = nc.vector.scalar_tensor_tensor(out=y, in0=O, scalar=coef[:, s], in1=y,
                                                             op0=ALU.mult, op1=ALU.add)
                ins.then_inc(y_done, 1)

            for i in range(J + 2):
                if i < J:
                    row_max(i)
                if 1 <= i <= J:
                    copy_pt_dve(i - 1)
                if i >= 2:
                    finish(i - 2)

            dve.wait_ge(pe_turned, 1)
            nc.vector.tensor_copy(kcvc_T[:, :, NU:NU + 2], psum[6][:, 0:CMP_LEN].rearrange("p (o r) -> p r o", r=UNIT)
                                  ).then_inc(pe_copied, 1)
            for q in range(0, 2 + NB, 2):
                dve.wait_ge(cc_turned, q + 1)
                copy_units(nc.vector.tensor_copy, q).then_inc(cc_dve, 1)

            def by_head(v):
                return v.unsqueeze(2)

            def cmp_shift(qt):
                dve.wait_ge(c_scored, qt + 1)
                if qt >= 2:
                    dve.wait_ge(c_turned, qt - 1)
                S = psum[2 + qt % 2][:, 0:H * NC_P].rearrange("p (h n) -> p h n", h=H)
                m = head_v[:, 0, :]
                if qt:
                    dve.wait_ge(c_shifted, qt)
                link(nc.vector.tensor_reduce(m, S, AX.X, ALU.max, negate=True))
                nc.vector.tensor_tensor(P_buf[:, qt % 2, 0:H * NC_P].rearrange("p (h n) -> p h n", h=H), S,
                                        by_head(m).to_broadcast([P, H, NC_P]), ALU.add).then_inc(c_shifted, 1)

            def cmp_sum(qt):
                dve.wait_ge(c_exp, qt + 1)
                if qt >= 2:
                    dve.wait_ge(c_added, qt - 1)
                s, r = head_v[:, 1, :], head_v[:, 2 + qt % 2, :]
                link(nc.vector.tensor_reduce(s, P_buf[:, qt % 2, 0:H * NC_P].rearrange("p (h n) -> p h n", h=H), AX.X, ALU.add))
                link(nc.vector.reciprocal(s, s))
                link(nc.vector.tensor_tensor(r, s, gates[:, qt, 0, :], ALU.mult))
                if qt == 0:
                    link(nc.vector.tensor_scalar(r, r, any_cmp[:, 0:1], None, ALU.mult))

            def cmp_add(qt):
                dve.wait_ge(c_out, qt + 1)
                if qt:
                    dve.wait_ge(c_added, qt)
                t = P_buf[:, 0, 512:512 + GW]
                O = psum[6 + qt % 2][:, 0:GW].rearrange("p (h d) -> p h d", h=H)
                link(nc.vector.tensor_tensor(t.rearrange("p (h d) -> p h d", h=H), O,
                                             by_head(head_v[:, 2 + qt % 2, :]).to_broadcast([P, H, DH]), ALU.mult))
                nc.vector.tensor_tensor(fox_v[:, qt, :], fox_v[:, qt, :], t, ALU.add).then_inc(c_added, 1)

            dve.wait_ge(masks_ready, 11)
            for qt in range(NT + 2):
                if qt < NT:
                    cmp_shift(qt)
                if 1 <= qt <= NT:
                    cmp_sum(qt - 1)
                if qt >= 2:
                    cmp_add(qt - 2)

            nc.vector.tensor_scalar(new_m[:], same[:], -NEG, NEG, ALU.mult, ALU.add)
            link(nc.vector.tensor_reduce(left_f[:], same[:].rearrange("p (b t) -> p t b", b=NB), AX.X, ALU.add))
            nc.vector.tensor_scalar(left_m[:], left_f[:], NEG, None, ALU.mult)
            nc.vector.tensor_copy(spread_bf[:], spread[:])
            link(nc.vector.tensor_reduce(head_m[:], ident[:].rearrange("p (b h t) -> p h b t", b=4, h=H), AX.XY, ALU.add))
            dve.wait_ge(lf_ready, 2)
            for g in range(2):
                v = lf_new[:, g, :].rearrange("p (b h t) -> p b h t", b=4, h=H)
                for b in range(4):
                    nc.vector.tensor_tensor(v[:, b], v[:, b], lf[0:NS, :, NT:NT + 1].to_broadcast([NS, H, TN]), ALU.mult)
            dve.wait_ge(lf_past_in, 16 * NB * NPG)
            dve.wait_ge(conv_stored, 16 * 2 * (1 + NB))
            for g in range(2):
                for n in range(NPG):
                    for b in range(4):
                        nc.vector.tensor_copy(
                            lf_rep[:, g, n, 32 * b:32 * b + 32].rearrange("p (h t) -> p h t", h=H),
                            lf_past[:, (4 * g + b) * NPG + n, :].unsqueeze(2).to_broadcast([P, H, TN]))
            dve.wait_ge(s_ops, 1)
            link(nc.vector.tensor_copy(gather[:], psum[6][:, 0:2 * NS].rearrange("p (g n) -> p g n", g=2)))
            for g in range(2):
                link(nc.vector.tensor_tensor(gate_t[:], psum[7][:, 16 * g:16 * g + 12].rearrange("p (b h) -> p b h", b=3),
                                             head_m[:].unsqueeze(1).to_broadcast([P, 3, H]), ALU.mult))
                nc.vector.tensor_reduce(gate_s[:, g, :], gate_t[:], AX.X, ALU.add).then_inc(s_setup, 1)
                dve.wait_ge(s_setup, g + 1)

            def sample_finish(u):
                br, g = sjobs[u]
                dve.wait_ge(so_ready, u + 1)
                st = s_stat[:, u % 2, :]
                link(nc.vector.reciprocal(st[:, 2:3], st[:, 1:2]))
                if br == "fox":
                    c = o_coef[:, g, :]
                    link(nc.vector.tensor_scalar(c, head_m[:], st[:, 2:3], None, ALU.mult))
                    nc.vector.tensor_tensor(o_m[:, g, :].rearrange("p (h d) -> p h d", h=H),
                                            psum[7][:, 256:512].rearrange("p (h d) -> p h d", h=H),
                                            c.unsqueeze(2).to_broadcast([P, H, DH]), ALU.mult).then_inc(so_done, 1)
                    return
                i = {"cmp": 0, "sel": 1, "win": 2}[br]
                link(nc.vector.tensor_tensor(st[:, 3:4], st[:, 2:3], gate_s[:, g, i:i + 1], ALU.mult))
                O, y = psum[7][:, 256:256 + DH], o_nsa[:, g, :]
                if br == "sel":
                    nc.vector.tensor_scalar(y, O, st[:, 3:4], None, ALU.mult).then_inc(so_done, 1)
                else:
                    nc.vector.scalar_tensor_tensor(out=y, in0=O, scalar=st[:, 3:4], in1=y, op0=ALU.mult, op1=ALU.add
                                                   ).then_inc(so_done, 1)
                dve.wait_ge(so_done, u + 1)
                if br == "cmp":
                    nc.vector.tensor_tensor(o_m[:, 2 + g, :].rearrange("p (h d) -> p h d", h=H),
                                            y.unsqueeze(1).to_broadcast([P, H, DH]),
                                            head_m[:].unsqueeze(2).to_broadcast([P, H, DH]), ALU.mult
                                            ).then_inc(om_ready, 1)

            def copy_sample_pt(u):
                dve.wait_ge(sp_turned, u + 1)
                if u >= 1:
                    dve.wait_ge(so_ready, u)
                if sjobs[u][0] == "cmp":
                    nc.vector.tensor_copy(PTs[0:NC_S, 0, :], psum[6][0:NC_S, 0:P]).then_inc(spt_ready, 1)
                else:
                    nc.vector.tensor_copy(PTs[:, 0:NPG, :], psum[6][:].rearrange("p (n k) -> p n k", n=NPG))
                    nc.vector.tensor_copy(PTs[0:NS, NPG, :], psum[7][0:NS, 0:P]).then_inc(spt_ready, 1)

            k = 0
            for u, (br, g) in enumerate(sjobs):
                while k < len(units) and units[k][0] == u:
                    if k % 2 == 0:
                        copy_keys(dve, nc.vector.tensor_copy, k).then_inc(kt_dve, 1)
                    k += 1
                dve.wait_ge(ss_ready, u + 1)
                if u >= 2:
                    dve.wait_ge(sp_ready, u - 1)
                w = NC_S if br == "cmp" else SW
                nc.vector.tensor_reduce(s_stat[:, u % 2, 0:1], banks(2 * (u % 2), 2)[:, 0:w], AX.X, ALU.max, negate=True
                                        ).then_inc(smax_ready, 1)
                if u >= 1:
                    copy_sample_pt(u - 1)
                    sample_finish(u - 1)
            copy_sample_pt(len(sjobs) - 1)
            sample_finish(len(sjobs) - 1)
            dve.wait_ge(ys_ready, 1)
            nc.vector.tensor_copy(uv[0:NS, NT, GW:2 * GW], psum[0][0:NS, 0:GW])
            nc.vector.tensor_copy(fox_v[0:NS, NT, :], psum[1][0:NS, 0:GW]).then_inc(ys_copied, 1)

            def add_residual(t):
                n = rows_of[t]
                dve.wait_ge(r_done, t + 1)
                dve.wait_ge(x_res_in[t % 2], 16 * (t // 2 + 1))
                st = ln_s[0:n, t % 2, :]
                if t >= 2:
                    dve.wait_ge(normed, t - 1)
                link(nc.vector.scalar_tensor_tensor(out=layer[0:n, t, :], in0=x_res[0:n, t % 2, :], scalar=ALPHA,
                                                    in1=banks(2 * (t % 2), 2)[0:n, :], op0=ALU.mult, op1=ALU.add,
                                                    accum_out=st[:, 0:1]))
                nc.vector.tensor_scalar(st[:, 1:2], st[:, 0:1], -1.0 / D, None, ALU.mult).then_inc(mean_ready, 1)

            def norm(i, t):
                n, m = rows_of[t], TILES * i + t
                st, v = ln_s[0:n, m % 2, :], layer[0:n, t, :]
                dve.wait_ge(std_ready, m + 1)
                link(nc.vector.reciprocal(st[:, 3:4], st[:, 2:3]))
                if t == 0:
                    dve.wait_ge(ln_in, 32 * (i + 1))
                link(nc.vector.scalar_tensor_tensor(out=v, in0=v, scalar=st[:, 1:2], in1=ln_row[i][0:n, 0, :],
                                                    op0=ALU.add, op1=ALU.mult))
                nc.vector.scalar_tensor_tensor(out=v, in0=v, scalar=st[:, 3:4], in1=ln_row[i][0:n, 1, :],
                                               op0=ALU.mult, op1=ALU.add).then_inc(normed, 1)

            def copy_mix(t):
                n = rows_of[t]
                dve.wait_ge(mix_turned, t + 1)
                if t >= 2:
                    dve.wait_ge(r_done, t - 1)
                nc.vector.tensor_copy(mix_T[:, t % 2, 0:4, 0:n], psum[4][:].rearrange("p (k n) -> p k n", k=4)[:, :, 0:n]
                                      ).then_inc(mix_dve, 1)

            def copy_x1T(t):
                n = rows_of[t]
                dve.wait_ge(x1_turned, t + 1)
                nc.vector.tensor_copy(x1T[:, 4:8, tok0(t):tok0(t) + n],
                                      psum[7][:].rearrange("p (k n) -> p k n", k=4)[:, :, 0:n]).then_inc(x1T_dve, 1)

            copy_mix(0)
            for t in range(TILES):
                if t + 1 < TILES:
                    copy_mix(t + 1)
                add_residual(t)
                norm(0, t)
                if t:
                    copy_x1T(t - 1)
            copy_x1T(TILES - 1)

            V = nc.vector
            full = [P, TILES, NE]
            t16 = lambda v: v.unsqueeze(2).to_broadcast(full)
            g44 = lambda v: v.rearrange("p t (g e) -> p (t g) e", g=EG)
            f4 = lambda v: v[:].rearrange("p t g -> p (t g)")
            in_group = lambda v: f4(v).unsqueeze(2).to_broadcast([P, TILES * EG, EG])
            dve.wait_ge(logits_done, 1)
            dve.wait_ge(masks_ready, 13)
            link(V.tensor_copy(iota_f[:], iota_i[:]))
            link(V.tensor_copy(tok_f[:], tok_i[:]))
            link(V.tensor_scalar(rank16[:], iota_f[:, 0:NE], -1.0, float(NE), ALU.mult, ALU.add))
            link(V.tensor_scalar(iota_p[:], iota_f[:, 0:NSL + 1], float(P), None, ALU.mult))
            link(V.tensor_tensor(le16[:], iota_f[:, 0:NE].unsqueeze(1).to_broadcast([P, NE, NE]),
                                 iota_f[:, 0:NE].unsqueeze(2).to_broadcast([P, NE, NE]), ALU.is_le))
            link(V.memset(picked[:, TILES, :], 0.0))
            link(V.memset(probs[:], 0.0))
            link(V.tensor_copy(probs[:, 0:NT, :], psum[5][:, 2 * P:2 * P + NT * NE].rearrange("p (t e) -> p t e", t=NT)))
            link(V.tensor_copy(probs[0:NS, NT, :], psum[5][0:NS, 2 * P + NT * NE:2 * P + TILES * NE]))
            link(V.tensor_reduce(r1[0][:], probs[:], AX.X, ALU.max, negate=True))
            V.tensor_tensor(probs[:], probs[:], t16(r1[0][:]), ALU.add).then_inc(rmax_ready, 1)
            dve.wait_ge(rexp_ready, 1)
            link(V.tensor_reduce(r1[0][:], probs[:], AX.X, ALU.add))
            link(V.reciprocal(r1[0][:], r1[0][:]))
            link(V.tensor_tensor(probs[:], probs[:], t16(r1[0][:]), ALU.mult))
            m1, cnt, m2, sel = r4
            link(V.tensor_reduce(f4(m1), g44(probs[:]), AX.X, ALU.max))
            link(V.tensor_tensor(g44(r16[0][:]), g44(probs[:]), in_group(m1), ALU.is_equal))
            link(V.tensor_reduce(f4(cnt), g44(r16[0][:]), AX.X, ALU.add))
            link(V.tensor_scalar(r16[1][:], r16[0][:], -2.0, None, ALU.mult))
            link(V.tensor_tensor(r16[1][:], r16[1][:], probs[:], ALU.add))
            link(V.tensor_reduce(f4(m2), g44(r16[1][:]), AX.X, ALU.max))
            link(V.tensor_scalar(cnt[:], cnt[:], 2.0, None, ALU.is_ge))
            link(V.tensor_tensor(cnt[:], cnt[:], m1[:], ALU.mult))
            link(V.tensor_tensor(m2[:], m2[:], cnt[:], ALU.max))
            link(V.tensor_tensor(m1[:], m1[:], m2[:], ALU.add))
            link(V.tensor_reduce(r1[0][:], m1[:], AX.X, ALU.max))
            t4 = lambda v: v.unsqueeze(2).to_broadcast([P, TILES, EG])
            rank4 = rank16[:, NE - EG:NE].unsqueeze(1).to_broadcast([P, TILES, EG])
            link(V.tensor_tensor(sel[:], m1[:], t4(r1[0][:]), ALU.is_equal))
            link(V.tensor_tensor(sel[:], sel[:], rank4, ALU.mult))
            link(V.tensor_reduce(r1[0][:], sel[:], AX.X, ALU.max))
            link(V.tensor_tensor(sel[:], sel[:], t4(r1[0][:]), ALU.is_equal))
            pm, tmp = r16[0], r16[1]
            link(V.tensor_tensor(g44(pm[:]), g44(probs[:]), in_group(sel), ALU.mult))
            link(V.tensor_scalar(sel[:], sel[:], -1.0, None, ALU.add))
            link(V.tensor_tensor(g44(pm[:]), g44(pm[:]), in_group(sel), ALU.add))
            rank = rank16[:].unsqueeze(1).to_broadcast(full)
            for k in range(TOP_K):
                link(V.tensor_reduce(r1[k][:], pm[:], AX.X, ALU.max))
                link(V.tensor_tensor(tmp[:], pm[:], t16(r1[k][:]), ALU.is_equal))
                link(V.tensor_tensor(tmp[:], tmp[:], rank, ALU.mult))
                link(V.tensor_reduce(r1[2][:], tmp[:], AX.X, ALU.max))
                link(V.tensor_tensor(hot[:, k], tmp[:], t16(r1[2][:]), ALU.is_equal))
                if k == 0:
                    link(V.scalar_tensor_tensor(out=pm[:], in0=hot[:, 0], scalar=-4.0, in1=pm[:], op0=ALU.mult, op1=ALU.add))
            link(V.memset(hot[NS:P, :, NT, :], 0.0))
            V.tensor_tensor(picked[:, 0:TILES, :], hot[:, 0], hot[:, 1], ALU.add).then_inc(picked_ready, 1)
            link(V.tensor_tensor(r1[2][:], r1[0][:], r1[1][:], ALU.add))
            link(V.reciprocal(r1[2][:], r1[2][:]))
            link(V.tensor_tensor(gate2[:, 0], r1[0][:], r1[2][:], ALU.mult))
            link(V.tensor_tensor(gate2[:, 1], r1[1][:], r1[2][:], ALU.mult))

            CH2 = TOP_K * TILES
            dve.wait_ge(ranked, 1)
            counts = psum[5][:, TILES * NE:(TILES + 1) * NE]
            ranks = psum[5][:, 0:TILES * NE].rearrange("p (t e) -> p t e", e=NE)
            link(V.tensor_tensor(over[:], counts.unsqueeze(2).to_broadcast([P, NE, TILES]),
                                 iota_p[:, 0:TILES].unsqueeze(1).to_broadcast([P, NE, TILES]), ALU.is_gt))
            link(V.tensor_reduce(n_tiles[:], over[:], AX.X, ALU.add))
            link(V.tensor_tensor(le16_x[:], le16[:], n_tiles[:].unsqueeze(1).to_broadcast([P, NE, NE]), ALU.mult))
            link(V.tensor_reduce(upto[:], le16_x[:], AX.X, ALU.add))
            link(V.tensor_tensor(n_tiles[:], upto[:], n_tiles[:], ALU.subtract))
            link(V.scalar_tensor_tensor(out=pos16[:], in0=n_tiles[:].unsqueeze(1).to_broadcast(full), scalar=float(P),
                                        in1=ranks, op0=ALU.mult, op1=ALU.add))
            link(V.tensor_tensor(pos_x[:].rearrange("p (k t) e -> p k t e", k=TOP_K), hot[:],
                                 pos16[:].unsqueeze(1).to_broadcast([P, TOP_K, TILES, NE]), ALU.mult))
            link(V.tensor_reduce(pos[:], pos_x[:], AX.X, ALU.add))
            link(V.tensor_tensor(ge_tile[:], pos[:].unsqueeze(2).to_broadcast([P, CH2, NSL + 1]),
                                 iota_p[:].unsqueeze(1).to_broadcast([P, CH2, NSL + 1]), ALU.is_gt))
            link(V.tensor_reduce(hi_cnt[:], ge_tile[:], AX.X, ALU.add))
            link(V.scalar_tensor_tensor(out=lo_pos[:], in0=hi_cnt[:], scalar=-float(P), in1=pos[:],
                                        op0=ALU.mult, op1=ALU.add))
            link(V.tensor_scalar(lo_pos[:], lo_pos[:], float(P - 1), None, ALU.add))
            link(V.tensor_tensor(lo_hot[:], lo_pos[:].unsqueeze(2).to_broadcast([P, CH2, P]),
                                 iota_f[:].unsqueeze(1).to_broadcast([P, CH2, P]), ALU.is_equal))
            link(V.tensor_tensor(hi_hot[:], ge_tile[:, :, 0:NSL], ge_tile[:, :, 1:NSL + 1], ALU.subtract))
            for k in range(TOP_K):
                kt = slice(k * TILES, (k + 1) * TILES)
                V.tensor_tensor(slot_vals[:, kt, 0:NSL], hi_hot[:, kt, :],
                                tok_f[:].unsqueeze(2).to_broadcast([P, TILES, NSL]), ALU.mult)
                ins = V.tensor_tensor(slot_vals[:, kt, NSL:2 * NSL], hi_hot[:, kt, :],
                                      gate2[:, k].unsqueeze(2).to_broadcast([P, TILES, NSL]), ALU.mult)
            ins.then_inc(hots_ready, 1)
            link(V.tensor_scalar(pos[:], pos[:], -1.0, None, ALU.add))
            link(V.tensor_copy(slot_of[:], pos[:]))
            link(V.tensor_tensor(e_cmp[:], upto[0:1, 0:NE - 1].unsqueeze(1).to_broadcast([1, NSL, NE - 1]),
                                 iota_f[0:1, 0:NSL].unsqueeze(2).to_broadcast([1, NSL, NE - 1]), ALU.is_le))
            link(V.tensor_reduce(e_f[:, 0:NSL], e_cmp[:], AX.X, ALU.add))
            link(V.tensor_scalar(e_f[:, T_E1:T_E1 + NSL], e_f[:, 0:NSL], 1.0, None, ALU.max))
            link(V.tensor_copy(e_f[:, T_UPTO:T_UPTO + NE], upto[0:1, :]))
            link(V.tensor_scalar(n_tiles[0:1, :], iota_f[0:1, 0:NE], 2.0, None, ALU.mult))
            link(V.tensor_tensor(n_tiles[0:1, :], upto[0:1, NE - 1:NE].to_broadcast([1, NE]), n_tiles[0:1, :], ALU.is_gt))
            link(V.tensor_reduce(e_f[:, T_PAIRS:T_PAIRS + 1], n_tiles[0:1, :], AX.X, ALU.add))
            link(V.tensor_scalar(e_f[:, T_PAIRS + 1:T_PAIRS + 2], e_f[:, T_PAIRS:T_PAIRS + 1], -1.0, PAIRS_MAX + 1.0,
                                 ALU.mult, ALU.add))
            link(V.tensor_copy(table[:], e_f[:]))
            dve.wait_ge(slots_done, 1)
            link(V.tensor_copy(slot_gate[:], psum[6][:, NSL:2 * NSL]))
            V.tensor_copy(slot_tok[:], psum[6][:, 0:NSL]).then_inc(slots_ready, 1)
            dve.wait_ge(slots_ready, 1)

            def copy_x(n_turned, p):
                dve.wait_ge(xs_turned, n_turned)
                V.tensor_copy(xT_slot[:, p, 0:4, :], psum[4][:].rearrange("p (k n) -> p k n", k=4)).then_inc(xs_dve, 1)

            pairs = pairs_of(dve)
            copy_x(1, 0)

            def slot_pair(pair):
                for p in range(2):
                    t1 = pair * 2 + (p + 1)
                    dve.wait_ge(sil_ready, t1)
                    V.scalar_tensor_tensor(out=h_row[:], in0=psum[p][:, F:2 * F], scalar=slot_gate[:, bass.ds(pair * 2 + p, 1)],
                                           in1=sil[:], op0=ALU.mult, op1=ALU.mult).then_inc(h_ready, 1)
                    copy_x(pair * 4 + (2 * p + 3), 1 - p)
                    dve.wait_ge(h_turned, t1)
                    V.tensor_copy(h_T[:].rearrange("p f n -> p (f n)"), psum[6][:, 0:F]).then_inc(hT_ready, 1)
                    if not isinstance(pair, int):
                        dve.wait_ge(ys_stored[p], pair * 16)
                    dve.wait_ge(down_done, t1 + 1)
                    V.tensor_copy(y_slot[:, p, 0:512], psum[2][:]).then_inc(y_dve, 1)

            slot_pair(0)
            with dve.Fori(1, pairs) as pair:
                slot_pair(pair)

            for t in range(TILES + 1):
                if t < TILES:
                    n, m = rows_of[t], TILES + t
                    st = ln_s[0:n, m % 2, :]
                    if t >= 2:
                        dve.wait_ge(normed, m - 1)
                    v = layer[0:n, t, :]
                    dve.wait_ge(yp_in[t % 3], 32 * (t // 3 + 1))
                    link(V.scalar_tensor_tensor(out=v, in0=v, scalar=ALPHA, in1=y_pair[0:n, t % 3, 0, :],
                                                op0=ALU.mult, op1=ALU.add))
                    link(V.scalar_tensor_tensor(out=v, in0=v, scalar=1.0, in1=y_pair[0:n, t % 3, 1, :],
                                                op0=ALU.mult, op1=ALU.add, accum_out=st[:, 0:1]))
                    nc.vector.tensor_scalar(st[:, 1:2], st[:, 0:1], -1.0 / D, None, ALU.mult).then_inc(mean_ready, 1)
                if t >= 1:
                    norm(1, t - 1)


_INS = ['x_prompt', 'x_sample', 'cache_fox_kv', 'cache_fox_logf', 'cache_nsa_kv', 'state_nsa_win', 'state_conv',
        'page_table', 'w_in', 'fox_b_f', 'gmlp_w_s', 'gmlp_b_s', 'nsa_cmp_pe', 'nsa_cmp_w1', 'nsa_cmp_w2', 'conv_w',
        'w_out', 'ln_g', 'ln_b', 'w_router', 'w_exp_gate', 'w_exp_up', 'w_exp_down']

_OUTS = [(1, 1024, 1024), (8, 8, 1024), (1, 1, 1024, 2, 4, 64), (1, 8, 8, 2, 4, 64), (1, 1, 1024, 4), (1, 8, 8, 4),
         (1, 1, 1024, 4, 64), (1, 8, 8, 4, 64), (1, 1, 512, 2, 64), (1, 8, 512, 2, 64), (1, 1, 2, 256), (1, 8, 2, 256),
         (1, 8, 8, 4, 64)]


def kernel(**inputs):
    import numpy as np
    import concourse.bacc as bacc
    from concourse.bass_utils import run_bass_kernel_spmd as run

    nc = bacc.Bacc("TRN2", target_bir_lowering=False, num_devices=1)
    arrays, args = {}, []
    for name in _INS:
        a = np.ascontiguousarray(inputs[name])
        arrays[f"in_{name}"] = a
        args.append(nc.dram_tensor(f"in_{name}", a.shape, mybir.dt.from_np(a.dtype), kind="ExternalInput").ap())
    for i, shape in enumerate(_OUTS):
        args.append(nc.dram_tensor(f"out_{i}", shape, F32, kind="ExternalOutput").ap())
    build(nc, *args)
    r = run(nc, [arrays], core_ids=[0])
    return tuple(r.results[0][f"out_{i}"] for i in range(len(_OUTS)))
```

```python
from contextlib import ExitStack

import concourse.bass as bass
from concourse import mybir

ALU = mybir.AluOpType
ACT = mybir.ActivationFunctionType
F32 = mybir.dt.float32
BF16 = mybir.dt.bfloat16
I32 = mybir.dt.int32
AX = mybir.AxisListType

P = 128
NEG = -1e30
LN_EPS = 1e-5


def build(nc, x_prompt, x_sample, cache_fox_kv, cache_fox_logf, cache_nsa_kv, state_nsa_win, state_conv,
          page_table, w_in, fox_b_f, gmlp_w_s, gmlp_b_s, nsa_cmp_pe, nsa_cmp_w1, nsa_cmp_w2, conv_w, w_out,
          ln_g, ln_b, w_router, w_exp_gate, w_exp_up, w_exp_down, *outs):
    (y_prompt, y_sample, fox_kv_p, fox_kv_s, fox_lf_p, fox_lf_s, nsa_kv_p, nsa_kv_s, nsa_win_p, nsa_win_s,
     conv_p, conv_s, gmlp_v_s) = outs

    SEQ, D = x_prompt.shape[1], x_prompt.shape[2]
    NB, TN = x_sample.shape[0], x_sample.shape[1]
    H, DH = 4, 64
    GW = H * DH
    KD = D // P
    NT = SEQ // P
    TILES = NT + 1
    NS = NB * TN
    TOK = SEQ + NS
    PAST = state_nsa_win.shape[2]
    PAGE = cache_nsa_kv.shape[2]
    NPG = PAST // PAGE
    NPOOL = cache_nsa_kv.shape[1]
    WINDOW = 512
    SEL_LEN, SEL_TOPK = 64, 16
    assert PAGE == P and NS == 64 and PAST == WINDOW
    assert max(SEQ, PAST + SEL_LEN) <= SEL_LEN * SEL_TOPK
    SCALE = DH ** -0.5
    rows_of = [P] * NT + [NS]

    A_U, A_V, B_Q, B_K, B_V, B_F = 0, GW, 2 * GW, 3 * GW, 4 * GW, 5 * GW
    C_Q = B_F + H
    C_KV = C_Q + GW
    C_G = C_KV + 6 * DH
    D_H = C_G + 3 * H
    D_B, D_C = D_H + GW, D_H + 2 * GW

    ctx = ExitStack()
    with ctx:
        def sb(name, shape, dt=F32):
            return ctx.enter_context(nc.sbuf_tensor(name, shape, dt))

        def sem(name):
            return ctx.enter_context(nc.semaphore(name))

        psum_all = ctx.enter_context(nc.psum_tensor("psum_all", [P, 8, 512], F32))
        psum = [psum_all[:, i, :] for i in range(8)]

        def banks(i, n):
            return psum_all[:, i:i + n, :].rearrange("p i n -> p (i n)")

        arena = sb("arena", [P, 47084])

        def at(off, *dims, part=P):
            n = 1
            for d in dims:
                n *= d
            v = arena[0:part, off:off + n]
            names = " ".join(f"d{i}" for i in range(len(dims)))
            return v.rearrange(f"p ({names}) -> p {names}", **{f"d{i}": d for i, d in enumerate(dims)}) if len(dims) > 1 else v

        R_X = 0
        R_W = R_X + KD * TOK
        R_FOX = R_W + 2 * KD * 512
        R_NQ = R_FOX + 2 * H * SEQ
        R_XR = R_NQ + H * SEQ
        R_UV = R_XR + 2 * D + 2 * 512
        R_FV = R_UV + TILES * 2 * GW
        R_NR = R_FV + TILES * GW
        R_SK = R_NR + TILES * (6 * DH + 12)
        R_YD = R_SK + 2 * TOK

        ident = sb("ident", [P, P])
        ident_bf = sb("ident_bf", [P, P], BF16)
        ones = sb("ones", [P, P])
        tri_u = sb("tri_u", [P, P])

        causal_m = sb("causal_m", [P, P], BF16)
        far_m = sb("far_m", [P, P], BF16)
        zeros_bf = sb("zeros_bf", [P, P], BF16)

        x_rows = at(R_XR, 2, D)
        xT = at(R_X, KD, TOK)
        w_buf = at(R_W, 2, KD * 512)
        uv = at(R_UV, TILES, 2 * GW)
        qk_rows = at(R_XR + 2 * D, 2, 2 * GW)
        foxT_q = at(R_FOX, H, SEQ, part=DH + 2)
        foxT_k = at(R_FOX + H * SEQ, H, SEQ, part=DH + 2)
        nsaT_q = at(R_NQ, H, SEQ, part=DH)
        fox_v = at(R_FV, TILES, GW)
        nsa_rows = at(R_NR, TILES, 6 * DH + 12)
        b_f = sb("b_f", [P, H, TILES])
        selT_k = at(R_SK, TOK, part=DH)
        winT_k = at(R_SK + TOK, TOK, part=DH)
        yd_T = at(R_YD, 2, TOK)

        ws_T = sb("ws_T", [P, H, P])
        ws_rows = qk_rows[:, 0, :].rearrange("p (h s) -> p h s", h=H)
        ws_s = sb("ws_s", [NS, H, NS])
        bs = sb("bs", [P, 2, H])
        ln_stat = sb("ln_stat", [P, TILES, H, 2])
        ln_sq = sb("ln_sq", [P, GW])
        lnc = sb("lnc", [P, 4])
        cw = sb("cw", [P, 2, 3])
        tail_w = R_W + KD * 512 + KD * 3 * P
        conv_y = at(tail_w, 512)
        dh_T = [at(tail_w + 512, 512), at(R_XR + 2 * (2 + SEQ), 512), at(R_XR + 2 * (2 + SEQ) + 512, NS)]
        z_p = at(R_XR, 2, 2 + SEQ)
        z_s = sb("z_s", [P, 2, NB, 2 + TN])

        foxS_q = sb("foxS_q", [P, 2, NB, H, TN])
        foxS_k = sb("foxS_k", [P, 2, NS])
        nsaS_q = sb("nsaS_q", [DH, NB, H, TN])

        bias_f = sb("bias_f", [P, H])
        lf_x = sb("lf_x", [P, H, TILES])
        lf_e = sb("lf_e", [P, H, TILES])
        lf = sb("lf", [P, H, TILES])
        lf_rows = sb("lf_rows", [P, TILES, H])
        carry = sb("carry", [P, H, NT])
        cum = sb("cum", [P, H, NT])
        cum_T = sb("cum_T", [H * NT, 2, P])

        P_buf = at(R_W, 2, SEQ)
        PT_buf = at(R_W + 2 * SEQ, 2, SEQ)
        gates = sb("gates", [P, TILES, 3, H])
        neg_max = sb("neg_max", [P, 4])
        row_sum = sb("row_sum", [P, 4])
        recip = sb("recip", [P, 4])
        coef = sb("coef", [P, 4])
        win_tiles = WINDOW // P
        jobs = [("fox", qt, h) for qt in range(NT) for h in range(H)]
        N_FOX = len(jobs)
        jobs += [(br, qt, h) for qt in range(NT) for h in range(H) for br in ("sel", "win")]
        J = len(jobs)

        def keys_of(i):
            br, qt, _ = jobs[i]
            k0 = max(0, qt - win_tiles) if br == "win" else 0
            return k0, qt + 1 - k0

        def wide_jobs(i):
            return sum(keys_of(n)[1] > 4 for n in range(i + 1))

        x_biased = sem("x_biased")
        lf_parts = sem("lf_parts")
        lf_ready = sem("lf_ready")
        cum_done = sem("cum_done")
        c_ready = sem("c_ready")
        cT_done = sem("cT_done")
        cT_copied = sem("cT_copied")
        c_rows = sem("c_rows")
        gate_x = sem("gate_x")
        gates_ready = sem("gates_ready")
        s_ready = sem("s_ready")
        max_ready = sem("max_ready")
        p_ready = sem("p_ready")
        p_turned = sem("p_turned")
        pt_dve = sem("pt_dve")
        pt_act = sem("pt_act")
        o_ready = sem("o_ready")
        y_done = sem("y_done")

        CMP_LEN, UNIT = nsa_cmp_pe.shape[2], 16
        HID = nsa_cmp_w1.shape[3]
        U_P, U_S = SEQ // UNIT, PAST // UNIT
        NU = U_P + NB * U_S
        NC_P, NC_S = U_P - 1, U_S - 1
        NCB = NU - 1
        kcvc_T = at(R_X, 2, UNIT // 2, NU + 2)
        cmp_w1 = at(R_W + 4 * SEQ, 2, CMP_LEN // 2, HID)
        cmp_w2 = sb("cmp_w2", [HID, 2, DH])
        pe_rows = sb("pe_rows", [CMP_LEN, 2 * DH])
        hid_bias = sb("hid_bias", [HID, 2])
        hid = at(R_XR, 2, NU)
        cmpT_k = at(R_XR + 2 * NU, NU, part=DH)
        cmp_v_p = at(R_XR + 3 * NU, DH)
        cmp_v_s = at(R_XR + 3 * NU + DH, NB, DH)
        lf_rep = at(R_XR + 3 * NU + DH + NB * DH, 2, NPG, P)
        nsa_cache = at(R_FOX, NB * NPG, 4 * DH)
        fox_cache = at(R_X, 4 * NPG, 2 * GW)
        win_cache = at(R_W + 4 * SEQ, NB, NPG, 2 * DH)
        lf_past = sb("lf_past", [P, NB * NPG, H])
        pages = sb("pages", [1, NB * NPG], I32)
        cmp_m = sb("cmp_m", [P, NT, NC_P], BF16)
        any_cmp = sb("any_cmp", [P, 1])
        head_v = sb("head_v", [P, 4, H])

        sjobs = [("fox", 0), ("sel", 0), ("sel", 1), ("win", 0), ("win", 1), ("cmp", 0), ("cmp", 1), ("fox", 1)]
        units = []
        for u, (br, g) in enumerate(sjobs):
            if br != "cmp":
                units += [(u, b, pr) for b in range(4) for pr in range(2 if br == "fox" else 1)]
        SW = PAST + NS
        Ps = at(R_W, 2, SW)
        PTs = at(R_W + 2 * SW, NPG + 1, P)
        KTs = at(R_W + 2 * SW + (NPG + 1) * P, 4, PAST)
        o_m = at(R_NQ + D, 4, GW)
        o_nsa = at(R_NQ + D + 4 * GW, 2, DH)
        o_coef = at(R_NQ + D + 4 * GW + 2 * DH, 2, H)
        later = sb("later", [P, PAST])
        same = sb("same", [NS, NS])
        new_m = sb("new_m", [NS, NS], BF16)
        left_m = sb("left_m", [NS, TN], BF16)
        left_f = sb("left_f", [NS, TN])
        spread = sb("spread", [NS, 2, P])
        spread_bf = sb("spread_bf", [NS, 2, P], BF16)
        gather = sb("gather", [P, 2, NS])
        lf_new = sb("lf_new", [NS, 2, P])
        head_m = sb("head_m", [P, H])
        gate_s = sb("gate_s", [P, 2, 3])
        gate_t = sb("gate_t", [P, 3, H])
        s_stat = sb("s_stat", [P, 2, 4])

        pages_loaded = sem("pages_loaded")
        nsa_cache_in = sem("nsa_cache_in")
        cmp_w_in = sem("cmp_w_in")
        fox_cache_in = sem("fox_cache_in")
        win_cache_in = sem("win_cache_in")
        masks_ready = sem("masks_ready")
        cc_turned = sem("cc_turned")
        cc_dve = sem("cc_dve")
        cc_act = sem("cc_act")
        pe_turned = sem("pe_turned")
        pe_copied = sem("pe_copied")
        comp_done = sem("comp_done")
        hid_ready = sem("hid_ready")
        cmp_proj = sem("cmp_proj")
        cmp_kv = sem("cmp_kv")
        c_scored = sem("c_scored")
        c_shifted = sem("c_shifted")
        c_exp = sem("c_exp")
        c_turned = sem("c_turned")
        c_pt = sem("c_pt")
        c_out = sem("c_out")
        c_added = sem("c_added")
        conv_stored = sem("conv_stored")
        s_masks = sem("s_masks")
        s_setup = sem("s_setup")
        s_ops = sem("s_ops")
        kt_turned = sem("kt_turned")
        kt_dve = sem("kt_dve")
        kt_act = sem("kt_act")
        kt_used = sem("kt_used")
        ss_ready = sem("ss_ready")
        smax_ready = sem("smax_ready")
        sp_ready = sem("sp_ready")
        sp_turned = sem("sp_turned")
        spt_ready = sem("spt_ready")
        so_ready = sem("so_ready")
        so_done = sem("so_done")
        om_ready = sem("om_ready")
        ys_ready = sem("ys_ready")
        ys_copied = sem("ys_copied")

        ALPHA = 2 ** 0.25
        NE, F = w_router.shape[1], w_exp_gate.shape[3]
        EG = 4
        layer = at(R_W, TILES, D)
        R_WO = R_W + TILES * D
        wo = at(R_WO, KD, D)
        x1T = at(R_X, KD, TOK)
        x_res = at(R_NR, 2, D)
        mix_T = at(R_NR + 2 * D, 2, 6, P)
        ln_row = [at(R_NR + 2 * D + 12 * P, 2, D), at(R_WO + 2 * KD * F + F // P * D, 2, D)]
        ln_s = sb("ln_s", [P, 2, 4])
        ln2_s = sb("ln2_s", [P, TILES, 4])
        gained = sem("gained")
        scale_ready = sem("scale_ready")
        scaled = sem("scaled")
        w_r = sb("w_r", [P, KD, NE])
        R_R = R_UV + 2 * TILES * P
        probs, *r16 = [at(R_R + i * TILES * NE, TILES, NE) for i in range(3)]
        R_R4 = R_R + 3 * TILES * NE
        r4 = [at(R_R4 + i * TILES * EG, TILES, EG) for i in range(2)]
        R_R1 = R_R4 + 2 * TILES * EG
        r1 = [at(R_R1 + i * TILES, TILES) for i in range(3)]
        rank16 = at(R_R1 + 3 * TILES, NE)
        iota_i = sb("iota_i", [P, P], I32)
        tok_i = sb("tok_i", [P, TILES], I32)

        wo_in = sem("wo_in")
        x_res_in = [sem(f"x_res_in{i}") for i in range(2)]
        ln_in = sem("ln_in")
        router_in = sem("router_in")
        mix_turned = sem("mix_turned")
        mix_dve = sem("mix_dve")
        mix_act = sem("mix_act")
        r_done = sem("r_done")
        mean_ready = sem("mean_ready")
        std_ready = sem("std_ready")
        normed = sem("normed")
        x1_turned = sem("x1_turned")
        x1T_dve = sem("x1T_dve")
        x1T_act = sem("x1T_act")
        logits_done = sem("logits_done")
        rmax_ready = sem("rmax_ready")
        rexp_ready = sem("rexp_ready")

        TOP_K = 2
        MAX_SLOTS = (TOP_K * TOK + NE * (P - 1)) // P
        MIN_SLOTS = -(-TOP_K * TOK // P)
        NSL = MAX_SLOTS + 1
        x1_dram = nc.dram_tensor("x1_scratch", [TOK, D], F32, kind="Internal").ap()
        y_dram = nc.dram_tensor("slot_rows", [NSL, P, D], F32, kind="Internal").ap()
        slot_tok = sb("slot_tok", [P, NSL], I32)
        slot_gate = sb("slot_gate", [P, NSL])
        slot_of = sb("slot_of", [P, TOP_K * TILES], I32)
        T_UPTO, T_LAST = NSL, NSL + NE
        table = sb("table", [1, NSL + NE + 2], I32)
        free = [R_R1 + 3 * TILES + NE]

        def more(*dims):
            off = free[0]
            n = 1
            for d in dims:
                n *= d
            free[0] += n
            assert free[0] <= R_SK
            return at(off, *dims)

        no_rows = at(R_UV, D)
        no_rows_ready = sem("no_rows_ready")
        rest_cleared = sem("rest_cleared")
        lo_hot = at(R_UV, TOP_K * TILES, P)
        hot = more(TOP_K, TILES, NE)
        picked = more((TILES + 1) * NE // 2).bitcast(BF16).rearrange("p (t e) -> p t e", e=NE)
        ones_bf, tri_bf = more(P // 2).bitcast(BF16), more(P // 2).bitcast(BF16)
        pair_sums = more(TILES * EG, 6)
        le16 = more(NE, NE)
        le16_x = more(NE, NE)
        over = more(NE, TILES - 1)
        n_tiles, upto, alt16 = more(NE), more(NE), more(NE)
        pos16 = more(TILES, NE)
        pos_x = more(TOP_K * TILES, NE)
        pos, lo_pos, hi_cnt = [more(TOP_K * TILES) for _ in range(3)]
        ge_tile = more(TOP_K * TILES, NSL + 1)
        hi_hot = more(TOP_K * TILES, NSL)
        slot_vals = more(TOP_K * TILES, 2 * NSL)
        iota_f = more(P)
        iota_p = more(NSL + 1)
        tok_f = more(TILES)
        gate2 = more(TOP_K, TILES)
        e_cmp = more(NSL, NE - 1)[0:1]
        e_f = more(NSL + NE + 2)[0:1]

        N_EW = 3
        R_EW = [R_WO + i * KD * D for i in range(N_EW)]
        loads_of = [len(range(i, NE, N_EW)) for i in range(N_EW)]
        x_slot = at(R_X, D)
        xT_slot = at(R_X + 2 * D, KD, P)
        y_slot = at(R_X + 4 * D, D)
        sil = at(R_X + 6 * D, F)
        h_row = at(R_X + 6 * D + F, F)
        h_T = at(R_X + 6 * D + 2 * F, F // P, P)
        y_pair = at(R_EW[1], TILES, TOP_K, D)
        ew_in = [sem(f"ew_in{i}") for i in range(N_EW)]
        EW_FIRST = [0, 16, 16]
        picked_ready = sem("picked_ready")
        ranked = sem("ranked")
        hots_ready = sem("hots_ready")
        slots_done = sem("slots_done")
        slots_ready = sem("slots_ready")
        x1_stored = sem("x1_stored")
        xs_in = sem("xs_in")
        tok_now = sb("tok_now", [P, 1], I32)
        tok_set = sem("tok_set")
        xs_turned = sem("xs_turned")
        xs_dve = sem("xs_dve")
        xs_act = sem("xs_act")
        hid_done = sem("hid_done")
        sil_ready = sem("sil_ready")
        h_ready = sem("h_ready")
        h_turned = sem("h_turned")
        hT_ready = sem("hT_ready")
        down_done = sem("down_done")
        y_dve = sem("y_dve")
        y_act = sem("y_act")
        ys_stored = sem("ys_stored")
        yp_in = [sem(f"yp_in{i}") for i in range(TILES)]
        odd_normed = sem("odd_normed")

        def last_tile(eng):
            return eng.value_load(table[0:1, T_LAST:T_LAST + 1], min_val=MIN_SLOTS - 1, max_val=MAX_SLOTS - 1)

        consts_ready = sem("consts_ready")
        x_loaded = [sem(f"x_loaded{i}") for i in range(2)]
        w_loaded = [sem(f"w_loaded{i}") for i in range(2)]
        w_half_loaded = sem("w_half_loaded")
        small_loaded = sem("small_loaded")
        turned = sem("turned")
        turn_copied = sem("turn_copied")
        proj_done = sem("proj_done")
        proj_copied = sem("proj_copied")
        dve_step = sem("dve_step")
        var_ready = sem("var_ready")
        lnv_ready = sem("lnv_ready")
        rstd_ready = sem("rstd_ready")
        v_ready = sem("v_ready")
        zg_done = sem("zg_done")
        zg_used = sem("zg_used")
        ws_turned = sem("ws_turned")
        ws_copied = sem("ws_copied")
        ws_masked = sem("ws_masked")
        z_used = sem("z_used")
        out_sem = sem("out_stored")
        outs_n = [0]

        GROUPS = [(A_U, 512), (B_Q, 512), (B_V, GW + H), (C_Q, GW), (C_KV, 6 * DH + 12)]
        LOADS = [[(c, w)] for c, w in GROUPS] + [[(D_H + f * P, P), (D_C + f * P, P), (D_B + f * P, P)]
                                                 for f in range(2)]
        NRG = len(GROUPS)
        N_ROWJ = NRG * TILES
        CHUNKS = [(0, 512), (512, 512), (SEQ, NS)]

        def w_view(g):
            n = sum(w for _, w in LOADS[g])
            return w_buf[:, g % 2, 0:KD * n].rearrange("p (k n) -> p k n", k=KD)

        def tok0(t):
            return t * P

        def halves(t, w):
            return [(0, 0, w)] if t < NT else [(0, 0, w // 2), (NS, w // 2, w - w // 2)]

        def w_last_use(g):
            return (g + 1) * TILES if g < NRG else N_ROWJ + 9 * (g - NRG + 1)

        k_stored = [sem(f"k_stored{i}") for i in range(2)]
        lf_past_in = sem("lf_past_in")

        def tail(sp):
            sp.wait_ge(k_stored[0], 16 * ((TILES + 1) // 2))
            sp.wait_ge(k_stored[1], 16 * (TILES // 2))
            sp.wait_ge(out_sem, 16 * outs_n[0])
            sp.wait_ge(conv_stored, 16 * 2 * (1 + NB))

        pool_step = sem("pool_step")
        ws_s_ready = sem("ws_s_ready")

        ws_loaded = sem("ws_loaded")

        def gate_rows(pe, t):
            n = rows_of[t]
            bank = psum[4 + t % 2]
            pe.wait_ge(v_ready, t + 1)
            if t == 0:
                pe.wait_ge(ws_masked, 1)
                pe.wait_ge(turn_copied, 2 * TILES - 1)
            if t == NT:
                pe.wait_ge(ws_s_ready, 16 * NB)
            if t >= 2:
                pe.wait_ge(zg_used, t - 1)
            for h in range(H):
                w = ws_T[:, h, :] if t < NT else ws_s[:, h, :]
                ins = nc.tensor.matmul(bank[0:n, h * DH:(h + 1) * DH], w, uv[0:n, t, GW + h * DH:GW + (h + 1) * DH],
                                       start=True, stop=True)
            ins.then_inc(zg_done, 1)

        def w_count(g):
            return 16 * sum(len(LOADS[i]) for i in range(g % 2, g + 1, 2))

        def bank_free(pe, j):
            i = j - 4
            if i < N_ROWJ:
                pe.wait_ge(proj_copied, i + 1)
                return
            f, part, c = (i - N_ROWJ) // 9, (i - N_ROWJ) % 9 // 3, (i - N_ROWJ) % 3
            if part == 0:
                pe.wait_ge(proj_copied, N_ROWJ + 3 * f + c + 1)
            else:
                pe.wait_ge(z_used, 6 * f + 3 * (part - 1) + c + 1)

        def copy_units(copy, src, u0):
            n = src.shape[-1] // UNIT
            for c in range(2):
                for odd in range(2):
                    ins = copy(kcvc_T[odd * DH:(odd + 1) * DH, c, :, u0:u0 + n],
                               src[c * DH:(c + 1) * DH, :].rearrange("p (u r o) -> p o r u", r=UNIT // 2, o=2)[:, odd])
            return ins

        def bank_units(copy, q):
            return copy_units(copy, psum[4 + q % 2], q * (512 // UNIT))

        def copy_keys(eng, copy, k):
            rows = P if sjobs[units[k][0]][0] == "fox" else DH
            eng.wait_ge(kt_turned, k + 1)
            if k >= 4:
                eng.wait_ge(kt_used, k - 3)
            return copy(KTs[0:rows, k % 4, :], psum[4 + k % 2][0:rows, :])

        act_step = sem("act_step")
        y_stored = sem("y_stored")

        def load_expert(sp, e, i):
            def src(w):
                return (w[0, e] if isinstance(e, int) else w[0, bass.ds(e, 1)].rearrange("o a b -> (o a) b")
                        ).rearrange("(k p) n -> p k n", p=P)
            gu = at(R_EW[i], KD, 2, F)
            sp.dma_start(gu[:, :, 0, :], src(w_exp_gate)).then_inc(ew_in[i], 16)
            sp.dma_start(gu[:, :, 1, :], src(w_exp_up)).then_inc(ew_in[i], 16)
            sp.dma_start(at(R_EW[i] + KD * 2 * F, F // P, D), src(w_exp_down)).then_inc(ew_in[i], 16)

        block = ctx.enter_context(nc.Block())

        @block.sync
        def _(sp):
            def load_x(t):
                if t >= 2:
                    sp.wait_ge(turned, t - 1)
                src = x_prompt[0, tok0(t):tok0(t) + P, :] if t < NT else x_sample.rearrange("b t d -> (b t) d")
                sp.dma_start(x_rows[0:rows_of[t], t % 2, :], src).then_inc(x_loaded[t % 2], 16)

            def load_w(g):
                if g >= 2:
                    sp.wait_ge(proj_done, w_last_use(g - 2))
                v, at = w_view(g), 0
                for c, w in LOADS[g]:
                    src = w_in[0, :, c:c + w].rearrange("(k p) n -> p k n", p=P)
                    k0 = 0
                    if g == 0:
                        k0 = KD // 2
                        sp.dma_start(v[:, 0:k0, at:at + w], src[:, 0:k0]).then_inc(w_half_loaded, 16)
                        load_x(1)
                    sp.dma_start(v[:, k0:KD, at:at + w], src[:, k0:KD]).then_inc(w_loaded[g % 2], 16)
                    at += w

            load_x(0)
            load_w(0)
            for t in range(2, 4):
                load_x(t)
            load_w(1)
            for t in range(4, TILES):
                load_x(t)

            def store(dst, src, sem_=out_sem):
                outs_n[0] += 1
                sp.dma_start(dst, src).then_inc(sem_, 16)

            def store_slow(dst, src):
                sp.dma_start(dst, src, allow_slow_non_contiguous=True).then_inc(conv_stored, 16)

            j = 0
            for g in range(NRG):
                if g >= 1:
                    load_w(g + 1)
                for t in range(TILES):
                    j += 1
                    n = rows_of[t]
                    if g == 1:
                        sp.wait_ge(proj_copied, j)
                        kr = qk_rows[0:n, t % 2, GW:2 * GW].rearrange("p (h d) -> p h d", h=H)
                        dst = (fox_kv_p[0, 0, tok0(t):tok0(t) + P, 0] if t < NT
                               else fox_kv_s[0, :, :, 0].rearrange("b t h d -> (b t) h d"))
                        sp.dma_start(dst, kr).then_inc(k_stored[t % 2], 16)
                if g == 2:
                    sp.wait_ge(proj_copied, j)
                    store(fox_kv_p[0, 0, :, 1].rearrange("(t p) h d -> p t (h d)", p=P), fox_v[:, 0:NT, :])
                    store(fox_kv_s[0, :, :, 1].rearrange("b t h d -> (b t) (h d)"), fox_v[0:NS, NT, :])
                if g == 4:
                    sp.wait_ge(lf_ready, 2)
                    sp.wait_ge(cT_copied, 1)
                    sp.dma_start(foxT_q[DH:DH + 1, :, :].rearrange("o h (t n) -> o (h t) n", n=P),
                                 cum_T[:, 0, :]).then_inc(c_rows, 16)
                    sp.dma_start(foxT_k[DH + 1:DH + 2, :, :].rearrange("o h (t n) -> o (h t) n", n=P),
                                 cum_T[:, 1, :]).then_inc(c_rows, 16)
                    sp.wait_ge(proj_copied, j)
                    store(nsa_kv_p[0, 0].rearrange("(t p) c d -> p t (c d)", p=P), nsa_rows[:, 0:NT, 0:4 * DH])
                    store(nsa_kv_s[0].rearrange("b t c d -> (b t) (c d)"), nsa_rows[0:NS, NT, 0:4 * DH])
                    keep = WINDOW // P
                    store(nsa_win_p[0, 0].rearrange("(t p) c d -> p t (c d)", p=P),
                          nsa_rows[:, NT - keep:NT, 4 * DH:6 * DH])
                    for b in range(NB):
                        store(nsa_win_s[0, b, PAST - TN:PAST].rearrange("t c d -> t (c d)"),
                              nsa_rows[TN * b:TN * b + TN, NT, 4 * DH:6 * DH])
                    store(nsa_win_s[0, :, 0:PAST - TN].rearrange("b t c d -> b (t c d)"),
                          state_nsa_win[0, :, TN:PAST].rearrange("b t c d -> b (t c d)"))

            load_w(NRG + 1)
            store(fox_lf_p[0, 0].rearrange("(t p) h -> p t h", p=P), lf_rows[:, 0:NT, :])
            store(fox_lf_s[0].rearrange("b t h -> (b t) h"), lf_rows[0:NS, NT, :])
            sp.wait_ge(v_ready, TILES)
            store(gmlp_v_s[0].rearrange("b t h d -> (b t) (h d)"), uv[0:NS, NT, GW:2 * GW])
            sp.wait_ge(z_used, 12)
            for f in range(2):
                fs = slice(f * P, f * P + P)
                store_slow(conv_p[0, 0, :, fs].rearrange("j p -> p j"), z_p[:, f, SEQ:SEQ + 2])
                for b in range(NB):
                    store_slow(conv_s[0, b, :, fs].rearrange("j p -> p j"), z_s[:, f, b, TN:TN + 2])

            def load_pages(cache, dst, n, first, done):
                with sp.Fori(0, n // NPG) as i:
                    table = [sp.value_load(pages[0:1, bass.ds(i * NPG + (first + k), 1)], min_val=0, max_val=NPOOL - 1)
                             for k in range(NPG)]
                    for k, page in enumerate(table):
                        sp.dma_start(dst[:, bass.ds(i * NPG + k, 1), :], cache[bass.ds(page, 1)]).then_inc(done, 16)

            sp.dma_start(pages[:], page_table.rearrange("(o b) n -> o (b n)", o=1)).then_inc(pages_loaded, 16)
            sp.wait_ge(z_used, 12)
            for c in range(2):
                sp.dma_start(cmp_w1[:, c], nsa_cmp_w1[0, c].rearrange("(l p) n -> p l n", p=2 * DH)
                             ).then_inc(cmp_w_in, 16)
                sp.dma_start(pe_rows[:, c * DH:(c + 1) * DH], nsa_cmp_pe[0, c]).then_inc(cmp_w_in, 16)
                sp.dma_start(cmp_w2[:, c, :], nsa_cmp_w2[0, c]).then_inc(cmp_w_in, 16)
            sp.wait_ge(pages_loaded, 16)
            load_pages(cache_fox_logf[0].rearrange("n p h -> n p h"), lf_past, NB * NPG, 0, lf_past_in)
            sp.wait_ge(s_ready, N_FOX)
            load_pages(cache_nsa_kv[0].rearrange("n p c d -> n p (c d)"), nsa_cache, NB * NPG, 0, nsa_cache_in)
            sp.wait_ge(comp_done, 2)
            fox_pages = cache_fox_kv[0].rearrange("n p c h d -> n p (c h d)")
            load_pages(fox_pages, fox_cache, 4 * NPG, 0, fox_cache_in)
            for b in range(NB):
                sp.dma_start(win_cache[:, b], state_nsa_win[0, b].rearrange("(n p) c d -> p n (c d)", p=P)
                             ).then_inc(win_cache_in, 16)
            sp.wait_ge(so_ready, 1)
            load_pages(fox_pages, fox_cache, 4 * NPG, 4 * NPG, fox_cache_in)
            sp.dma_start(w_r[:], w_router.rearrange("(k p) e -> p k e", p=P)).then_inc(router_in, 16)
            sp.wait_ge(so_ready, 3)
            sp.dma_start(wo[:], w_out[0].rearrange("(k p) n -> p k n", p=P)).then_inc(wo_in, 16)
            sp.wait_ge(so_ready, 5)
            sp.wait_ge(out_sem, 16 * outs_n[0])

            def rows_dram(x_p, x_s, t):
                return x_p[0, tok0(t):tok0(t) + P, :] if t < NT else x_s.rearrange("b t d -> (b t) d")

            sp.wait_ge(so_ready, len(sjobs))
            for i, row in enumerate((ln_g, ln_b)):
                sp.dma_start(ln_row[0][:, i, :], row[0, 0].partition_broadcast(P)).then_inc(ew_in[1 + i], 16)

            def store_x1(t):
                sp.wait_ge(normed, t + 1)
                sp.dma_start(x1_dram[tok0(t):tok0(t) + rows_of[t]], layer[0:rows_of[t], t, :]).then_inc(x1_stored, 16)

            for t in range(TILES):
                if t >= 2:
                    sp.wait_ge(mean_ready, t - 1)
                sp.dma_start(x_res[0:rows_of[t], t % 2, :], rows_dram(x_prompt, x_sample, t)
                             ).then_inc(x_res_in[t % 2], 16)
                if t == 2:
                    sp.wait_ge(ys_ready, 1)
                    sp.wait_ge(ew_in[1], EW_FIRST[1])
                    sp.wait_ge(ew_in[2], EW_FIRST[2])
                    load_expert(sp, 1, 1)
                if t >= 2:
                    store_x1(t - 2)
            store_x1(TILES - 2)
            store_x1(TILES - 1)
            sp.wait_ge(r_done, TILES)
            load_expert(sp, 0, 0)
            for i, row in enumerate((ln_g, ln_b)):
                sp.dma_start(ln_row[1][:, i, :], row[0, 1].partition_broadcast(P)).then_inc(ln_in, 16)
            sp.wait_ge(slots_ready, 1)
            sp.wait_ge(xs_in, 16)
            load_expert(sp, 2, 2)

            sp.wait_ge(no_rows_ready, 1)
            sp.wait_ge(down_done, 2)
            with sp.Fori(last_tile(sp) + 1, NSL) as t:
                sp.dma_start(y_dram[bass.ds(t, 1)].rearrange("s p d -> (s p) d"), no_rows[:]).then_inc(rest_cleared, 16)
            def next_expert(turn, i):
                done = sp.value_load(table[0:1, bass.ds(turn * N_EW + (T_UPTO + i), 1)], min_val=0, max_val=MAX_SLOTS)
                done, arrived = sp.to_reg(done + 1), sp.to_reg(turn * 48 + (48 + EW_FIRST[i]))
                sp.wait_ge(down_done, done)
                sp.wait_ge(ew_in[i], arrived)
                load_expert(sp, turn * N_EW + (N_EW + i), i)

            with sp.Fori(0, NE // N_EW - 1) as turn:
                for i in range(N_EW):
                    next_expert(turn, i)
            next_expert(NE // N_EW - 1, 0)

            for t in range(TILES):
                if t % 2:
                    sp.wait_ge(odd_normed, t // 2 + 1)
                else:
                    sp.wait_ge(normed, TILES + t // 2 + 1)
                sp.dma_start(rows_dram(y_prompt, y_sample, t), layer[0:rows_of[t], t, :]).then_inc(y_stored, 16)
            sp.wait_ge(y_stored, 16 * TILES)
            tail(sp)

        @block.gpsimd
        def _(pool):
            pool.memset(ident[:], 0.0).then_inc(pool_step, 1)
            pool.memset(ident_bf[:], 0.0).then_inc(pool_step, 1)
            pool.memset(ones[:], 1.0).then_inc(pool_step, 1)
            pool.memset(zeros_bf[:], 0.0).then_inc(pool_step, 1)
            pool.wait_ge(pool_step, 4)
            for m in (ident, ident_bf):
                pool.affine_select(out=m[:], in_=m[:], compare_op=ALU.not_equal, fill=1.0, base=0,
                                   pattern=[[-1, P]], channel_multiplier=1).then_inc(consts_ready, 1)
            pool.affine_select(out=tri_u[:], in_=ones[:], compare_op=ALU.is_ge, fill=0.0, base=0,
                               pattern=[[1, P]], channel_multiplier=-1).then_inc(consts_ready, 1)
            pool.affine_select(out=causal_m[:], in_=zeros_bf[:], compare_op=ALU.is_ge, fill=NEG, base=0,
                               pattern=[[-1, P]], channel_multiplier=1).then_inc(consts_ready, 1)
            pool.affine_select(out=far_m[:], in_=zeros_bf[:], compare_op=ALU.is_gt, fill=NEG, base=0,
                               pattern=[[1, P]], channel_multiplier=-1).then_inc(consts_ready, 1)
            pool.memset(cmp_m[:], 0.0).then_inc(pool_step, 1)
            pool.memset(same[:], 1.0).then_inc(pool_step, 1)
            pool.memset(later[:], 1.0).then_inc(pool_step, 1)
            pool.memset(spread[:], 0.0).then_inc(pool_step, 1)
            pool.memset(lf_new[:], 1.0).then_inc(pool_step, 1)
            pool.wait_ge(pool_step, 9)
            pool.affine_select(out=cmp_m[:], in_=cmp_m[:], compare_op=ALU.is_ge, fill=NEG, base=1 - CMP_LEN,
                               pattern=[[P, NT], [-UNIT, NC_P]], channel_multiplier=1).then_inc(masks_ready, 1)
            pool.affine_select(out=any_cmp[:], in_=ones[:, 0:1], compare_op=ALU.is_ge, fill=0.0, base=1 - CMP_LEN,
                               pattern=[[0, 1]], channel_multiplier=1).then_inc(masks_ready, 1)
            pool.affine_select(out=later[:, PAST - P:PAST], in_=later[:, PAST - P:PAST], compare_op=ALU.is_gt, fill=0.0,
                               base=0, pattern=[[-1, P]], channel_multiplier=1).then_inc(masks_ready, 1)
            pool.affine_select(out=same[:], in_=same[:], compare_op=ALU.is_ge, fill=0.0, base=0,
                               pattern=[[-TN, NB], [-1, TN]], channel_multiplier=1).then_inc(masks_ready, 1)
            for g in range(2):
                base = -4 * TN * g
                pool.affine_select(out=spread[:, g, :], in_=spread[:, g, :], compare_op=ALU.not_equal, fill=1.0,
                                   base=base, pattern=[[-TN, 4], [0, H], [-1, TN]], channel_multiplier=1
                                   ).then_inc(masks_ready, 1)
                pool.affine_select(out=lf_new[:, g, :], in_=lf_new[:, g, :], compare_op=ALU.is_ge, fill=0.0,
                                   base=base, pattern=[[-TN, 4], [0, H], [0, TN]], channel_multiplier=1
                                   ).then_inc(masks_ready, 1)
            pool.wait_ge(masks_ready, 8)
            pool.affine_select(out=same[:], in_=same[:], compare_op=ALU.is_ge, fill=0.0, base=TN - 1,
                               pattern=[[TN, NB], [0, TN]], channel_multiplier=-1).then_inc(masks_ready, 1)
            for g in range(2):
                pool.affine_select(out=lf_new[:, g, :], in_=lf_new[:, g, :], compare_op=ALU.is_ge, fill=0.0,
                                   base=4 * TN * g, pattern=[[TN, 4], [0, H], [1, TN]], channel_multiplier=-1
                                   ).then_inc(masks_ready, 1)
            pool.iota(iota_i[:], pattern=[[1, P]], base=0, channel_multiplier=0).then_inc(masks_ready, 1)
            pool.iota(tok_i[:], pattern=[[P, TILES]], base=0, channel_multiplier=1).then_inc(masks_ready, 1)
            pool.wait_ge(ws_copied, 1)
            pool.affine_select(out=ws_T[:], in_=ws_T[:], compare_op=ALU.is_ge, fill=0.0, base=0,
                               pattern=[[0, H], [1, P]], channel_multiplier=-1).then_inc(ws_masked, 1)
            pool.memset(ws_s[:], 0.0).then_inc(pool_step, 1)
            pool.wait_ge(pool_step, 10)
            pool.wait_ge(ws_masked, 1)
            for b in range(NB):
                pool.dma_start(ws_s[TN * b:TN * b + TN, :, TN * b:TN * b + TN], ws_T[0:TN, :, 0:TN]
                               ).then_inc(ws_s_ready, 16)

            def gather_x1(col, n):
                pool.tensor_copy(tok_now[:], slot_tok[:, col]).then_inc(tok_set, 1)
                pool.wait_ge(x1_stored, 16 * TILES)
                pool.wait_ge(tok_set, n)
                pool.indirect_dma_start(x_slot[:], None, x1_dram,
                                        bass.IndirectOffsetOnAxis(ap=tok_now[:], axis=0)).then_inc(xs_in, 16)

            pool.wait_ge(slots_ready, 1)
            gather_x1(slice(0, 1), 1)
            last = last_tile(pool)
            rest = pool.value_load(table[0:1, T_LAST + 1:T_LAST + 2], min_val=1, max_val=NSL - MIN_SLOTS)
            pool.memset(no_rows[:], 0.0).then_inc(no_rows_ready, 1)
            with pool.Fori(0, last + 1) as t:
                pool.wait_ge(xs_turned, t * 2 + 2)
                gather_x1(bass.ds(t + 1, 1), pool.to_reg(t + 2))
            pool.wait_ge(xs_in, last * 16 + 32)
            stored, cleared = pool.to_reg(last * 16 + 16), pool.to_reg(rest * 16)
            for i in range(N_EW):
                pool.wait_ge(ew_in[i], 48 * loads_of[i] + EW_FIRST[i])
            pool.wait_ge(ys_stored, stored)
            pool.wait_ge(rest_cleared, cleared)
            rows = y_dram.rearrange("s p d -> (s p) d")

            for t in range(TILES):
                n = rows_of[t]
                for k in range(TOP_K):
                    c = k * TILES + t
                    pool.indirect_dma_start(y_pair[0:n, t, k, :], None, rows,
                                            bass.IndirectOffsetOnAxis(ap=slot_of[0:n, c:c + 1], axis=0)
                                            ).then_inc(yp_in[t], 16)
            for t in range(1, TILES, 2):
                n = rows_of[t]
                v = layer[0:n, t, :]
                pool.wait_ge(gained, t + 1)
                pool.tensor_tensor(v, v, ln_row[1][0:n, 1, :], ALU.add).then_inc(odd_normed, 1)

        @block.scalar
        def _(act):
            act.dma_start(ws_rows, gmlp_w_s[0].rearrange("h t s -> t h s")).then_inc(ws_loaded, 16)
            act.dma_start(bs[:, 0, :], gmlp_b_s[0].rearrange("h t -> t h"),
                          allow_slow_non_contiguous=True).then_inc(small_loaded, 16)
            for b in range(NB):
                act.dma_start(bs[TN * b:TN * b + TN, 1, :], gmlp_b_s[0, :, 0:TN].rearrange("h t -> t h"),
                              allow_slow_non_contiguous=True).then_inc(small_loaded, 16)
            act.dma_start(bias_f[:], fox_b_f[0].partition_broadcast(P)).then_inc(small_loaded, 16)
            for f in range(2):
                act.dma_start(cw[:, f, :], conv_w[0, :, f * P:(f + 1) * P].rearrange("j p -> p j"),
                              allow_slow_non_contiguous=True).then_inc(small_loaded, 16)
            for f in range(2):
                for b in range(NB):
                    act.dma_start(z_s[:, f, b, 0:2], state_conv[0, b, :, f * P:(f + 1) * P].rearrange("j p -> p j"),
                                  allow_slow_non_contiguous=True).then_inc(small_loaded, 16)
            for t in range(TILES):
                act.wait_ge(proj_done, t + 1)
                n = rows_of[t]
                for p0, c0, cn in halves(t, 2 * GW):
                    ins = nc.scalar.activation(uv[0:n, t, c0:c0 + cn], psum[t % 4][p0:p0 + n, 0:cn], ACT.Gelu_apprx_tanh)
                ins.then_inc(proj_copied, 1)
            act.wait_ge(var_ready, TILES + 1)
            nc.scalar.activation(ln_stat[:, :, :, 1], ln_stat[:, :, :, 1], ACT.Ln, bias=lnc[:, 0:1]).then_inc(lnv_ready, 1)
            act.wait_ge(lnv_ready, 1)
            nc.scalar.activation(ln_stat[:, :, :, 1], ln_stat[:, :, :, 1], ACT.Exp, scale=-0.5).then_inc(rstd_ready, 1)
            j = TILES
            for g in range(1, NRG):
                for t in range(TILES):
                    n, w = rows_of[t], GROUPS[g][1]
                    act.wait_ge(proj_done, j + 1)
                    if g == 1 and t >= 2:
                        act.wait_ge(turned, TILES + t - 1)
                        act.wait_ge(k_stored[t % 2], 16 * (t // 2))
                    if g == 1 and t < 2:
                        act.wait_ge(ws_turned, 1)
                    if g == 3:
                        act.wait_ge(turned, 2 * TILES + max(t - 1, 0))
                        if t < 2:
                            act.wait_ge(k_stored[t % 2], 16 * ((TILES + 1 - t) // 2))
                    ps = psum[j % 4]
                    if g == 1:
                        out = qk_rows[0:n, t % 2, :]
                    elif g == 2:
                        out = fox_v[0:n, t, :]
                    elif g == 3:
                        out = qk_rows[0:n, t % 2, 0:GW]
                    else:
                        out = nsa_rows[0:n, t, :]
                    for p0, c0, cn in halves(t, w):
                        rows = min(cn, out.shape[-1] - c0)
                        ins = nc.scalar.copy(out[:, c0:c0 + rows], ps[p0:p0 + n, 0:rows])
                        if rows < cn:
                            ins = nc.scalar.copy(b_f[0:n, :, t], ps[p0:p0 + n, rows:cn])
                    ins.then_inc(proj_copied, 1)
                    j += 1
                    if (g, t) == (3, 0):
                        act.wait_ge(x_biased, 1)
                        nc.scalar.activation(lf_e[:], lf_x[:], ACT.Abs).then_inc(lf_parts, 1)
                        act.wait_ge(lf_parts, 1)
                        nc.scalar.activation(lf_e[:], lf_e[:], ACT.Exp, scale=-1.0).then_inc(lf_parts, 1)
                        act.wait_ge(lf_parts, 2)
                        nc.scalar.activation(lf_e[:], lf_e[:], ACT.Ln, bias=lnc[:, 1:2]).then_inc(lf_parts, 1)
            act.wait_ge(proj_copied, N_ROWJ)
            nc.scalar.activation(gates[:].rearrange("p t b h -> p t (b h)"), nsa_rows[:, :, 6 * DH:6 * DH + 12],
                                 ACT.Exp, scale=-1.0).then_inc(gate_x, 1)
            for f in range(2):
                if f:
                    act.wait_ge(z_used, 3)
                for c, (c0, cn) in enumerate(CHUNKS):
                    act.wait_ge(proj_done, N_ROWJ + 9 * f + c + 1)
                    nc.scalar.copy(dh_T[c], psum[(N_ROWJ + 9 * f + c) % 4][:, 0:cn]).then_inc(proj_copied, 1)

            def exp_scores(i):
                n = keys_of(i)[1]
                act.wait_ge(max_ready, i + 1)
                if i >= 2:
                    act.wait_ge(p_turned, i - 1)
                if i >= 4:
                    act.wait_ge(y_done, i - 3)
                nc.scalar.activation(P_buf[:, i % 2, 0:n * P], banks(2 * (i % 2), 2)[:, 0:n * P], ACT.Exp,
                                     bias=neg_max[:, i % 4:i % 4 + 1],
                                     accum_out=row_sum[:, i % 4:i % 4 + 1]).then_inc(p_ready, 1)

            def copy_pt_act(i):
                n = keys_of(i)[1]
                if n > 4:
                    act.wait_ge(p_turned, i + 1)
                    if i >= 2:
                        act.wait_ge(o_ready, i - 1)
                    nc.scalar.copy(PT_buf[:, i % 2, 512:n * P], psum[5][:, 0:(n - 4) * P]).then_inc(pt_act, 1)

            for i in range(J + 1):
                if i < J:
                    exp_scores(i)
                if i >= 1:
                    copy_pt_act(i - 1)

            for q in range(1, 2 + NB, 2):
                act.wait_ge(cc_turned, q + 1)
                bank_units(nc.scalar.copy, q).then_inc(cc_act, 1)
            act.wait_ge(comp_done, 2)
            act.wait_ge(conv_stored, 16 * 2 * (1 + NB))
            for c in range(2):
                ins = nc.scalar.copy(hid_bias[:, c:c + 1], psum[c][:, NU:NU + 1])
            ins.then_inc(act_step, 1)
            act.wait_ge(act_step, 1)
            for c in range(2):
                nc.scalar.activation(hid[:, c, 0:NCB], psum[c][:, 0:NCB], ACT.Gelu_apprx_tanh,
                                     bias=hid_bias[:, c:c + 1]).then_inc(hid_ready, 1)
            act.wait_ge(cmp_proj, 1)
            nc.scalar.copy(cmpT_k[:, 0:NCB], psum[2][0:DH, 0:NCB])
            nc.scalar.copy(cmp_v_p[0:NC_P, :], psum[3][0:NC_P, 0:DH])
            nc.scalar.copy(cmp_v_s[0:NC_S], psum[4][0:NC_S, 0:NB * DH].rearrange("p (b d) -> p b d", b=NB)
                           ).then_inc(cmp_kv, 1)
            for qt in range(NT + 1):
                if qt < NT:
                    act.wait_ge(c_shifted, qt + 1)
                    v = P_buf[:, qt % 2, 0:H * NC_P]
                    nc.scalar.activation(v, v, ACT.Exp).then_inc(c_exp, 1)
                if qt >= 1:
                    act.wait_ge(c_turned, qt)
                    if qt >= 3:
                        act.wait_ge(c_out, qt - 2)
                    nc.scalar.copy(PT_buf[0:NC_P, (qt - 1) % 2, 0:512], psum[4 + (qt - 1) % 2][0:NC_P, :]
                                   ).then_inc(c_pt, 1)
            k = 0
            for u, (br, g) in enumerate(sjobs):
                while k < len(units) and units[k][0] == u:
                    if k % 2:
                        copy_keys(act, nc.scalar.copy, k).then_inc(kt_act, 1)
                    k += 1
                act.wait_ge(smax_ready, u + 1)
                if u >= 2:
                    act.wait_ge(sp_turned, u - 1)
                    act.wait_ge(so_done, u - 1)
                w = NC_S if br == "cmp" else SW
                nc.scalar.activation(Ps[:, u % 2, 0:w], banks(2 * (u % 2), 2)[:, 0:w], ACT.Exp,
                                     bias=s_stat[:, u % 2, 0:1], accum_out=s_stat[:, u % 2, 1:2]).then_inc(sp_ready, 1)
            steps = [1]

            def link(ins):
                steps[0] += 1
                ins.then_inc(act_step, 1)
                act.wait_ge(act_step, steps[0])

            def copy_mix(t):
                n = rows_of[t]
                act.wait_ge(mix_turned, t + 1)
                if t >= 2:
                    act.wait_ge(r_done, t - 1)
                nc.scalar.copy(mix_T[:, t % 2, 4:6, 0:n], psum[5][:, 0:2 * P].rearrange("p (k n) -> p k n", k=2)[:, :, 0:n]
                               ).then_inc(mix_act, 1)

            def deviation(i, t):
                n, m = rows_of[t], TILES * i + t
                st = ln2_s[0:n, t, :] if i else ln_s[0:n, t % 2, :]
                act.wait_ge(mean_ready, m + 1)
                link(nc.scalar.activation(banks(2 * (m % 2), 2)[0:n, :], layer[0:n, t, :], ACT.Square, bias=st[:, 1:2],
                                          accum_out=st[:, 2:3]))
                nc.scalar.activation(st[:, 2:3], st[:, 2:3], ACT.Sqrt, bias=lnc[0:n, 0:1], scale=1.0 / D).then_inc(std_ready, 1)

            def after_turn(t):
                n = rows_of[t]
                act.wait_ge(x1_turned, t + 1)
                nc.scalar.copy(x1T[:, 0:4, tok0(t):tok0(t) + n],
                               psum[6][:].rearrange("p (k n) -> p k n", k=4)[:, :, 0:n]).then_inc(x1T_act, 1)

            act.wait_ge(ys_ready, 1)
            copy_mix(0)
            for t in range(TILES + 1):
                if t + 1 < TILES:
                    copy_mix(t + 1)
                if t < TILES:
                    deviation(0, t)
                if t >= 1:
                    after_turn(t - 1)
            act.wait_ge(rmax_ready, 1)
            pv = probs[:].rearrange("p t e -> p (t e)")
            nc.scalar.activation(pv, pv, ACT.Exp).then_inc(rexp_ready, 1)
            def copy_x(n_turned):
                act.wait_ge(xs_turned, n_turned)
                nc.scalar.copy(xT_slot[:, 4:8, :], psum[5][:].rearrange("p (k n) -> p k n", k=4)).then_inc(xs_act, 1)

            def copy_rows(n, before):
                if not isinstance(before, int) or before > 0:
                    act.wait_ge(ys_stored, before)
                act.wait_ge(down_done, n + 1)
                nc.scalar.copy(y_slot[:, 512:1024], psum[3][:]).then_inc(y_act, 1)

            def store_rows(n):
                act.wait_ge(y_act, n)
                act.wait_ge(y_dve, n)
                act.dma_start(y_dram[bass.ds(n - 1, 1)].rearrange("s p d -> (s p) d"), y_slot[:]).then_inc(ys_stored, 16)

            def slot_tile(t, before):
                some = not isinstance(t, int) or t > 0
                act.wait_ge(hid_done, t + 1)
                nc.scalar.activation(sil[:], psum[0][:, 0:F], ACT.Silu).then_inc(sil_ready, 1)
                copy_x(t * 2 + 4)
                if some:
                    copy_rows(t, before * 16)
                act.wait_ge(h_turned, t + 1)
                nc.scalar.copy(h_T[:].rearrange("p f n -> p (f n)"), psum[6][:, 0:F]).then_inc(hT_ready, 1)
                if some:
                    store_rows(t)

            act.wait_ge(slots_ready, 1)
            last = last_tile(act)
            copy_x(2)
            slot_tile(0, -1)
            slot_tile(1, 0)
            with act.Fori(1, last) as before:
                slot_tile(before + 1, before)
            copy_rows(last + 1, last * 16)
            store_rows(last + 1)

            def scale(t):
                n = rows_of[t]
                v = layer[0:n, t, :]
                act.wait_ge(scale_ready, t + 1)
                nc.scalar.activation(v, v, ACT.Identity, scale=ln2_s[0:n, t, 3:4], bias=ln2_s[0:n, t, 0:1]).then_inc(scaled, 1)

            for t in range(TILES + 1):
                if t < TILES:
                    deviation(1, t)
                if t >= 1:
                    scale(t - 1)

        @block.tensor
        def _(pe):
            def turn_x(t):
                n = rows_of[t]
                pe.wait_ge(x_loaded[t % 2], 16 * (t // 2 + 1))
                if t >= 2:
                    pe.wait_ge(turn_copied, t - 1)
                for k in range(KD):
                    ins = nc.tensor.transpose(psum[4 + 2 * (t % 2) + k // 4][:, (k % 4) * P:(k % 4) * P + n],
                                              x_rows[0:n, t % 2, k * P:(k + 1) * P], ident[0:n, 0:n])
                ins.then_inc(turned, 1)

            def project_rows(g, t):
                j = g * TILES + t
                n, w = rows_of[t], GROUPS[g][1]
                if (g, t) == (0, 0):
                    pe.wait_ge(w_half_loaded, 16)
                elif t == 0:
                    pe.wait_ge(w_loaded[g % 2], w_count(g))
                if g == 0:
                    pe.wait_ge(turn_copied, t + 1)
                if j >= 4:
                    pe.wait_ge(proj_copied, j - 3)
                wv = w_view(g)
                for k in range(KD):
                    if (g, t, k) == (0, 0, KD // 2):
                        pe.wait_ge(w_loaded[0], w_count(0))
                    for p0, c0, cn in halves(t, w):
                        ins = nc.tensor.matmul(psum[j % 4][p0:p0 + n, 0:cn], xT[:, k, tok0(t):tok0(t) + n],
                                               wv[:, k, c0:c0 + cn], start=(k == 0), stop=(k == KD - 1),
                                               tile_position=(0, p0) if t == NT else None, skip_group_check=(t == NT))
                ins.then_inc(proj_done, 1)

            def turn_rows(g, t):
                e = {1: 1, 3: 2, 4: 3}[g] * TILES + t
                n = rows_of[t]
                pe.wait_ge(proj_copied, g * TILES + t + 1)
                pe.wait_ge(turn_copied, e - 1)
                if e == 2 * TILES:
                    pe.wait_ge(zg_used, TILES)
                A, B = psum[4 + 2 * (e % 2)], psum[5 + 2 * (e % 2)]
                I = ident[0:n, 0:n]
                if g == 1 and t < NT:
                    for h in range(H):
                        for bank, c in ((A, 0), (B, GW)):
                            ins = nc.tensor.transpose(bank[0:DH, h * P:(h + 1) * P],
                                                      qk_rows[:, t % 2, c + h * DH:c + (h + 1) * DH], I)
                elif g == 1:
                    for pair in range(2):
                        for bank, c in ((A, 0), (B, GW)):
                            ins = nc.tensor.transpose(bank[:, pair * P:pair * P + n],
                                                      qk_rows[0:n, t % 2, c + pair * P:c + (pair + 1) * P], I)
                elif g == 3:
                    for h in range(H):
                        ins = nc.tensor.transpose(A[0:DH, h * P:h * P + n],
                                                  qk_rows[0:n, t % 2, h * DH:(h + 1) * DH], I)
                else:
                    for i, c in enumerate((2, 4)):
                        ins = nc.tensor.transpose(A[0:DH, i * P:i * P + n], nsa_rows[0:n, t, c * DH:(c + 1) * DH], I)
                ins.then_inc(turned, 1)

            pe.wait_ge(consts_ready, 5)
            for t in range(TILES):
                turn_x(t)
                if t >= 1:
                    project_rows(0, t - 1)
            pe.wait_ge(ws_loaded, 16)
            pe.wait_ge(turn_copied, TILES)
            for h in range(H):
                ins = nc.tensor.transpose(psum[6][:, h * P:(h + 1) * P], ws_rows[:, h, :], ident[:])
            ins.then_inc(ws_turned, 1)
            project_rows(0, TILES - 1)
            pe.wait_ge(ws_copied, 1)
            for g in range(1, NRG):
                for t in range(TILES):
                    project_rows(g, t)
                    if g != 2 and t >= 1:
                        turn_rows(g, t - 1)
                    if g == 2:
                        gate_rows(pe, t)
                    if g in (2, 4) and t == 0:
                        turn_rows(g - 1, TILES - 1)
                    if (g, t) == (3, TILES - 1):
                        pe.wait_ge(lf_ready, 1)
                        lfp = lf[:, :, 0:NT]
                        nc.tensor.matmul(psum[5][:, 0:H * NT], tri_u[:], lfp, start=True, stop=True)
                        nc.tensor.matmul(psum[5][:, 64:64 + H * NT], ones[:], lfp, start=True, stop=True
                                         ).then_inc(cum_done, 1)
                    if (g, t) == (4, 1):
                        pe.wait_ge(c_ready, 1)
                        nc.tensor.transpose(psum[7][0:H * NT, 0:P], cum[:].rearrange("p h t -> p (h t)"), ident[:]
                                            ).then_inc(cT_done, 1)
            for f in range(2):
                g = NRG + f
                pe.wait_ge(w_loaded[g % 2], w_count(g))
                wv = w_view(g)
                for part in range(3):
                    for c, (c0, cn) in enumerate(CHUNKS):
                        j = N_ROWJ + 9 * f + 3 * part + c
                        bank_free(pe, j)
                        for k in range(KD):
                            ins = nc.tensor.matmul(psum[j % 4][:, 0:cn], wv[:, k, part * P:(part + 1) * P],
                                                   xT[:, k, c0:c0 + cn], start=(k == 0), stop=(k == KD - 1))
                        ins.then_inc(proj_done, 1)
                    if f == 0 and part == 0:
                        turn_rows(4, TILES - 1)

            def scores(i):
                br, qt, h = jobs[i]
                k0, n = keys_of(i)
                if i >= 2:
                    pe.wait_ge(p_ready, i - 1)
                elif i == 0:
                    pe.wait_ge(z_used, 12)
                    pe.wait_ge(turn_copied, 4 * TILES)
                    pe.wait_ge(c_rows, 32)
                q = (foxT_q if br == "fox" else nsaT_q)[:, h, qt * P:(qt + 1) * P]
                kT = foxT_k[:, h, :] if br == "fox" else selT_k if br == "sel" else winT_k
                S = banks(2 * (i % 2), 2)
                for c0 in range(0, n * P, 512):
                    cn = min(512, n * P - c0)
                    masks = []
                    if c0 + cn == n * P:
                        masks.append((n * P - P, causal_m))
                    if br == "win" and qt >= win_tiles and c0 == 0:
                        masks.append((0, far_m))
                    ins = nc.tensor.matmul(S[:, c0:c0 + cn], q, kT[:, k0 * P + c0:k0 * P + c0 + cn],
                                           start=True, stop=not masks, skip_group_check=True)
                    for k, (m0, m) in enumerate(masks):
                        ins = nc.tensor.matmul(S[:, m0:m0 + P], ident_bf[:], m[:], start=False,
                                               stop=(k == len(masks) - 1), skip_group_check=True)
                ins.then_inc(s_ready, 1)

            def turn_p(i):
                n = keys_of(i)[1]
                pe.wait_ge(p_ready, i + 1)
                if i >= 1:
                    pe.wait_ge(pt_dve, i)
                    if wide_jobs(i - 1):
                        pe.wait_ge(pt_act, wide_jobs(i - 1))
                for k in range(n):
                    ins = nc.tensor.transpose(psum[4 + k // 4][:, (k % 4) * P:(k % 4 + 1) * P],
                                              P_buf[:, i % 2, k * P:(k + 1) * P], ident[:])
                ins.then_inc(p_turned, 1)

            def p_times_v(i):
                br, qt, h = jobs[i]
                k0, n = keys_of(i)
                pe.wait_ge(pt_dve, i + 1)
                if wide_jobs(i):
                    pe.wait_ge(pt_act, wide_jobs(i))
                if i >= 2:
                    pe.wait_ge(y_done, i - 1)
                for k in range(n):
                    if br == "fox":
                        v = fox_v[:, k0 + k, h * DH:(h + 1) * DH]
                    else:
                        c = 3 if br == "sel" else 5
                        v = nsa_rows[:, k0 + k, c * DH:(c + 1) * DH]
                    ins = nc.tensor.matmul(psum[6 + i % 2][:, 0:DH], PT_buf[:, i % 2, k * P:(k + 1) * P], v,
                                           start=(k == 0), stop=(k == n - 1))
                ins.then_inc(o_ready, 1)

            for i in range(J + 2):
                if i < J:
                    scores(i)
                if 1 <= i <= J:
                    turn_p(i - 1)
                if i >= 2:
                    p_times_v(i - 2)

            pe.wait_ge(pt_dve, J)
            pe.wait_ge(pt_act, wide_jobs(J - 1))
            pe.wait_ge(y_done, J)
            pe.wait_ge(cmp_w_in, 16 * 6)
            nc.tensor.transpose(psum[6][:, 0:CMP_LEN], pe_rows[:], ident[0:CMP_LEN, 0:CMP_LEN]).then_inc(pe_turned, 1)
            for q in range(2 + NB):
                if q >= 2:
                    pe.wait_ge(cc_act if q % 2 else cc_dve, q // 2)
                if q == 2:
                    pe.wait_ge(nsa_cache_in, 16 * NB * NPG)
                for k in range(4):
                    src = nsa_rows[:, 4 * q + k, 0:2 * DH] if q < 2 else nsa_cache[:, (q - 2) * NPG + k, 0:2 * DH]
                    ins = nc.tensor.transpose(psum[4 + q % 2][:, k * P:(k + 1) * P], src, ident[:])
                ins.then_inc(cc_turned, 1)
            pe.wait_ge(pe_copied, 1)
            pe.wait_ge(cc_dve, 1 + NB // 2)
            pe.wait_ge(cc_act, 1 + NB // 2)
            for c in range(2):
                for l in range(CMP_LEN // 2):
                    u0, r = l // (UNIT // 2), l % (UNIT // 2)
                    ins = nc.tensor.matmul(psum[c][:, 0:NU + 1], cmp_w1[:, c, l, :], kcvc_T[:, c, r, u0:u0 + NU + 1],
                                           start=(l == 0), stop=(l == CMP_LEN // 2 - 1))
                ins.then_inc(comp_done, 1)
            pe.wait_ge(hid_ready, 2)
            nc.tensor.matmul(psum[2][0:DH, 0:NCB], cmp_w2[:, 0, :], hid[:, 0, 0:NCB], start=True, stop=True)
            nc.tensor.matmul(psum[3][0:NC_P, 0:DH], hid[:, 1, 0:NC_P], cmp_w2[:, 1, :], start=True, stop=True)
            for b in range(NB):
                u0 = U_P + U_S * b
                ins = nc.tensor.matmul(psum[4][0:NC_S, b * DH:(b + 1) * DH], hid[:, 1, u0:u0 + NC_S], cmp_w2[:, 1, :],
                                       start=True, stop=True)
            ins.then_inc(cmp_proj, 1)

            def cmp_scores(qt):
                if qt == 0:
                    pe.wait_ge(cmp_kv, 1)
                    pe.wait_ge(masks_ready, 11)
                if qt >= 2:
                    pe.wait_ge(c_shifted, qt - 1)
                S = psum[2 + qt % 2]
                for h in range(H):
                    nc.tensor.matmul(S[:, h * NC_P:(h + 1) * NC_P], nsaT_q[:, h, qt * P:(qt + 1) * P],
                                     cmpT_k[:, 0:NC_P], start=True, stop=False, skip_group_check=True)
                    ins = nc.tensor.matmul(S[:, h * NC_P:(h + 1) * NC_P], ident_bf[:], cmp_m[:, qt, :],
                                           start=False, stop=True, skip_group_check=True)
                ins.then_inc(c_scored, 1)

            def cmp_turn(qt):
                pe.wait_ge(c_exp, qt + 1)
                if qt >= 2:
                    pe.wait_ge(c_pt, qt - 1)
                for h in range(H):
                    ins = nc.tensor.transpose(psum[4 + qt % 2][0:NC_P, h * P:(h + 1) * P],
                                              P_buf[:, qt % 2, h * NC_P:(h + 1) * NC_P], ident[:])
                ins.then_inc(c_turned, 1)

            def cmp_out(qt):
                pe.wait_ge(c_pt, qt + 1)
                if qt >= 2:
                    pe.wait_ge(c_added, qt - 1)
                for h in range(H):
                    ins = nc.tensor.matmul(psum[6 + qt % 2][:, h * DH:(h + 1) * DH],
                                           PT_buf[0:NC_P, qt % 2, h * P:(h + 1) * P], cmp_v_p[0:NC_P, :],
                                           start=True, stop=True)
                ins.then_inc(c_out, 1)

            for qt in range(NT + 2):
                if qt < NT:
                    cmp_scores(qt)
                if 1 <= qt <= NT:
                    cmp_turn(qt - 1)
                if qt >= 2:
                    cmp_out(qt - 2)

            pe.wait_ge(c_added, NT)
            for g in range(2):
                nc.tensor.transpose(psum[6][:, g * NS:(g + 1) * NS], spread[:, g, :], ident[0:NS, 0:NS])
                ins = nc.tensor.matmul(psum[7][:, 16 * g:16 * g + 12], spread[:, g, :],
                                       gates[0:NS, NT].rearrange("p b h -> p (b h)"), start=True, stop=True)
            ins.then_inc(s_ops, 1)

            def turn_keys(k):
                u, b, pr = units[k]
                br, g = sjobs[u]
                if k < 2:
                    pe.wait_ge(c_pt, NT)
                else:
                    pe.wait_ge(kt_act if k % 2 else kt_dve, k // 2)
                if b == 0 and pr == 0:
                    if br == "fox":
                        pe.wait_ge(fox_cache_in, 16 * 4 * NPG * (g + 1))
                    if br == "win":
                        pe.wait_ge(win_cache_in, 16 * NB)
                bs_ = 4 * g + b
                for n in range(NPG):
                    if br == "fox":
                        src, rows = fox_cache[:, b * NPG + n, pr * P:(pr + 1) * P], P
                    elif br == "sel":
                        src, rows = nsa_cache[:, bs_ * NPG + n, 2 * DH:3 * DH], DH
                    else:
                        src, rows = win_cache[:, bs_, n, 0:DH], DH
                    ins = nc.tensor.transpose(psum[4 + k % 2][0:rows, n * P:(n + 1) * P], src, ident[:])
                ins.then_inc(kt_turned, 1)

            def score_keys(k):
                u, b, pr = units[k]
                br, g = sjobs[u]
                S = psum[2 * (u % 2)][32 * b:32 * b + 32, :]
                pe.wait_ge(kt_act if k % 2 else kt_dve, k // 2 + 1)
                if br == "fox":
                    ins = nc.tensor.matmul(S, foxS_q[:, pr, 4 * g + b].rearrange("p h t -> p (h t)"), KTs[:, k % 4, :],
                                           start=False, stop=(pr == 1), skip_group_check=True, tile_position=(0, 32 * b))
                else:
                    ins = nc.tensor.matmul(S, nsaS_q[:, 4 * g + b].rearrange("p h t -> p (h t)"), KTs[0:DH, k % 4, :],
                                           start=True, stop=(br == "sel"), skip_group_check=True,
                                           tile_position=(0, 32 * b))
                ins.then_inc(kt_used, 1)

            def new_scores(u):
                br, g = sjobs[u]
                S, Sn = psum[2 * (u % 2)], psum[2 * (u % 2) + 1][:, 0:NS]
                if u >= 2:
                    pe.wait_ge(sp_ready, u - 1)
                rows = slice(4 * g, 4 * g + 4)
                if br == "fox":
                    for n in range(NPG - 1, -1, -1):
                        w = (n + 1) * P
                        nc.tensor.matmul(S[:, 0:w], lf_rep[:, g, n, :], later[:, PAST - w:PAST],
                                         start=(n == NPG - 1), stop=False, skip_group_check=True)
                    for c in range(0, PAST, P):
                        nc.tensor.matmul(S[:, c:c + P], lf_new[:, g, :], ones[0:NS, :],
                                         start=False, stop=False, skip_group_check=True)
                    nc.tensor.matmul(Sn, lf_new[:, g, :], later[0:NS, PAST - P:PAST - P + NS], start=True, stop=False,
                                     skip_group_check=True)
                    for pr in range(2):
                        nc.tensor.matmul(Sn, foxS_q[:, pr, rows].rearrange("p b h t -> p (b h t)"), foxS_k[:, pr, :],
                                         start=False, stop=False, skip_group_check=True)
                else:
                    kT = selT_k if br == "sel" else winT_k
                    nc.tensor.matmul(Sn, nsaS_q[:, rows].rearrange("p b h t -> p (b h t)"), kT[:, SEQ:SEQ + NS],
                                     start=True, stop=False, skip_group_check=True)

            def cmp_sample_scores(u):
                g = sjobs[u][1]
                if u >= 2:
                    pe.wait_ge(sp_ready, u - 1)
                for b in range(4):
                    u0 = U_P + U_S * (4 * g + b)
                    ins = nc.tensor.matmul(psum[2 * (u % 2)][32 * b:32 * b + 32, 0:NC_S],
                                           nsaS_q[:, 4 * g + b].rearrange("p h t -> p (h t)"),
                                           cmpT_k[:, u0:u0 + NC_S], start=True, stop=True, tile_position=(0, 32 * b))
                ins.then_inc(ss_ready, 1)

            def turn_sample_p(u):
                br = sjobs[u][0]
                pe.wait_ge(sp_ready, u + 1)
                if u >= 1:
                    pe.wait_ge(spt_ready, u)
                    pe.wait_ge(so_done, u)
                if u == 0:
                    pe.wait_ge(s_setup, 2)
                if br == "cmp":
                    ins = nc.tensor.transpose(psum[6][0:NC_S, 0:P], Ps[:, u % 2, 0:NC_S], ident[:])
                else:
                    for n in range(NPG):
                        nc.tensor.transpose(psum[6][:, n * P:(n + 1) * P], Ps[:, u % 2, n * P:(n + 1) * P], ident[:])
                    ins = nc.tensor.transpose(psum[7][0:NS, 0:P], Ps[:, u % 2, PAST:SW], ident[:])
                ins.then_inc(sp_turned, 1)

            def sample_p_times_v(u):
                br, g = sjobs[u]
                pe.wait_ge(spt_ready, u + 1)
                if u >= 1:
                    pe.wait_ge(so_done, u)
                w = GW if br == "fox" else DH
                O = psum[7][:, 256:256 + w]
                if br != "cmp":
                    v = fox_v[0:NS, NT, :] if br == "fox" else nsa_rows[0:NS, NT, (3 if br == "sel" else 5) * DH:][:, 0:DH]
                    nc.tensor.matmul(O, PTs[0:NS, NPG, :], v, start=True, stop=False, skip_group_check=True)
                for b in range(4):
                    Ob, bs_ = O[32 * b:32 * b + 32, :], 4 * g + b
                    if br == "cmp":
                        ins = nc.tensor.matmul(Ob, PTs[0:NC_S, 0, 32 * b:32 * b + 32], cmp_v_s[0:NC_S, bs_, :],
                                               start=True, stop=True, tile_position=(0, 32 * b))
                        continue
                    for n in range(NPG):
                        if br == "fox":
                            v = fox_cache[:, b * NPG + n, GW:2 * GW]
                        elif br == "sel":
                            v = nsa_cache[:, bs_ * NPG + n, 3 * DH:4 * DH]
                        else:
                            v = win_cache[:, bs_, n, DH:2 * DH]
                        ins = nc.tensor.matmul(Ob, PTs[:, n, 32 * b:32 * b + 32], v, start=False, stop=(n == NPG - 1),
                                               skip_group_check=True, tile_position=(0, 32 * b))
                ins.then_inc(so_ready, 1)

            k = 0
            for u, (br, g) in enumerate(sjobs):
                mine = [i for i, x in enumerate(units) if x[0] == u]
                if br == "cmp":
                    cmp_sample_scores(u)
                else:
                    if u == 0:
                        pe.wait_ge(s_masks, 8 * NPG)
                    turn_keys(mine[0])
                    new_scores(u)
                    if u >= 1:
                        turn_sample_p(u - 1)
                    for i in mine:
                        if i + 1 in mine:
                            turn_keys(i + 1)
                        score_keys(i)
                    if br == "win":
                        nc.tensor.matmul(psum[2 * (u % 2)][:, 0:TN], spread_bf[:, g, :], left_m[:],
                                         start=False, stop=True, skip_group_check=True)
                    nc.tensor.matmul(psum[2 * (u % 2) + 1][:, 0:NS], spread_bf[:, g, :], new_m[:],
                                     start=False, stop=True, skip_group_check=True).then_inc(ss_ready, 1)
                if u >= 1:
                    if br == "cmp":
                        turn_sample_p(u - 1)
                    sample_p_times_v(u - 1)
            turn_sample_p(len(sjobs) - 1)
            sample_p_times_v(len(sjobs) - 1)
            pe.wait_ge(om_ready, 2)
            pe.wait_ge(so_done, len(sjobs))
            for i in range(2):
                for g in range(2):
                    ins = nc.tensor.matmul(psum[i][0:NS, 0:GW], gather[:, g, :], o_m[:, 2 * i + g, :],
                                           start=(g == 0), stop=(g == 1))
            ins.then_inc(ys_ready, 1)

            def logits(t):
                n = rows_of[t]
                if t == 0:
                    pe.wait_ge(router_in, 16)
                pe.wait_ge(x1T_dve, t + 1)
                pe.wait_ge(x1T_act, t + 1)
                for k in range(KD):
                    ins = nc.tensor.matmul(psum[5][0:n, 2 * P + t * NE:2 * P + (t + 1) * NE], x1T[:, k, tok0(t):tok0(t) + n],
                                           w_r[:, k, :], start=(k == 0), stop=(k == KD - 1))
                if t == TILES - 1:
                    ins.then_inc(logits_done, 1)

            def turn_mix(t):
                n = rows_of[t]
                if t == 0:
                    pe.wait_ge(kt_act, len(units) // 2)
                    pe.wait_ge(kt_dve, len(units) // 2)
                else:
                    pe.wait_ge(mix_dve, t)
                    pe.wait_ge(mix_act, t)
                if t == NT:
                    pe.wait_ge(ys_copied, 1)
                if t >= 4:
                    logits(t - 4)
                srcs = [uv[0:n, t, i * P:(i + 1) * P] for i in range(4)] + [fox_v[0:n, t, i * P:(i + 1) * P] for i in range(2)]
                for k, src in enumerate(srcs):
                    ins = nc.tensor.transpose(psum[4 + k // 4][:, (k % 4) * P:(k % 4) * P + n], src, ident[0:n, 0:n])
                ins.then_inc(mix_turned, 1)

            def mix_out(t):
                n = rows_of[t]
                if t == 0:
                    pe.wait_ge(wo_in, 16)
                    pe.wait_ge(ys_copied, 1)
                pe.wait_ge(mix_dve, t + 1)
                pe.wait_ge(mix_act, t + 1)
                if t >= 2:
                    pe.wait_ge(std_ready, t - 1)
                order = [(i, k) for i in range(2) for k in range(KD)] if t < NT else [(i, k) for k in range(KD) for i in range(2)]
                for i, k in order:
                    lhs = mix_T[:, t % 2, k, 0:n] if k < 6 else yd_T[:, k - 6, tok0(t):tok0(t) + n]
                    p0 = NS * i if t == NT else 0
                    ins = nc.tensor.matmul(psum[2 * (t % 2) + i][p0:p0 + n, :], lhs, wo[:, k, i * 512:(i + 1) * 512],
                                           start=(k == 0), stop=(k == KD - 1), tile_position=(0, p0) if t == NT else None,
                                           skip_group_check=(t == NT))
                ins.then_inc(r_done, 1)

            def turn_x1(t):
                n = rows_of[t]
                pe.wait_ge(normed, t + 1)
                if t:
                    pe.wait_ge(x1T_dve, t)
                    pe.wait_ge(x1T_act, t)
                for k in range(KD):
                    ins = nc.tensor.transpose(psum[6 + k // 4][:, (k % 4) * P:(k % 4) * P + n],
                                              layer[0:n, t, k * P:(k + 1) * P], ident[0:n, 0:n])
                ins.then_inc(x1_turned, 1)

            turn_mix(0)
            for t in range(TILES):
                if t + 1 < TILES:
                    turn_mix(t + 1)
                mix_out(t)
                if t >= 1:
                    turn_x1(t - 1)
            pe.wait_ge(mix_act, TILES)
            for t in range(TILES - 4, TILES - 1):
                logits(t)
            turn_x1(TILES - 1)
            logits(TILES - 1)

            pe.wait_ge(picked_ready, 1)
            nc.tensor.matmul(psum[5][:, 0:(TILES + 1) * NE], tri_bf[:], picked[:].rearrange("p t e -> p (t e)"),
                             start=True, stop=False)
            for t in range(TILES):
                ins = nc.tensor.matmul(psum[5][:, (t + 1) * NE:(TILES + 1) * NE].rearrange("p (t e) -> p t e", e=NE), ones_bf[:],
                                       picked[:, t:t + 1, :].to_broadcast([P, TILES - t, NE]),
                                       start=False, stop=(t == TILES - 1))
            ins.then_inc(ranked, 1)
            pe.wait_ge(hots_ready, 1)
            for j in range(TOP_K * TILES):
                ins = nc.tensor.matmul(psum[6][:, 0:2 * NSL], lo_hot[:, j, :], slot_vals[:, j, :],
                                       start=(j == 0), stop=(j == TOP_K * TILES - 1))
                if j == 0:
                    ins.then_inc(down_done, 1)
            ins.then_inc(slots_done, 1)

            def turn_slots(n_in):
                pe.wait_ge(xs_in, n_in)
                for k in range(KD):
                    ins = nc.tensor.transpose(psum[4 + k // 4][:, (k % 4) * P:(k % 4 + 1) * P],
                                              x_slot[:, k * P:(k + 1) * P], ident[:])
                    if k % 4 == 3:
                        ins.then_inc(xs_turned, 1)

            def weights_of(t):
                e = pe.value_load(table[0:1, bass.ds(t, 1)], min_val=0, max_val=NE - 1)
                return (e % N_EW) * (R_EW[1] - R_EW[0]) + R_EW[0], e

            def down(w_at, n):
                pe.wait_ge(hT_ready, n)
                if not isinstance(n, int) or n > 1:
                    pe.wait_ge(y_dve, n - 1)
                for half in range(2):
                    for f in range(F // P):
                        ins = nc.tensor.matmul(psum[2 + half][:], h_T[:, f, :],
                                               arena[:, bass.ds(w_at + (KD * 2 * F + f * D + half * 512), 512)],
                                               start=(f == 0), stop=(f == F // P - 1))
                ins.then_inc(down_done, 1)

            def slot_tile(t):
                w_at, e = weights_of(t)
                for i in range(N_EW):
                    pe.wait_ge(ew_in[i], ((e + (N_EW - i)) // N_EW) * 48 + EW_FIRST[i])
                pe.wait_ge(xs_dve, t + 1)
                pe.wait_ge(xs_act, t + 1)
                for k in range(KD):
                    ins = nc.tensor.matmul(psum[0][:], xT_slot[:, k, :], arena[:, bass.ds(w_at + k * 2 * F, 2 * F)],
                                           start=(k == 0), stop=(k == KD - 1))
                ins.then_inc(hid_done, 1)
                turn_slots(t * 16 + 32)
                if not isinstance(t, int) or t > 0:
                    down(weights_of(t - 1)[0], t)
                pe.wait_ge(h_ready, t + 1)
                for f in range(F // P):
                    ins = nc.tensor.transpose(psum[6][:, f * P:(f + 1) * P], h_row[:, f * P:(f + 1) * P], ident[:])
                ins.then_inc(h_turned, 1)

            pe.wait_ge(slots_ready, 1)
            last = last_tile(pe)
            turn_slots(16)
            slot_tile(0)
            with pe.Fori(1, last + 1) as t:
                slot_tile(t)
            down(weights_of(last)[0], last + 1)

        @block.vector
        def _(dve):
            steps = [0]

            def link(ins):
                steps[0] += 1
                ins.then_inc(dve_step, 1)
                dve.wait_ge(dve_step, steps[0])

            nc.vector.memset(lnc[:, 0:1], LN_EPS).then_inc(var_ready, 1)
            nc.vector.memset(lnc[:, 1:2], 1.0)
            nc.vector.memset(ln_stat[:], 1.0)
            nc.vector.memset(b_f[:], 0.0)
            nc.vector.memset(nsa_rows[NS:P, NT, :], 0.0)

            def center_v(t):
                n = rows_of[t]
                dve.wait_ge(proj_copied, t + 1)
                v = uv[0:n, t, GW:2 * GW].rearrange("p (h d) -> p h d", h=H)
                sq = ln_sq[0:n, :].rearrange("p (h d) -> p h d", h=H)
                m = ln_stat[0:n, t, :, 0]
                link(nc.vector.tensor_reduce(m, v, AX.X, ALU.add))
                link(nc.vector.tensor_scalar(m, m, 1.0 / DH, None, ALU.mult))
                link(nc.vector.tensor_tensor(v, v, m.unsqueeze(2).to_broadcast([n, H, DH]), ALU.subtract))
                link(nc.vector.tensor_tensor(sq, v, v, ALU.mult))
                link(nc.vector.tensor_reduce(ln_stat[0:n, t, :, 1], sq, AX.X, ALU.add))
                nc.vector.tensor_scalar(ln_stat[0:n, t, :, 1], ln_stat[0:n, t, :, 1], 1.0 / DH, None,
                                        ALU.mult).then_inc(var_ready, 1)

            def scale_v(t):
                n = rows_of[t]
                v = uv[0:n, t, GW:2 * GW].rearrange("p (h d) -> p h d", h=H)
                r = ln_stat[0:n, t, :, 1]
                nc.vector.tensor_tensor(v, v, r.unsqueeze(2).to_broadcast([n, H, DH]), ALU.mult).then_inc(v_ready, 1)

            def copy_x(t):
                n = rows_of[t]
                dve.wait_ge(turned, t + 1)
                for i in range(2):
                    ins = nc.vector.tensor_copy(
                        xT[:, 4 * i:4 * i + 4, tok0(t):tok0(t) + n],
                        psum[4 + 2 * (t % 2) + i][:].rearrange("p (k n) -> p k n", k=4)[:, :, 0:n])
                ins.then_inc(turn_copied, 1)

            def copy_turned(g, t):
                e = {1: 1, 3: 2, 4: 3}[g] * TILES + t
                A, B = psum[4 + 2 * (e % 2)], psum[5 + 2 * (e % 2)]
                dve.wait_ge(turned, e + 1)
                ts = slice(tok0(t), tok0(t) + rows_of[t])
                av = A[0:DH, :].rearrange("p (h n) -> p h n", h=H)
                if g == 1 and t < NT:
                    nc.vector.tensor_scalar(foxT_q[0:DH, :, ts], av, SCALE, None, ALU.mult)
                    ins = nc.vector.tensor_copy(foxT_k[0:DH, :, ts], B[0:DH, :].rearrange("p (h n) -> p h n", h=H))
                elif g == 1:
                    for pair in range(2):
                        for i in range(2):
                            q = slice(DH * i, DH * i + DH)
                            nc.vector.tensor_scalar(foxS_q[q, pair, :, 2 * pair + i, :],
                                                    A[q, pair * P:pair * P + NS].rearrange("p (b t) -> p b t", b=NB),
                                                    SCALE, None, ALU.mult)
                    ins = nc.vector.tensor_copy(foxS_k[:], B[:, 0:2 * P].rearrange("p (i n) -> p i n", i=2)[:, :, 0:NS])
                elif g == 3 and t < NT:
                    ins = nc.vector.tensor_scalar(nsaT_q[:, :, ts], av, SCALE, None, ALU.mult)
                elif g == 3:
                    ins = nc.vector.tensor_scalar(nsaS_q[:].rearrange("p b h t -> p h b t"),
                                                  av[:, :, 0:NS].rearrange("p h (b t) -> p h b t", b=NB),
                                                  SCALE, None, ALU.mult)
                else:
                    nc.vector.tensor_copy(selT_k[:, ts], A[0:DH, 0:rows_of[t]])
                    ins = nc.vector.tensor_copy(winT_k[:, ts], A[0:DH, P:P + rows_of[t]])
                ins.then_inc(turn_copied, 1)

            def gate_u(t):
                n = rows_of[t]
                i = 0 if t < NT else 1
                dve.wait_ge(zg_done, t + 1)
                if t:
                    dve.wait_ge(zg_used, t)
                z = psum[4 + t % 2][0:n, 0:GW].rearrange("p (h d) -> p h d", h=H)
                b = bs[0:n, i, :].unsqueeze(2).to_broadcast([n, H, DH])
                sq = ln_sq[0:n, :].rearrange("p (h d) -> p h d", h=H)
                link(nc.vector.tensor_tensor(sq, z, b, ALU.add))
                u = uv[0:n, t, 0:GW]
                nc.vector.tensor_tensor(u, u, ln_sq[0:n, :], ALU.mult).then_inc(zg_used, 1)

            for t in range(TILES):
                copy_x(t)
                if t == 1:
                    nc.vector.memset(foxT_q[DH:DH + 2, :, :], 1.0)
                    nc.vector.memset(foxS_q[:], 0.0)
                if t == 2:
                    nc.vector.memset(foxT_k[DH:DH + 2, :, :], 1.0)
                if t >= 2:
                    center_v(t - 2)
            dve.wait_ge(ws_turned, 1)
            nc.vector.tensor_copy(ws_T[:], psum[6][:].rearrange("p (h n) -> p h n", h=H)).then_inc(ws_copied, 1)
            center_v(TILES - 2)
            center_v(TILES - 1)
            copy_turned(1, 0)
            dve.wait_ge(rstd_ready, 1)
            dve.wait_ge(small_loaded, 16 * (1 + NB + 1 + 2 + 2 * NB))
            for t in range(TILES):
                scale_v(t)
                if t + 1 < TILES:
                    copy_turned(1, t + 1)
            for t in range(TILES):
                gate_u(t)
            for t in range(TILES):
                if t == 1:
                    dve.wait_ge(proj_copied, 3 * TILES)
                    nc.vector.tensor_tensor(lf_x[:], b_f[:], bias_f[:].unsqueeze(2).to_broadcast([P, H, TILES]),
                                            ALU.add).then_inc(x_biased, 1)
                if t == 3:
                    dve.wait_ge(lf_parts, 3)
                    dve.wait_ge(x_biased, 1)
                    nc.vector.scalar_tensor_tensor(out=lf[:], in0=lf_x[:], scalar=0.0, in1=lf_e[:],
                                                   op0=ALU.min, op1=ALU.subtract).then_inc(lf_ready, 1)
                    dve.wait_ge(lf_ready, 1)
                    nc.vector.tensor_copy(lf_rows[:].rearrange("p t h -> p h t"), lf[:]).then_inc(lf_ready, 1)
                if t == TILES - 1:
                    link(nc.vector.memset(carry[:, :, 0], 0.0))
                    dve.wait_ge(cum_done, 1)
                    tot = psum[5][:, 64:64 + H * NT].rearrange("p (h t) -> p h t", h=H)
                    for i in range(1, NT):
                        link(nc.vector.tensor_tensor(carry[:, :, i], carry[:, :, i - 1], tot[:, :, i - 1], ALU.add))
                    nc.vector.tensor_tensor(cum[:], psum[5][:, 0:H * NT].rearrange("p (h t) -> p h t", h=H),
                                            carry[:], ALU.add).then_inc(c_ready, 1)
                copy_turned(3, t)
            for t in range(TILES):
                copy_turned(4, t)
                if t == 0:
                    dve.wait_ge(cT_done, 1)
                    nc.vector.tensor_copy(cum_T[:, 0, :], psum[7][0:H * NT, 0:P])
                    nc.vector.tensor_scalar(cum_T[:, 1, :], psum[7][0:H * NT, 0:P], -1.0, None,
                                            ALU.mult).then_inc(cT_copied, 1)
            gv = gates[:].rearrange("p t b h -> p (t b h)")
            dve.wait_ge(gate_x, 1)
            link(nc.vector.tensor_scalar(gv, gv, 1.0, None, ALU.add))
            nc.vector.reciprocal(gv, gv).then_inc(gates_ready, 1)
            dve.wait_ge(turned, 3 * TILES)
            dve.wait_ge(k_stored[0], 16 * ((TILES + 1) // 2))
            dve.wait_ge(k_stored[1], 16 * (TILES // 2))
            link(nc.vector.memset(z_p[:, :, 0:2], 0.0))
            for f in range(2):
                j0 = N_ROWJ + 9 * f
                for c, (c0, cn) in enumerate(CHUNKS):
                    dve.wait_ge(proj_copied, N_ROWJ + 3 * f + c + 1)
                    dve.wait_ge(proj_done, j0 + 4 + c)
                    src = psum[(j0 + 3 + c) % 4][:, 0:cn]
                    dh = dh_T[c]
                    if c0 < SEQ:
                        dst = z_p[:, f, 2 + c0:2 + c0 + cn]
                    else:
                        dst = z_s[:, f, :, 2:2 + TN]
                        src = src.rearrange("p (b t) -> p b t", b=NB)
                        dh = dh.rearrange("p (b t) -> p b t", b=NB)
                    ins = nc.vector.tensor_tensor(dst, src, dh, ALU.mult)
                    ins.then_inc(z_used, 1)
                dve.wait_ge(z_used, 6 * f + 3)
                for c, (c0, cn) in enumerate(CHUNKS):
                    dve.wait_ge(proj_done, j0 + 7 + c)
                    dve.wait_ge(z_used, 6 * f + 3 + c)
                    if c0 < SEQ:
                        sh = [z_p[:, f, c0 + i:c0 + i + cn] for i in range(3)]
                        y, out = conv_y[:, 0:cn], yd_T[:, f, c0:c0 + cn]
                        ps = psum[(j0 + 6 + c) % 4][:, 0:cn]
                    else:
                        sh = [z_s[:, f, :, i:i + TN] for i in range(3)]
                        y, out, ps = [a.rearrange("p (b t) -> p b t", b=NB) for a in (
                            conv_y[:, 0:cn], yd_T[:, f, c0:c0 + cn], psum[(j0 + 6 + c) % 4][:, 0:cn])]
                    link(nc.vector.tensor_scalar(y, sh[0], cw[:, f, 0:1], None, ALU.mult))
                    link(nc.vector.scalar_tensor_tensor(out=y, in0=sh[1], scalar=cw[:, f, 1:2], in1=y,
                                                        op0=ALU.mult, op1=ALU.add))
                    link(nc.vector.scalar_tensor_tensor(out=y, in0=sh[2], scalar=cw[:, f, 2:3], in1=y,
                                                        op0=ALU.mult, op1=ALU.add))
                    nc.vector.tensor_tensor(out, ps, y, ALU.mult).then_inc(z_used, 1)
                dve.wait_ge(z_used, 6 * f + 6)

            dve.wait_ge(gates_ready, 1)

            def row_max(i):
                n = keys_of(i)[1]
                dve.wait_ge(s_ready, i + 1)
                if i >= 4:
                    dve.wait_ge(p_ready, i - 3)
                nc.vector.tensor_reduce(neg_max[:, i % 4:i % 4 + 1], banks(2 * (i % 2), 2)[:, 0:n * P], AX.X,
                                        ALU.max, negate=True).then_inc(max_ready, 1)

            def copy_pt_dve(i):
                n = min(4, keys_of(i)[1])
                dve.wait_ge(p_turned, i + 1)
                if i >= 2:
                    dve.wait_ge(o_ready, i - 1)
                nc.vector.tensor_copy(PT_buf[:, i % 2, 0:n * P], psum[4][:, 0:n * P]).then_inc(pt_dve, 1)

            def finish(i):
                br, qt, h = jobs[i]
                dve.wait_ge(o_ready, i + 1)
                s = slice(i % 4, i % 4 + 1)
                link(nc.vector.reciprocal(recip[:, s], row_sum[:, s]))
                O = psum[6 + i % 2][:, 0:DH]
                if br == "fox":
                    ins = nc.vector.tensor_scalar(uv[:, qt, GW + h * DH:GW + (h + 1) * DH], O, recip[:, s], None, ALU.mult)
                else:
                    b = 1 if br == "sel" else 2
                    link(nc.vector.tensor_tensor(coef[:, s], recip[:, s], gates[:, qt, b, h:h + 1], ALU.mult))
                    y = fox_v[:, qt, h * DH:(h + 1) * DH]
                    if br == "sel":
                        ins = nc.vector.tensor_scalar(y, O, coef[:, s], None, ALU.mult)
                    else:
                        ins = nc.vector.scalar_tensor_tensor(out=y, in0=O, scalar=coef[:, s], in1=y,
                                                             op0=ALU.mult, op1=ALU.add)
                ins.then_inc(y_done, 1)

            for i in range(J + 2):
                if i < J:
                    row_max(i)
                if 1 <= i <= J:
                    copy_pt_dve(i - 1)
                if i >= 2:
                    finish(i - 2)

            dve.wait_ge(pe_turned, 1)
            copy_units(nc.vector.tensor_copy, psum[6][:, 0:CMP_LEN], NU).then_inc(pe_copied, 1)
            for q in range(0, 2 + NB, 2):
                dve.wait_ge(cc_turned, q + 1)
                bank_units(nc.vector.tensor_copy, q).then_inc(cc_dve, 1)

            dve.wait_ge(masks_ready, 11)
            nc.vector.tensor_scalar(new_m[:], same[:], -NEG, NEG, ALU.mult, ALU.add)
            link(nc.vector.tensor_reduce(left_f[:], same[:].rearrange("p (b t) -> p t b", b=NB), AX.X, ALU.add))
            nc.vector.tensor_scalar(left_m[:], left_f[:], NEG, None, ALU.mult)
            nc.vector.tensor_copy(spread_bf[:], spread[:])
            link(nc.vector.tensor_reduce(head_m[:], ident[:].rearrange("p (b h t) -> p h b t", b=4, h=H), AX.XY, ALU.add))
            dve.wait_ge(lf_ready, 2)
            for g in range(2):
                v = lf_new[:, g, :].rearrange("p (b h t) -> p b h t", b=4, h=H)
                for b in range(4):
                    nc.vector.tensor_tensor(v[:, b], v[:, b], lf[0:NS, :, NT:NT + 1].to_broadcast([NS, H, TN]), ALU.mult)
            dve.wait_ge(lf_past_in, 16 * NB * NPG)
            dve.wait_ge(conv_stored, 16 * 2 * (1 + NB))
            for g in range(2):
                for n in range(NPG):
                    for b in range(4):
                        nc.vector.tensor_copy(
                            lf_rep[:, g, n, 32 * b:32 * b + 32].rearrange("p (h t) -> p h t", h=H),
                            lf_past[:, (4 * g + b) * NPG + n, :].unsqueeze(2).to_broadcast([P, H, TN])
                            ).then_inc(s_masks, 1)
            def by_head(v):
                return v.unsqueeze(2)

            def cmp_shift(qt):
                dve.wait_ge(c_scored, qt + 1)
                if qt >= 2:
                    dve.wait_ge(c_turned, qt - 1)
                S = psum[2 + qt % 2][:, 0:H * NC_P].rearrange("p (h n) -> p h n", h=H)
                m = head_v[:, 0, :]
                if qt:
                    dve.wait_ge(c_shifted, qt)
                link(nc.vector.tensor_reduce(m, S, AX.X, ALU.max, negate=True))
                nc.vector.tensor_tensor(P_buf[:, qt % 2, 0:H * NC_P].rearrange("p (h n) -> p h n", h=H), S,
                                        by_head(m).to_broadcast([P, H, NC_P]), ALU.add).then_inc(c_shifted, 1)

            def cmp_sum(qt):
                dve.wait_ge(c_exp, qt + 1)
                if qt >= 2:
                    dve.wait_ge(c_added, qt - 1)
                s, r = head_v[:, 1, :], head_v[:, 2 + qt % 2, :]
                link(nc.vector.tensor_reduce(s, P_buf[:, qt % 2, 0:H * NC_P].rearrange("p (h n) -> p h n", h=H), AX.X, ALU.add))
                link(nc.vector.reciprocal(s, s))
                link(nc.vector.tensor_tensor(r, s, gates[:, qt, 0, :], ALU.mult))
                if qt == 0:
                    link(nc.vector.tensor_scalar(r, r, any_cmp[:, 0:1], None, ALU.mult))

            def cmp_add(qt):
                dve.wait_ge(c_out, qt + 1)
                if qt:
                    dve.wait_ge(c_added, qt)
                t = P_buf[:, 0, 512:512 + GW]
                O = psum[6 + qt % 2][:, 0:GW].rearrange("p (h d) -> p h d", h=H)
                link(nc.vector.tensor_tensor(t.rearrange("p (h d) -> p h d", h=H), O,
                                             by_head(head_v[:, 2 + qt % 2, :]).to_broadcast([P, H, DH]), ALU.mult))
                nc.vector.tensor_tensor(fox_v[:, qt, :], fox_v[:, qt, :], t, ALU.add).then_inc(c_added, 1)

            dve.wait_ge(masks_ready, 11)
            for qt in range(NT + 2):
                if qt < NT:
                    cmp_shift(qt)
                if 1 <= qt <= NT:
                    cmp_sum(qt - 1)
                if qt >= 2:
                    cmp_add(qt - 2)

            dve.wait_ge(s_ops, 1)
            link(nc.vector.tensor_copy(gather[:], psum[6][:, 0:2 * NS].rearrange("p (g n) -> p g n", g=2)))
            for g in range(2):
                link(nc.vector.tensor_tensor(gate_t[:], psum[7][:, 16 * g:16 * g + 12].rearrange("p (b h) -> p b h", b=3),
                                             head_m[:].unsqueeze(1).to_broadcast([P, 3, H]), ALU.mult))
                nc.vector.tensor_reduce(gate_s[:, g, :], gate_t[:], AX.X, ALU.add).then_inc(s_setup, 1)
                dve.wait_ge(s_setup, g + 1)

            def sample_finish(u):
                br, g = sjobs[u]
                dve.wait_ge(so_ready, u + 1)
                st = s_stat[:, u % 2, :]
                link(nc.vector.reciprocal(st[:, 2:3], st[:, 1:2]))
                if br == "fox":
                    c = o_coef[:, g, :]
                    link(nc.vector.tensor_scalar(c, head_m[:], st[:, 2:3], None, ALU.mult))
                    nc.vector.tensor_tensor(o_m[:, g, :].rearrange("p (h d) -> p h d", h=H),
                                            psum[7][:, 256:512].rearrange("p (h d) -> p h d", h=H),
                                            c.unsqueeze(2).to_broadcast([P, H, DH]), ALU.mult).then_inc(so_done, 1)
                    return
                i = {"cmp": 0, "sel": 1, "win": 2}[br]
                link(nc.vector.tensor_tensor(st[:, 3:4], st[:, 2:3], gate_s[:, g, i:i + 1], ALU.mult))
                O, y = psum[7][:, 256:256 + DH], o_nsa[:, g, :]
                if br == "sel":
                    nc.vector.tensor_scalar(y, O, st[:, 3:4], None, ALU.mult).then_inc(so_done, 1)
                else:
                    nc.vector.scalar_tensor_tensor(out=y, in0=O, scalar=st[:, 3:4], in1=y, op0=ALU.mult, op1=ALU.add
                                                   ).then_inc(so_done, 1)
                dve.wait_ge(so_done, u + 1)
                if br == "cmp":
                    nc.vector.tensor_tensor(o_m[:, 2 + g, :].rearrange("p (h d) -> p h d", h=H),
                                            y.unsqueeze(1).to_broadcast([P, H, DH]),
                                            head_m[:].unsqueeze(2).to_broadcast([P, H, DH]), ALU.mult
                                            ).then_inc(om_ready, 1)

            def copy_sample_pt(u):
                dve.wait_ge(sp_turned, u + 1)
                if u >= 1:
                    dve.wait_ge(so_ready, u)
                if sjobs[u][0] == "cmp":
                    nc.vector.tensor_copy(PTs[0:NC_S, 0, :], psum[6][0:NC_S, 0:P]).then_inc(spt_ready, 1)
                else:
                    nc.vector.tensor_copy(PTs[:, 0:NPG, :], psum[6][:].rearrange("p (n k) -> p n k", n=NPG))
                    nc.vector.tensor_copy(PTs[0:NS, NPG, :], psum[7][0:NS, 0:P]).then_inc(spt_ready, 1)

            k = 0
            for u, (br, g) in enumerate(sjobs):
                first = True
                while k < len(units) and units[k][0] == u:
                    if k % 2 == 0:
                        copy_keys(dve, nc.vector.tensor_copy, k).then_inc(kt_dve, 1)
                        if first and u >= 1:
                            copy_sample_pt(u - 1)
                        first = False
                    k += 1
                if first and u >= 1:
                    copy_sample_pt(u - 1)
                dve.wait_ge(ss_ready, u + 1)
                if u >= 2:
                    dve.wait_ge(sp_ready, u - 1)
                w = NC_S if br == "cmp" else SW
                nc.vector.tensor_reduce(s_stat[:, u % 2, 0:1], banks(2 * (u % 2), 2)[:, 0:w], AX.X, ALU.max, negate=True
                                        ).then_inc(smax_ready, 1)
                if u >= 1:
                    sample_finish(u - 1)
            copy_sample_pt(len(sjobs) - 1)
            sample_finish(len(sjobs) - 1)
            dve.wait_ge(ys_ready, 1)
            nc.vector.tensor_copy(uv[0:NS, NT, GW:2 * GW], psum[0][0:NS, 0:GW])
            nc.vector.tensor_copy(fox_v[0:NS, NT, :], psum[1][0:NS, 0:GW]).then_inc(ys_copied, 1)

            def add_residual(t):
                n = rows_of[t]
                dve.wait_ge(r_done, t + 1)
                dve.wait_ge(x_res_in[t % 2], 16 * (t // 2 + 1))
                st = ln_s[0:n, t % 2, :]
                if t >= 2:
                    dve.wait_ge(normed, t - 1)
                if t < NT:
                    link(nc.vector.scalar_tensor_tensor(out=layer[0:n, t, :], in0=x_res[0:n, t % 2, :], scalar=ALPHA,
                                                        in1=banks(2 * (t % 2), 2)[0:n, :], op0=ALU.mult, op1=ALU.add,
                                                        accum_out=st[:, 0:1]))
                else:
                    for i in range(2):
                        cols = slice(i * 512, (i + 1) * 512)
                        link(nc.vector.scalar_tensor_tensor(out=layer[0:n, t, cols], in0=x_res[0:n, t % 2, cols],
                                                            scalar=ALPHA, in1=psum[2 * (t % 2) + i][NS * i:NS * i + n, :],
                                                            op0=ALU.mult, op1=ALU.add, accum_out=st[:, i:i + 1]))
                    link(nc.vector.tensor_tensor(st[:, 0:1], st[:, 0:1], st[:, 1:2], ALU.add))
                nc.vector.tensor_scalar(st[:, 1:2], st[:, 0:1], -1.0 / D, None, ALU.mult).then_inc(mean_ready, 1)

            def norm(t):
                n = rows_of[t]
                st, v = ln_s[0:n, t % 2, :], layer[0:n, t, :]
                dve.wait_ge(std_ready, t + 1)
                link(nc.vector.reciprocal(st[:, 3:4], st[:, 2:3]))
                if t == 0:
                    dve.wait_ge(ew_in[1], EW_FIRST[1])
                    dve.wait_ge(ew_in[2], EW_FIRST[2])
                link(nc.vector.scalar_tensor_tensor(out=v, in0=v, scalar=st[:, 1:2], in1=ln_row[0][0:n, 0, :],
                                                    op0=ALU.add, op1=ALU.mult))
                nc.vector.scalar_tensor_tensor(out=v, in0=v, scalar=st[:, 3:4], in1=ln_row[0][0:n, 1, :],
                                               op0=ALU.mult, op1=ALU.add).then_inc(normed, 1)

            def copy_mix(t):
                n = rows_of[t]
                dve.wait_ge(mix_turned, t + 1)
                if t >= 2:
                    dve.wait_ge(r_done, t - 1)
                nc.vector.tensor_copy(mix_T[:, t % 2, 0:4, 0:n], psum[4][:].rearrange("p (k n) -> p k n", k=4)[:, :, 0:n]
                                      ).then_inc(mix_dve, 1)

            def copy_x1T(t):
                n = rows_of[t]
                dve.wait_ge(x1_turned, t + 1)
                nc.vector.tensor_copy(x1T[:, 4:8, tok0(t):tok0(t) + n],
                                      psum[7][:].rearrange("p (k n) -> p k n", k=4)[:, :, 0:n]).then_inc(x1T_dve, 1)

            copy_mix(0)
            for t in range(TILES):
                if t + 1 < TILES:
                    copy_mix(t + 1)
                add_residual(t)
                norm(t)
                if t:
                    copy_x1T(t - 1)
            copy_x1T(TILES - 1)

            V = nc.vector
            full = [P, TILES, NE]
            t16 = lambda v: v.unsqueeze(2).to_broadcast(full)
            g44 = lambda v: v.rearrange("p t (g e) -> p (t g) e", g=EG)
            f4 = lambda v: v[:].rearrange("p t g -> p (t g)")
            in_group = lambda v: f4(v).unsqueeze(2).to_broadcast([P, TILES * EG, EG])
            dve.wait_ge(masks_ready, 13)
            link(V.tensor_copy(iota_f[:], iota_i[:]))
            link(V.tensor_copy(tok_f[:], tok_i[:]))
            link(V.tensor_scalar(rank16[:], iota_f[:, 0:NE], -1.0, float(NE), ALU.mult, ALU.add))
            link(V.tensor_scalar(iota_p[:], iota_f[:, 0:NSL + 1], float(P), None, ALU.mult))
            link(V.tensor_tensor(le16[:], iota_f[:, 0:NE].unsqueeze(1).to_broadcast([P, NE, NE]),
                                 iota_f[:, 0:NE].unsqueeze(2).to_broadcast([P, NE, NE]), ALU.is_le))
            link(V.memset(picked[:, TILES, :], 0.0))
            link(V.tensor_copy(ones_bf[:], ones[:]))
            link(V.tensor_copy(tri_bf[:], tri_u[:]))
            link(V.memset(probs[:], 0.0))
            dve.wait_ge(logits_done, 1)
            link(V.tensor_copy(probs[:, 0:NT, :], psum[5][:, 2 * P:2 * P + NT * NE].rearrange("p (t e) -> p t e", t=NT)))
            link(V.tensor_copy(probs[0:NS, NT, :], psum[5][0:NS, 2 * P + NT * NE:2 * P + TILES * NE]))
            link(V.tensor_reduce(r1[0][:], probs[:], AX.X, ALU.max, negate=True))
            V.tensor_tensor(probs[:], probs[:], t16(r1[0][:]), ALU.add).then_inc(rmax_ready, 1)
            dve.wait_ge(rexp_ready, 1)
            link(V.tensor_reduce(r1[0][:], probs[:], AX.X, ALU.add))
            link(V.reciprocal(r1[0][:], r1[0][:]))
            link(V.tensor_tensor(probs[:], probs[:], t16(r1[0][:]), ALU.mult))
            sel, best = r4
            p = g44(probs[:])
            link(V.tensor_tensor(pair_sums[:, :, 0:3], p[:, :, 0:3], p[:, :, 1:4], ALU.add))
            link(V.tensor_tensor(pair_sums[:, :, 3:5], p[:, :, 0:2], p[:, :, 2:4], ALU.add))
            link(V.tensor_tensor(pair_sums[:, :, 5:6], p[:, :, 0:1], p[:, :, 3:4], ALU.add))
            link(V.tensor_reduce(f4(best), pair_sums[:], AX.X, ALU.max))
            link(V.tensor_reduce(r1[0][:], best[:], AX.X, ALU.max))
            t4 = lambda v: v.unsqueeze(2).to_broadcast([P, TILES, EG])
            rank4 = rank16[:, NE - EG:NE].unsqueeze(1).to_broadcast([P, TILES, EG])
            link(V.tensor_tensor(sel[:], best[:], t4(r1[0][:]), ALU.is_equal))
            link(V.tensor_tensor(sel[:], sel[:], rank4, ALU.mult))
            link(V.tensor_reduce(r1[0][:], sel[:], AX.X, ALU.max))
            link(V.tensor_tensor(sel[:], sel[:], t4(r1[0][:]), ALU.is_equal))
            pm, tmp = r16[0], r16[1]
            link(V.tensor_tensor(g44(pm[:]), g44(probs[:]), in_group(sel), ALU.mult))
            link(V.tensor_scalar(sel[:], sel[:], -1.0, None, ALU.add))
            link(V.tensor_tensor(g44(pm[:]), g44(pm[:]), in_group(sel), ALU.add))
            rank = rank16[:].unsqueeze(1).to_broadcast(full)
            for k in range(TOP_K):
                link(V.tensor_reduce(r1[k][:], pm[:], AX.X, ALU.max))
                link(V.tensor_tensor(tmp[:], pm[:], t16(r1[k][:]), ALU.is_equal))
                link(V.tensor_tensor(tmp[:], tmp[:], rank, ALU.mult))
                link(V.tensor_reduce(r1[2][:], tmp[:], AX.X, ALU.max))
                link(V.tensor_tensor(hot[:, k], tmp[:], t16(r1[2][:]), ALU.is_equal))
                if k == 0:
                    link(V.scalar_tensor_tensor(out=pm[:], in0=hot[:, 0], scalar=-4.0, in1=pm[:], op0=ALU.mult, op1=ALU.add))
            link(V.memset(hot[NS:P, :, NT, :], 0.0))
            V.tensor_tensor(picked[:, 0:TILES, :], hot[:, 0], hot[:, 1], ALU.add).then_inc(picked_ready, 1)
            link(V.tensor_tensor(r1[2][:], r1[0][:], r1[1][:], ALU.add))
            link(V.reciprocal(r1[2][:], r1[2][:]))
            link(V.tensor_tensor(gate2[:, 0], r1[0][:], r1[2][:], ALU.mult))
            link(V.tensor_tensor(gate2[:, 1], r1[1][:], r1[2][:], ALU.mult))

            CH2 = TOP_K * TILES
            dve.wait_ge(ranked, 1)
            counts = psum[5][:, TILES * NE:(TILES + 1) * NE]
            ranks = psum[5][:, 0:TILES * NE].rearrange("p (t e) -> p t e", e=NE)
            link(V.tensor_tensor(over[:], counts.unsqueeze(2).to_broadcast([P, NE, TILES - 1]),
                                 iota_p[:, 1:TILES].unsqueeze(1).to_broadcast([P, NE, TILES - 1]), ALU.is_gt))
            link(V.tensor_reduce(n_tiles[:], over[:], AX.X, ALU.add))
            link(V.tensor_scalar(n_tiles[:], n_tiles[:], 1.0, None, ALU.add))
            link(V.tensor_tensor(le16_x[:], le16[:], n_tiles[:].unsqueeze(1).to_broadcast([P, NE, NE]), ALU.mult))
            link(V.tensor_reduce(upto[:], le16_x[:], AX.X, ALU.add))
            link(V.tensor_tensor(n_tiles[:], upto[:], n_tiles[:], ALU.subtract))
            link(V.scalar_tensor_tensor(out=pos16[:], in0=n_tiles[:].unsqueeze(1).to_broadcast(full), scalar=float(P),
                                        in1=ranks, op0=ALU.mult, op1=ALU.add))
            link(V.tensor_tensor(pos_x[:].rearrange("p (k t) e -> p k t e", k=TOP_K), hot[:],
                                 pos16[:].unsqueeze(1).to_broadcast([P, TOP_K, TILES, NE]), ALU.mult))
            link(V.tensor_reduce(pos[:], pos_x[:], AX.X, ALU.add))
            link(V.tensor_tensor(ge_tile[:], pos[:].unsqueeze(2).to_broadcast([P, CH2, NSL + 1]),
                                 iota_p[:].unsqueeze(1).to_broadcast([P, CH2, NSL + 1]), ALU.is_gt))
            link(V.tensor_reduce(hi_cnt[:], ge_tile[:], AX.X, ALU.add))
            link(V.scalar_tensor_tensor(out=lo_pos[:], in0=hi_cnt[:], scalar=-float(P), in1=pos[:],
                                        op0=ALU.mult, op1=ALU.add))
            link(V.tensor_scalar(lo_pos[:], lo_pos[:], float(P - 1), None, ALU.add))
            link(V.tensor_tensor(lo_hot[:], lo_pos[:].unsqueeze(2).to_broadcast([P, CH2, P]),
                                 iota_f[:].unsqueeze(1).to_broadcast([P, CH2, P]), ALU.is_equal))
            link(V.tensor_tensor(hi_hot[:], ge_tile[:, :, 0:NSL], ge_tile[:, :, 1:NSL + 1], ALU.subtract))
            for k in range(TOP_K):
                kt = slice(k * TILES, (k + 1) * TILES)
                V.tensor_tensor(slot_vals[:, kt, 0:NSL], hi_hot[:, kt, :],
                                tok_f[:].unsqueeze(2).to_broadcast([P, TILES, NSL]), ALU.mult)
                ins = V.tensor_tensor(slot_vals[:, kt, NSL:2 * NSL], hi_hot[:, kt, :],
                                      gate2[:, k].unsqueeze(2).to_broadcast([P, TILES, NSL]), ALU.mult)
            ins.then_inc(hots_ready, 1)
            link(V.tensor_scalar(pos[:], pos[:], -1.0, None, ALU.add))
            link(V.tensor_copy(slot_of[:], pos[:]))
            link(V.tensor_tensor(e_cmp[:], upto[0:1, 0:NE - 1].unsqueeze(1).to_broadcast([1, NSL, NE - 1]),
                                 iota_f[0:1, 0:NSL].unsqueeze(2).to_broadcast([1, NSL, NE - 1]), ALU.is_le))
            link(V.tensor_reduce(e_f[:, 0:NSL], e_cmp[:], AX.X, ALU.add))
            link(V.tensor_copy(e_f[:, T_UPTO:T_UPTO + NE], upto[0:1, :]))
            for i, (a, b) in enumerate(((1.0, -1.0), (-1.0, float(NSL)))):
                link(V.tensor_scalar(e_f[:, T_LAST + i:T_LAST + i + 1], upto[0:1, NE - 1:NE], a, b, ALU.mult, ALU.add))
            link(V.tensor_copy(table[:], e_f[:]))
            dve.wait_ge(slots_done, 1)
            link(V.tensor_copy(slot_gate[:], psum[6][:, NSL:2 * NSL]))
            V.tensor_copy(slot_tok[:], psum[6][:, 0:NSL]).then_inc(slots_ready, 1)
            dve.wait_ge(slots_ready, 1)

            def copy_x(n_turned):
                dve.wait_ge(xs_turned, n_turned)
                V.tensor_copy(xT_slot[:, 0:4, :], psum[4][:].rearrange("p (k n) -> p k n", k=4)).then_inc(xs_dve, 1)

            def copy_rows(n, before):
                if not isinstance(before, int) or before > 0:
                    dve.wait_ge(ys_stored, before)
                dve.wait_ge(down_done, n + 1)
                V.tensor_copy(y_slot[:, 0:512], psum[2][:]).then_inc(y_dve, 1)

            def slot_tile(t, before):
                dve.wait_ge(sil_ready, t + 1)
                V.scalar_tensor_tensor(out=h_row[:], in0=psum[0][:, F:2 * F], scalar=slot_gate[:, bass.ds(t, 1)],
                                       in1=sil[:], op0=ALU.mult, op1=ALU.mult).then_inc(h_ready, 1)
                copy_x(t * 2 + 3)
                if not isinstance(t, int) or t > 0:
                    copy_rows(t, before * 16)

            last = last_tile(dve)
            copy_x(1)
            slot_tile(0, -1)
            slot_tile(1, 0)
            with dve.Fori(1, last) as before:
                slot_tile(before + 1, before)
            copy_rows(last + 1, last * 16)

            def add_rows(t):
                n = rows_of[t]
                st, v = ln2_s[0:n, t, :], layer[0:n, t, :]
                dve.wait_ge(yp_in[t], 16 * TOP_K)
                if t == 0:
                    dve.wait_ge(x1_stored, 16 * TILES)
                link(V.scalar_tensor_tensor(out=v, in0=v, scalar=ALPHA, in1=y_pair[0:n, t, 0, :],
                                            op0=ALU.mult, op1=ALU.add))
                link(V.scalar_tensor_tensor(out=v, in0=v, scalar=1.0, in1=y_pair[0:n, t, 1, :],
                                            op0=ALU.mult, op1=ALU.add, accum_out=st[:, 0:1]))
                V.tensor_scalar(st[:, 1:2], st[:, 0:1], -1.0 / D, None, ALU.mult).then_inc(mean_ready, 1)

            def scales(t):
                st = ln2_s[0:rows_of[t], t, :]
                dve.wait_ge(std_ready, TILES + t + 1)
                dve.wait_ge(mean_ready, TILES + t + 1)
                link(V.reciprocal(st[:, 3:4], st[:, 2:3]))
                V.tensor_tensor(st[:, 0:1], st[:, 1:2], st[:, 3:4], ALU.mult).then_inc(scale_ready, 1)

            def gain(t):
                n = rows_of[t]
                v = layer[0:n, t, :]
                dve.wait_ge(scaled, t + 1)
                if t == 0:
                    dve.wait_ge(ln_in, 32)
                V.tensor_tensor(v, v, ln_row[1][0:n, 0, :], ALU.mult).then_inc(gained, 1)
                if t % 2 == 0:
                    dve.wait_ge(gained, t + 1)
                    V.tensor_tensor(v, v, ln_row[1][0:n, 1, :], ALU.add).then_inc(normed, 1)

            for t in range(TILES + 2):
                if t < TILES:
                    add_rows(t)
                if 1 <= t <= TILES:
                    scales(t - 1)
                if t >= 2:
                    gain(t - 2)


_INS = ['x_prompt', 'x_sample', 'cache_fox_kv', 'cache_fox_logf', 'cache_nsa_kv', 'state_nsa_win', 'state_conv',
        'page_table', 'w_in', 'fox_b_f', 'gmlp_w_s', 'gmlp_b_s', 'nsa_cmp_pe', 'nsa_cmp_w1', 'nsa_cmp_w2', 'conv_w',
        'w_out', 'ln_g', 'ln_b', 'w_router', 'w_exp_gate', 'w_exp_up', 'w_exp_down']

_OUTS = [(1, 1024, 1024), (8, 8, 1024), (1, 1, 1024, 2, 4, 64), (1, 8, 8, 2, 4, 64), (1, 1, 1024, 4), (1, 8, 8, 4),
         (1, 1, 1024, 4, 64), (1, 8, 8, 4, 64), (1, 1, 512, 2, 64), (1, 8, 512, 2, 64), (1, 1, 2, 256), (1, 8, 2, 256),
         (1, 8, 8, 4, 64)]


def kernel(**inputs):
    import numpy as np
    import concourse.bacc as bacc
    from concourse.bass_utils import run_bass_kernel_spmd as run

    nc = bacc.Bacc("TRN2", target_bir_lowering=False, num_devices=1)
    arrays, args = {}, []
    for name in _INS:
        a = np.ascontiguousarray(inputs[name])
        arrays[f"in_{name}"] = a
        args.append(nc.dram_tensor(f"in_{name}", a.shape, mybir.dt.from_np(a.dtype), kind="ExternalInput").ap())
    for i, shape in enumerate(_OUTS):
        args.append(nc.dram_tensor(f"out_{i}", shape, F32, kind="ExternalOutput").ap())
    build(nc, *args)
    r = run(nc, [arrays], core_ids=[0])
    return tuple(r.results[0][f"out_{i}"] for i in range(len(_OUTS)))
```
